# Optimizing a Trainium2 kernel written in Bass

```python
import jax, jax.numpy as jnp
from jax import lax
import numpy as np

D_MODEL = 1024
BATCH = 1
SEQ = 1024
DEPTH = 1

CHUNK = 64
EPS = 1e-6

GDN_HEADS = 4
GDN_DK = 128
GDN_DV = 128
GDN_CONV = 4
MLA_HEADS = 8
MLA_NOPE = 64
MLA_ROPE = 32
MLA_V = 64
MLA_Q_LORA = 384
MLA_KV_LORA = 256
ROPE_THETA = 10000.0
Q_BLOCK = 128
D_MIX = GDN_HEADS * GDN_DV + MLA_HEADS * MLA_V

N_EXPERTS = 32
TOP_K = 4
D_FF = 1024
SWIGLU_LIMIT = 7.0
SWIGLU_ALPHA = 1.702
MOE_BLOCK = 128

IN_SIZES = (GDN_HEADS * GDN_DK,
            GDN_HEADS * GDN_DK,
            GDN_HEADS * GDN_DV,
            GDN_HEADS * GDN_DV,
            GDN_HEADS,
            GDN_HEADS,
            MLA_Q_LORA,
            MLA_KV_LORA,
            MLA_ROPE)
D_IN = 4 * GDN_HEADS * GDN_DK + 2 * GDN_HEADS + MLA_Q_LORA + MLA_KV_LORA + MLA_ROPE

kernel_name = "hybrid_gdn_mla_moe_block"

def _split_points(sizes):
    pts, acc = [], 0
    for s in sizes[:-1]:
        acc += s
        pts.append(acc)
    return pts

def rms_norm(x, w):
    xf = x.astype(jnp.float32)
    y = xf * lax.rsqrt(jnp.mean(xf * xf, axis=-1, keepdims=True) + EPS)
    return (y * w.astype(jnp.float32)).astype(x.dtype)

def l2_norm(x):
    return x * lax.rsqrt(jnp.sum(x * x, axis=-1, keepdims=True) + EPS)

def causal_conv(x, w):
    k = w.shape[0]
    xp = jnp.pad(x, ((0, 0), (k - 1, 0), (0, 0)))
    return lax.conv_general_dilated(xp, w[:, None, :].astype(x.dtype), window_strides=(1,), padding='VALID',
                                    dimension_numbers=('NWC', 'WIO', 'NWC'),
                                    feature_group_count=x.shape[-1])

def chunk_gated_delta_rule(q, k, v, g, beta):
    bsz, s, h, dk = q.shape
    dv = v.shape[-1]
    n = s // CHUNK

    def to_chunks(t):
        t = t.reshape((bsz, n, CHUNK, h) + t.shape[3:])
        return jnp.moveaxis(t, (1, 3), (0, 2))

    q, k, v, g, beta = (to_chunks(t) for t in (q, k, v, g, beta))
    G = jnp.cumsum(g, axis=-1)
    idx = jnp.arange(CHUNK)
    causal = idx[:, None] >= idx[None, :]
    strict = idx[:, None] > idx[None, :]
    decay = jnp.exp(jnp.where(causal, G[..., :, None] - G[..., None, :], -jnp.inf))
    kb = k * beta[..., None]
    a_mat = jnp.where(strict, jnp.einsum('nbhcd,nbhsd->nbhcs', kb, k) * decay, 0.0)
    eye = jnp.eye(CHUNK, dtype=jnp.float32)
    t_mat = lax.linalg.triangular_solve(eye + a_mat, jnp.broadcast_to(eye, a_mat.shape),
                                        left_side=True, lower=True, unit_diagonal=True)
    u = jnp.einsum('nbhcs,nbhsd->nbhcd', t_mat, v * beta[..., None])
    w = jnp.einsum('nbhcs,nbhsd->nbhcd', t_mat, kb * jnp.exp(G)[..., None])
    qk = jnp.einsum('nbhcd,nbhsd->nbhcs', q, k) * decay
    q_dec = q * jnp.exp(G)[..., None]
    k_dec = k * jnp.exp(G[..., -1:] - G)[..., None]
    g_tot = jnp.exp(G[..., -1])

    def step(state, inp):
        u_n, w_n, qk_n, q_n, k_n, gt_n = inp
        v_new = u_n - jnp.einsum('bhcd,bhde->bhce', w_n, state)
        o_n = jnp.einsum('bhcd,bhde->bhce', q_n, state) + jnp.einsum('bhcs,bhse->bhce', qk_n, v_new)
        state = state * gt_n[..., None, None] + jnp.einsum('bhcd,bhce->bhde', k_n, v_new)
        return state, o_n

    s0 = jnp.zeros((bsz, h, dk, dv), jnp.float32)
    _, o = lax.scan(step, s0, (u, w, qk, q_dec, k_dec, g_tot))
    return jnp.moveaxis(o, (0, 2), (1, 3)).reshape(bsz, s, h, dv)

def gated_deltanet(q, k, v, z, a, b, conv_w, a_log, dt_bias, gdn_norm_w):
    bsz, s, _ = q.shape
    qkv = jax.nn.silu(causal_conv(jnp.concatenate([q, k, v], axis=-1), conv_w))
    q, k, v = jnp.split(qkv, [GDN_HEADS * GDN_DK, 2 * GDN_HEADS * GDN_DK], axis=-1)
    q = l2_norm(q.reshape(bsz, s, GDN_HEADS, GDN_DK).astype(jnp.float32)) * (GDN_DK ** -0.5)
    k = l2_norm(k.reshape(bsz, s, GDN_HEADS, GDN_DK).astype(jnp.float32))
    v = v.reshape(bsz, s, GDN_HEADS, GDN_DV).astype(jnp.float32)
    beta = jax.nn.sigmoid(b.astype(jnp.float32))
    g = -jnp.exp(a_log.astype(jnp.float32)) * jax.nn.softplus(a.astype(jnp.float32) + dt_bias.astype(jnp.float32))
    o = chunk_gated_delta_rule(q, k, v, g, beta)
    zf = z.reshape(bsz, s, GDN_HEADS, GDN_DV).astype(jnp.float32)
    o = rms_norm(o, gdn_norm_w) * jax.nn.silu(zf)
    return o.reshape(bsz, s, GDN_HEADS * GDN_DV).astype(z.dtype)

def rope_angles(positions):
    half = MLA_ROPE // 2
    inv_freq = ROPE_THETA ** (-jnp.arange(half, dtype=jnp.float32) / half)
    ang = positions.astype(jnp.float32)[..., None] * inv_freq
    return jnp.cos(ang), jnp.sin(ang)

def apply_rope(x, cos, sin):
    half = x.shape[-1] // 2
    xf = x.astype(jnp.float32)
    x1, x2 = xf[..., :half], xf[..., half:]
    return jnp.concatenate([x1 * cos - x2 * sin, x2 * cos + x1 * sin], axis=-1).astype(x.dtype)

def mla(c_q, c_kv, k_r, positions, q_norm_w, w_uq, kv_norm_w, w_ukv, mla_out_norm_w):
    bsz, s, _ = c_q.shape
    cos, sin = rope_angles(positions)
    q = (rms_norm(c_q, q_norm_w) @ w_uq).reshape(bsz, s, MLA_HEADS, MLA_NOPE + MLA_ROPE)
    q_nope, q_pe = q[..., :MLA_NOPE], q[..., MLA_NOPE:]
    q_pe = apply_rope(q_pe, cos[:, :, None, :], sin[:, :, None, :])
    kv = (rms_norm(c_kv, kv_norm_w) @ w_ukv).reshape(bsz, s, MLA_HEADS, MLA_NOPE + MLA_V)
    k_nope, v = kv[..., :MLA_NOPE], kv[..., MLA_NOPE:]
    k_pe = apply_rope(k_r, cos, sin)[:, :, None, :]
    q = jnp.concatenate([q_nope, q_pe], axis=-1).transpose(0, 2, 1, 3)
    k = jnp.concatenate([k_nope, jnp.broadcast_to(k_pe, (bsz, s, MLA_HEADS, MLA_ROPE))],
                        axis=-1).transpose(0, 2, 1, 3)
    v = v.transpose(0, 2, 1, 3)
    n_qb = s // Q_BLOCK
    q_blocks = jnp.moveaxis(q.reshape(bsz, MLA_HEADS, n_qb, Q_BLOCK, MLA_NOPE + MLA_ROPE), 2, 0)
    k_chunk = jnp.arange(s) // CHUNK
    scale = (MLA_NOPE + MLA_ROPE) ** -0.5

    def attend(args):
        qb, start = args
        sc = jnp.einsum('bhqd,bhkd->bhqk', qb, k).astype(jnp.float32) * scale
        q_chunk = (start + jnp.arange(Q_BLOCK)) // CHUNK
        sc = jnp.where(k_chunk[None, :] <= q_chunk[:, None], sc, -jnp.inf)
        p = jax.nn.softmax(sc, axis=-1)
        return jnp.einsum('bhqk,bhkd->bhqd', p.astype(v.dtype), v)

    o = lax.map(attend, (q_blocks, jnp.arange(n_qb, dtype=jnp.int32) * Q_BLOCK))
    o = jnp.moveaxis(o, 0, 2).reshape(bsz, MLA_HEADS, s, MLA_V).transpose(0, 2, 1, 3)
    return rms_norm(o.reshape(bsz, s, MLA_HEADS * MLA_V), mla_out_norm_w)

def moe_ffn(h, router_w, router_b, w1, b1, w2, b2):
    bsz, s, d = h.shape
    t = bsz * s
    xf = h.reshape(t, d)
    logits = (xf @ router_w + router_b).astype(jnp.float32)
    top_logits, top_idx = lax.top_k(logits, TOP_K)
    gates = jax.nn.softmax(top_logits, axis=-1)
    flat_e = top_idx.reshape(-1)
    order = jnp.argsort(flat_e)
    sorted_e = flat_e[order]
    tok = order // TOP_K
    counts = jnp.bincount(flat_e, length=N_EXPERTS)
    padded = (counts + MOE_BLOCK - 1) // MOE_BLOCK * MOE_BLOCK
    start = jnp.cumsum(counts) - counts
    padded_end = jnp.cumsum(padded)
    padded_start = padded_end - padded
    dest = padded_start[sorted_e] + jnp.arange(t * TOP_K) - start[sorted_e]
    n_pad = t * TOP_K + N_EXPERTS * MOE_BLOCK
    n_blocks = n_pad // MOE_BLOCK
    buf = jnp.zeros((n_pad, d), h.dtype).at[dest].set(xf[tok])
    block_expert = jnp.minimum(jnp.searchsorted(padded_end, jnp.arange(n_blocks) * MOE_BLOCK, side='right'),
                               N_EXPERTS - 1)

    def expert_block(args):
        xb, e = args
        hp = xb @ w1[e] + b1[e]
        x_glu = jnp.minimum(hp[:, ::2], SWIGLU_LIMIT)
        x_lin = jnp.clip(hp[:, 1::2], -SWIGLU_LIMIT, SWIGLU_LIMIT)
        act = x_glu * jax.nn.sigmoid(SWIGLU_ALPHA * x_glu) * (x_lin + 1)
        return act @ w2[e] + b2[e]

    y_blocks = lax.map(expert_block, (buf.reshape(n_blocks, MOE_BLOCK, d), block_expert))
    y_assign = y_blocks.reshape(n_pad, d)[dest] * gates.reshape(-1)[order][:, None].astype(h.dtype)
    y = jnp.zeros((t, d), h.dtype).at[tok].add(y_assign)
    return y.reshape(bsz, s, d)

def setup_inputs(seed: int = 0) -> dict:
    key = jax.random.key(seed)
    ks = jax.random.split(key, 24)
    f32 = jnp.float32

    def nrm(k, shape, scale):
        return jax.random.normal(k, shape, f32) * scale

    def gain(k, shape):
        return 1.0 + 0.02 * jax.random.normal(k, shape, f32)

    offset = jax.random.randint(ks[1], (BATCH,), 0, 4096, dtype=jnp.int32)
    positions = offset[:, None] + jnp.arange(SEQ, dtype=jnp.int32)[None, :]
    return {
        "x": nrm(ks[0], (BATCH, SEQ, D_MODEL), 1.0),
        "positions": positions,
        "norm_mix_w": gain(ks[2], (DEPTH, D_MODEL)),
        "w_in": nrm(ks[3], (DEPTH, D_MODEL, D_IN), D_MODEL ** -0.5),
        "conv_w": nrm(ks[4], (DEPTH, GDN_CONV, 2 * GDN_HEADS * GDN_DK + GDN_HEADS * GDN_DV), 0.5),
        "a_log": jnp.log(jax.random.uniform(ks[5], (DEPTH, GDN_HEADS), f32, 1.0, 16.0)),
        "dt_bias": nrm(ks[6], (DEPTH, GDN_HEADS), 0.1),
        "gdn_norm_w": gain(ks[7], (DEPTH, GDN_DV)),
        "q_norm_w": gain(ks[8], (DEPTH, MLA_Q_LORA)),
        "w_uq": nrm(ks[9], (DEPTH, MLA_Q_LORA, MLA_HEADS * (MLA_NOPE + MLA_ROPE)), MLA_Q_LORA ** -0.5),
        "kv_norm_w": gain(ks[10], (DEPTH, MLA_KV_LORA)),
        "w_ukv": nrm(ks[11], (DEPTH, MLA_KV_LORA, MLA_HEADS * (MLA_NOPE + MLA_V)), MLA_KV_LORA ** -0.5),
        "mla_out_norm_w": gain(ks[12], (DEPTH, MLA_HEADS * MLA_V)),
        "w_out": nrm(ks[13], (DEPTH, D_MIX, D_MODEL), D_MIX ** -0.5),
        "norm_ffn_w": gain(ks[14], (DEPTH, D_MODEL)),
        "router_w": nrm(ks[15], (DEPTH, D_MODEL, N_EXPERTS), D_MODEL ** -0.5),
        "router_b": nrm(ks[16], (DEPTH, N_EXPERTS), 0.01),
        "w1": nrm(ks[17], (DEPTH, N_EXPERTS, D_MODEL, 2 * D_FF), D_MODEL ** -0.5),
        "b1": nrm(ks[18], (DEPTH, N_EXPERTS, 2 * D_FF), 0.01),
        "w2": nrm(ks[19], (DEPTH, N_EXPERTS, D_FF, D_MODEL), D_FF ** -0.5),
        "b2": nrm(ks[20], (DEPTH, N_EXPERTS, D_MODEL), 0.01),
        "norm_final_w": gain(ks[21], (D_MODEL,)),
    }

def reference(x, positions, norm_mix_w, w_in, conv_w, a_log, dt_bias, gdn_norm_w, q_norm_w, w_uq,
              kv_norm_w, w_ukv, mla_out_norm_w, w_out, norm_ffn_w, router_w, router_b, w1, b1, w2, b2,
              norm_final_w):
    split_pts = _split_points(IN_SIZES)
    for l in range(DEPTH):
        h = rms_norm(x, norm_mix_w[l])
        proj = h @ w_in[l]
        q_a, k_a, v_a, z_a, a_a, b_a, c_q, c_kv, k_r = jnp.split(proj, split_pts, axis=-1)
        o_a = gated_deltanet(q_a, k_a, v_a, z_a, a_a, b_a, conv_w[l], a_log[l], dt_bias[l], gdn_norm_w[l])
        o_b = mla(c_q, c_kv, k_r, positions, q_norm_w[l], w_uq[l], kv_norm_w[l], w_ukv[l], mla_out_norm_w[l])
        x = x + jnp.concatenate([o_a, o_b], axis=-1) @ w_out[l]
        x = x + moe_ffn(rms_norm(x, norm_ffn_w[l]), router_w[l], router_b[l], w1[l], b1[l], w2[l], b2[l])
    return rms_norm(x, norm_final_w)


_drawn_inputs = setup_inputs


def setup_inputs(seed=0):
    import zlib

    import numpy as np

    out = dict(_drawn_inputs(seed))
    spreads = {}
    factors = {'a_log': 22.488,
     'dt_bias': 37.864,
     'b1': 8.0,
     'b2': 8.0,
     'norm_final_w': 7.539,
     'gdn_norm_w': 2.921}
    for name, (base, spread) in spreads.items():
        noise = np.random.default_rng([zlib.crc32(name.encode()), seed]).standard_normal(out[name].shape)
        drawn = base * np.exp(spread * noise) if base else spread * noise
        out[name] = __import__('jax').numpy.asarray(drawn.astype(out[name].dtype))
    for name, factor in factors.items():
        out[name] = (out[name] * factor).astype(out[name].dtype)
    return out
```

```python
from contextlib import ExitStack

import concourse.bass as bass
import numpy as np
from concourse import mybir

F32 = mybir.dt.float32
I32 = mybir.dt.int32
U32 = mybir.dt.uint32
ALU = mybir.AluOpType
ACT = mybir.ActivationFunctionType
AX_X = mybir.AxisListType.X
ds = bass.ds

P = 128
SEQ, D_MODEL = 1024, 1024
EPS = 1e-6
NT = SEQ // P
KD = D_MODEL // P
CHUNK = 64
GH, GDK, CONV = 4, 128, 4
GW = GH * GDK
AH, NOPE, ROPE, AV = 8, 64, 32, 64
QK = NOPE + ROPE
HALF = ROPE // 2
Q_LORA, KV_LORA = 384, 256
KQ, KKV = Q_LORA // P, KV_LORA // P
A0 = 4 * GW
CQ0 = A0 + 2 * GH
CKV0 = CQ0 + Q_LORA
KR0 = CKV0 + KV_LORA
D_IN = KR0 + ROPE
NE, TOPK, D_FF = 32, 4, 1024
LIMIT, ALPHA = 7.0, 1.702
ITEM = 256
BLOCKS = ITEM // P
STEP = 64
WIDTHS = ITEM // STEP
START = 2
MAX_ITEMS = SEQ * TOPK // ITEM + NE
TABLE = 64
ITEMS_OF_EXPERT = -(-SEQ // ITEM)
PLACES = NE * SEQ
PAD = SEQ
assert MAX_ITEMS + 2 <= TABLE

_COLS = {}


def _constants():
    parts, at = [], 0

    def put(name, a):
        nonlocal at
        a = np.broadcast_to(np.asarray(a, np.float32), (P, np.shape(a)[1]))
        _COLS[name] = (at, at + a.shape[1])
        at += a.shape[1]
        parts.append(a)

    r, c = np.arange(P)[:, None], np.arange(P)[None, :]
    same = r // CHUNK == c // CHUNK
    put("ident", r == c)
    put("ones", np.ones((P, P)))
    put("cum", (r <= c) & same)
    put("same", same)
    put("first", np.broadcast_to(r < CHUNK, (P, P)))
    put("second", np.broadcast_to(r >= CHUNK, (P, P)))
    put("causal", (c >= r) & same)
    put("strict", (c > r) & same)
    put("before", r < c)
    for n in range(6):
        b = 1 << n
        put(f"level{n}", (r // (2 * b) == c // (2 * b)) & (c // b > r // b))
    put("chunk_cols", np.concatenate([r < CHUNK, r >= CHUNK], 1))
    put("freq", np.float32(10000.0) ** (-np.arange(HALF, dtype=np.float32) / np.float32(HALF))[None])
    put("experts", np.arange(NE)[None])
    put("expert_rows", (np.arange(NE) * SEQ)[None])
    put("bounds", (np.arange(ITEMS_OF_EXPERT) * ITEM)[None])
    put("steps", (np.arange(WIDTHS) * STEP)[None])
    put("row", np.arange(P)[:, None])
    put("seen_off", np.broadcast_to(np.where(np.arange(P) < CHUNK, 1.0, 0.0)[None], (P, P)))
    put("hide", np.full((1, CHUNK), -1e30))
    return np.concatenate(parts, 1)


CONST = _constants()
CONSTS = CONST.shape[1]


class Memory:

    def c(self, name, rows=P):
        return self.const[0:rows, _COLS[name][0]:_COLS[name][1]]


def bc(ap, shape):
    return ap.to_broadcast(list(shape))


def over_heads(ap, n=GH):
    return bc(ap.unsqueeze(1), [ap.shape[0], n, ap.shape[1]])


def over_width(ap, w):
    return bc(ap.unsqueeze(2), [ap.shape[0], ap.shape[1], w])


def starting(eng, *sems):
    for s in sems:
        eng.sem_inc(s, START)


class Chain:

    def __init__(self, eng, sem):
        self.eng, self.sem, self.n = eng, sem, 0

    def link(self, ins):
        self.n += 1
        ins.then_inc(self.sem, 1)
        self.eng.wait_ge(self.sem, self.n)


class Stages:

    def __init__(self, sem, names):
        self.sem, self.names, self.per, self.made = sem, names, len(names), []

    def start(self, eng):
        eng.sem_inc(self.sem, self.per)

    def mark(self, ins, name):
        assert self.names[len(self.made)] == name, (name, self.names[len(self.made)])
        self.made.append(name)
        ins.then_inc(self.sem, 1)

    def mark_now(self, eng, name):
        assert self.names[len(self.made)] == name, (name, self.names[len(self.made)])
        self.made.append(name)
        eng.sem_inc(self.sem, 1)

    def wait(self, eng, name, turn, back=0):
        eng.wait_ge(self.sem, turn * self.per + (1 - back) * self.per + self.names.index(name) + 1)

    def end(self):
        assert self.made == self.names, (self.made, self.names)


def project(nc, A, m):
    with ExitStack() as own:
        def sb(name, shape, dt=F32):
            return own.enter_context(nc.sbuf_tensor(name, shape, dt))

        def sem(name):
            return own.enter_context(nc.semaphore(name))

        w_in = sb("w_in_sb", [P, KD, D_IN])
        norm_w = sb("norm_w", [P, KD])
        qn_w = sb("qn_w", [P, KQ])
        kvn_w = sb("kvn_w", [P, KKV])
        conv_w = sb("conv_w_sb", [P, 12, CONV])
        x_in = [sb(f"x_in{u}", [P, D_MODEL]) for u in range(2)]
        h = sb("h", [P, D_MODEL])
        hT = [sb(f"hT{u}", [P, KD, P]) for u in range(2)]
        taps = [sb(f"taps{u}", [P, 12, CONV - 1 + P]) for u in range(2)]
        conv = sb("conv", [P, 12, P])
        gout = sb("gout", [P, 4 * GW])
        cn = sb("cn", [P, Q_LORA + KV_LORA])
        ss = [sb(f"ss{u}", [P, 1]) for u in range(2)]
        rs = [sb(f"rs{u}", [P, 1]) for u in range(2)]
        ss10 = sb("ss10", [P, 10])
        rs10 = sb("rs10", [P, 10])
        power = sb("power", [P, 16])
        squares = sb("squares", [P, 2 * D_MODEL + Q_LORA + KV_LORA], mybir.dt.bfloat16)
        pT = [own.enter_context(nc.psum_tensor(f"pT{n}", [P, 4, P], F32)) for n in range(2)]
        pQKV = [own.enter_context(nc.psum_tensor(f"pQKV{n}", [P, 4, P], F32)) for n in range(3)]
        pZ = own.enter_context(nc.psum_tensor("pZ", [P, 512], F32))
        pC = own.enter_context(nc.psum_tensor("pC", [P, 512], F32))
        pK = own.enter_context(nc.psum_tensor("pK", [P, 512], F32))

        consts_in, small_in, w_loaded = sem("consts_in"), sem("small_in"), sem("w_loaded")
        x_loaded = [sem(f"x_loaded{u}") for u in range(2)]
        ss_ready, ms_ready, rs_ready = sem("ss_ready"), sem("ms_ready"), sem("rs_ready")
        h_ready, hT_psum, hT_ready = sem("h_ready"), sem("hT_psum"), sem("hT_ready")
        qkv_psum, zck_psum, taps_ready = sem("qkv_psum"), sem("zck_psum"), sem("taps_ready")
        head_ready, conv_step = sem("head_ready"), sem("conv_step")
        silu_ready, back_psum = sem("silu_ready"), sem("back_psum")
        ss10_ready, ms10_ready, rs10_ready, rsq_ready = (
            sem("ss10_ready"), sem("ms10_ready"), sem("rs10_ready"), sem("rsq_ready"))
        cn_ready, cT_psum, cT_done = sem("cn_ready"), sem("cT_psum"), sem("cT_done")
        gout_dve, gout_act, gout_stored, gout_free = sem("gout_dve"), sem("gout_act"), sem("gout_stored"), sem("gout_free")
        psum_read = sem("psum_read")
        pool_turn, zeroed, act_step = sem("pool_turn"), sem("zeroed"), sem("act_step")
        ident = m.c("ident")

        block = own.enter_context(nc.Block())

        @block.sync
        def _(sp):
            sp.dma_start(m.const[:], A["const"]).then_inc(consts_in, 16)
            sp.dma_start(norm_w[:], A["norm_mix"]).then_inc(small_in, 16)
            sp.dma_start(qn_w[:], A["q_norm"]).then_inc(small_in, 16)
            sp.dma_start(kvn_w[:], A["kv_norm"]).then_inc(small_in, 16)
            sp.dma_start(conv_w[:], A["conv_w"]).then_inc(small_in, 16)
            with sp.Fori(0, NT // 2) as it:
                for u in range(2):
                    i = it * 2 + u
                    sp.wait_ge(h_ready, START + i - 1)
                    sp.dma_start(x_in[u][:], A["x"][ds(i * P, P), :]).then_inc(x_loaded[u], 16)

        @block.gpsimd
        def _(pool):
            starting(pool, rs_ready, rs10_ready, gout_free)
            pool.memset(power[:], -0.5).then_inc(zeroed, 1)
            pool.memset(taps[0][:, :, 0:CONV - 1], 0.0).then_inc(zeroed, 1)
            pool.wait_ge(zeroed, 2)
            with pool.Fori(0, NT // 2) as it:
                for u in range(2):
                    i = it * 2 + u
                    pool.wait_ge(ms_ready, START + i + 1)
                    pool.sem_inc(pool_turn, 1)
                    pool.tensor_tensor(rs[u][:], ss[u][:], power[:, 0:1], ALU.pow).then_inc(rs_ready, 1)
                    pool.wait_ge(ms10_ready, START + i + 1)
                    pool.sem_inc(pool_turn, 1)
                    pool.tensor_tensor(rs10[:], ss10[:], power[:, 0:10], ALU.pow).then_inc(rs10_ready, 1)
                    pool.wait_ge(gout_dve, START + i + 1)
                    pool.wait_ge(gout_act, START + i + 1)
                    pool.sem_inc(pool_turn, 1)
                    pool.dma_start(m.gdn_in[ds(i * P, P), :], gout[:]).then_inc(gout_stored, 16)
                    pool.wait_ge(gout_stored, 16 * i + 16)
                    pool.sem_inc(gout_free, 1)
            

        @block.scalar
        def _(act):
            starting(act, ss_ready, taps_ready, head_ready, silu_ready, act_step, ss10_ready, gout_act)
            for k in range(KD):
                act.dma_start(w_in[:, k, :], A["w_in"][k * P:(k + 1) * P, :]).then_inc(w_loaded, 16)
            with act.Fori(0, NT // 2) as it:
                for u in range(2):
                    i = it * 2 + u
                    act.wait_ge(x_loaded[u], 16 * it + 16)
                    act.activation(squares[:, 0:D_MODEL], x_in[u][:], ACT.Square, accum_out=ss[u][:]).then_inc(ss_ready, 1)
                    for g in range(3):
                        act.wait_ge(qkv_psum, START + 3 * i + g + 1)
                        act.copy(taps[u][:, 4 * g:4 * g + 4, CONV - 1:], pQKV[g][:]).then_inc(taps_ready, 1)
                    act.wait_ge(taps_ready, START + 3 * i + 3)
                    act.wait_ge(conv_step, START + CONV * i)
                    act.copy(taps[1 - u][:, :, 0:CONV - 1], taps[u][:, :, P:]).then_inc(head_ready, 1)
                    for g in range(3):
                        act.wait_ge(conv_step, START + 4 * i + 4)
                        act.activation(conv[:, 4 * g:4 * g + 4, :], conv[:, 4 * g:4 * g + 4, :],
                                       ACT.Silu).then_inc(silu_ready, 1)
                    act.wait_ge(gout_free, START + i)
                    act.wait_ge(zck_psum, START + 3 * i + 1)
                    act.activation(gout[:, 3 * GW:4 * GW], pZ[:], ACT.Silu).then_inc(act_step, 1)
                    act.wait_ge(zck_psum, START + 3 * i + 3)
                    act.activation(squares[:, 2 * D_MODEL:2 * D_MODEL + Q_LORA], pC[:, CQ0 - A0:CKV0 - A0], ACT.Square,
                                   accum_out=ss10[:, 8:9]).then_inc(act_step, 1)
                    act.activation(squares[:, 2 * D_MODEL + Q_LORA:], pK[:, 0:KV_LORA], ACT.Square,
                                   accum_out=ss10[:, 9:10]).then_inc(act_step, 1)
                    act.wait_ge(back_psum, START + 3 * i + 3)
                    act.copy(gout[:, 2 * GW:3 * GW].rearrange("p (h w) -> p h w", h=GH), pQKV[2][:]).then_inc(gout_act, 1)
                    for g in range(2):
                        for a in range(GH):
                            last = act.activation(squares[:, D_MODEL + P * (4 * g + a):D_MODEL + P * (4 * g + a + 1)], pQKV[g][:, a, :], ACT.Square,
                                                  accum_out=ss10[:, 4 * g + a:4 * g + a + 1])
                            if g == 0 or a < GH - 1:
                                last.then_inc(act_step, 1)
                    last.then_inc(ss10_ready, 1)

        @block.vector
        def _(dve):
            starting(dve, ms_ready, h_ready, hT_ready, conv_step, ms10_ready, rsq_ready, cn_ready, gout_dve, psum_read, cT_done)
            dve.wait_ge(small_in, 64)
            dve.wait_ge(consts_in, 16)
            dve.wait_ge(zeroed, 2)
            with dve.Fori(0, NT // 2) as it:
                for u in range(2):
                    i = it * 2 + u
                    dve.wait_ge(ss_ready, START + i + 1)
                    dve.tensor_scalar(ss[u][:], ss[u][:], 1.0 / D_MODEL, EPS, ALU.mult, ALU.add).then_inc(ms_ready, 1)
                    dve.wait_ge(rs_ready, START + i + 1)
                    dve.tensor_scalar(h[:], x_in[u][:], rs[u][:], None, ALU.mult).then_inc(h_ready, 1)
                    dve.wait_ge(hT_psum, START + 2 * i + 1)
                    dve.tensor_tensor(hT[u][:, 0:4, :], pT[0][:], over_width(norm_w[:, 0:4], P), ALU.mult).then_inc(hT_ready, 1)
                    dve.wait_ge(hT_psum, START + 2 * i + 2)
                    dve.tensor_tensor(hT[u][:, 4:8, :], pT[1][:], over_width(norm_w[:, 4:8], P), ALU.mult).then_inc(hT_ready, 1)
                    dve.wait_ge(taps_ready, START + 3 * i + 3)
                    dve.wait_ge(head_ready, START + i)
                    for tap in range(CONV - 1, -1, -1):
                        for ch in range(12):
                            src = taps[u][:, ch, tap:tap + P]
                            if tap == CONV - 1:
                                last = dve.tensor_scalar(conv[:, ch, :], src, conv_w[:, ch, tap:tap + 1], None, ALU.mult)
                            else:
                                last = dve.scalar_tensor_tensor(out=conv[:, ch, :], in0=src, scalar=conv_w[:, ch, tap:tap + 1],
                                                                in1=conv[:, ch, :], op0=ALU.mult, op1=ALU.add)
                        last.then_inc(conv_step, 1)
                        dve.wait_ge(conv_step, START + 4 * i + CONV - tap)
                    dve.wait_ge(ss10_ready, START + i + 1)
                    dve.tensor_scalar(ss10[:, 0:8], ss10[:, 0:8], EPS, None, ALU.add)
                    dve.tensor_scalar(ss10[:, 8:9], ss10[:, 8:9], 1.0 / Q_LORA, EPS, ALU.mult, ALU.add)
                    dve.tensor_scalar(ss10[:, 9:10], ss10[:, 9:10], 1.0 / KV_LORA, EPS, ALU.mult, ALU.add).then_inc(ms10_ready, 1)
                    dve.wait_ge(rs10_ready, START + i + 1)
                    dve.tensor_scalar(rs10[:, 0:GH], rs10[:, 0:GH], GDK ** -0.5, None, ALU.mult).then_inc(rsq_ready, 1)
                    dve.tensor_scalar(cn[:, 0:Q_LORA], pC[:, CQ0 - A0:CKV0 - A0], rs10[:, 8:9], None, ALU.mult)
                    dve.tensor_scalar(cn[:, Q_LORA:], pK[:, 0:KV_LORA], rs10[:, 9:10], None, ALU.mult).then_inc(cn_ready, 1)
                    dve.wait_ge(rsq_ready, START + i + 1)
                    dve.wait_ge(gout_free, START + i)
                    for g in range(2):
                        last = dve.tensor_tensor(gout[:, g * GW:(g + 1) * GW].rearrange("p (h w) -> p h w", h=GH), pQKV[g][:],
                                                 over_width(rs10[:, 4 * g:4 * g + 4], P), ALU.mult)
                    last.then_inc(gout_dve, 1)
                    dve.tensor_copy(m.ab[:, ds(i, 1), :], pC[:, 0:2 * GH].unsqueeze(1))
                    dve.tensor_copy(m.k_rope[:, ds(i, 1), :], pK[:, KV_LORA:KV_LORA + ROPE].unsqueeze(1)).then_inc(psum_read, 1)
                    dve.wait_ge(cT_psum, START + i + 1)
                    dve.tensor_tensor(m.cqT[:, :, ds(i * P, P)], pT[0][:, 0:KQ, :], over_width(qn_w[:], P), ALU.mult)
                    dve.tensor_tensor(m.ckvT[:, :, ds(i * P, P)], pT[1][:, 0:KKV, :], over_width(kvn_w[:], P), ALU.mult)\
                        .then_inc(cT_done, 1)

        @block.tensor
        def _(pe):
            starting(pe, hT_psum, qkv_psum, zck_psum, back_psum, cT_psum)
            pe.wait_ge(consts_in, 16)
            with pe.Fori(0, NT // 2) as it:
                for u in range(2):
                    i = it * 2 + u
                    pe.wait_ge(h_ready, START + i + 1)
                    pe.wait_ge(cT_done, START + i)
                    for k in range(KD):
                        last = pe.transpose(pT[k // 4][:, k % 4, :], h[:, k * P:(k + 1) * P], ident)
                        if k % 4 == 3:
                            last.then_inc(hT_psum, 1)
                    pe.wait_ge(ss10_ready, START + i)
                    pe.wait_ge(psum_read, START + i)
                    pe.wait_ge(hT_ready, START + 2 * i + 2)
                    pe.wait_ge(w_loaded, 16 * KD)
                    for g in range(3):
                        for c in range(4):
                            for k in range(KD):
                                at = (4 * g + c) * P
                                last = pe.matmul(pQKV[g][:, c, :], w_in[:, k, at:at + P], hT[u][:, k, :],
                                                 start=k == 0, stop=k == KD - 1)
                        last.then_inc(qkv_psum, 1)
                    for bank, at, end in ((pZ, 3 * GW, A0), (pC, A0, CKV0), (pK, CKV0, D_IN)):
                        for k in range(KD):
                            last = pe.matmul(bank[:, 0:end - at], hT[u][:, k, :], w_in[:, k, at:end],
                                             start=k == 0, stop=k == KD - 1)
                        last.then_inc(zck_psum, 1)
                    for g in range(3):
                        pe.wait_ge(silu_ready, START + 3 * i + g + 1)
                        for c in range(4):
                            last = pe.transpose(pQKV[g][:, c, :], conv[:, 4 * g + c, :], ident)
                        last.then_inc(back_psum, 1)
                    pe.wait_ge(cn_ready, START + i + 1)
                    for k in range(KQ + KKV):
                        bank, at = (pT[0], k) if k < KQ else (pT[1], k - KQ)
                        last = pe.transpose(bank[:, at, :], cn[:, k * P:(k + 1) * P], ident)
                    last.then_inc(cT_psum, 1)


def _parts_of_two_pi(n):
    rest, parts = 2 * np.pi, []
    for _ in range(n):
        step = 2.0 ** (np.floor(np.log2(rest)) - 7)
        parts.append(float(np.floor(rest / step) * step))
        rest -= parts[-1]
    return parts


ROUND = 1.5 * 2.0 ** 23
BELOW_PI = 3.1415925


def prepare(nc, A, m):
    with ExitStack() as own:
        def sb(name, shape, dt=F32):
            return own.enter_context(nc.sbuf_tensor(name, shape, dt))

        def sem(name):
            return own.enter_context(nc.semaphore(name))

        pos_i = sb("pos_i", [P, NT], I32)
        pos = sb("pos", [P, NT])
        angle, turns, high, low, wrap = (sb(n, [P, NT, HALF]) for n in ("angle", "turns", "high", "low", "wrap"))
        prod = [sb(f"prod{n}", [P, NT, HALF]) for n in range(4)]
        a_log, dt_bias = sb("a_log_sb", [P, GH]), sb("dt_bias_sb", [P, GH])
        x, ax, y, s, s2, p = (sb(n, [P, NT, GH]) for n in ("sp_x", "sp_ax", "sp_y", "sp_s", "sp_s2", "sp_p"))
        eb = sb("eb", [P, NT, GH])
        ea = sb("ea", [P, GH])
        loaded, dve_chain = sem("prep_loaded"), sem("prep_dve")
        ax_ready, exp_ready = sem("ax_ready"), sem("exp_ready")
        angles_ready, sin_ready = sem("angles_ready"), sem("sin_ready")
        shape = [P, NT, HALF]
        block = own.enter_context(nc.Block())

        @block.sync
        def _(sp):
            sp.dma_start(pos_i[:], A["positions"]).then_inc(loaded, 16)
            sp.dma_start(a_log[:], bc(A["a_log"], [P, GH])).then_inc(loaded, 16)
            sp.dma_start(dt_bias[:], bc(A["dt_bias"], [P, GH])).then_inc(loaded, 16)

        @block.vector
        def _(dve):
            link = Chain(dve, dve_chain).link
            dve.wait_ge(loaded, 48)
            link(dve.tensor_tensor(x[:], m.ab[:, :, 0:GH], bc(dt_bias[:].unsqueeze(1), [P, NT, GH]), ALU.add))
            dve.scalar_tensor_tensor(out=ax[:], in0=x[:], scalar=-1.0, in1=x[:], op0=ALU.mult, op1=ALU.max).then_inc(ax_ready, 1)
            link(dve.tensor_copy(pos[:], pos_i[:]))
            link(dve.tensor_tensor(angle[:], over_width(pos[:], HALF), over_heads(m.c("freq"), NT), ALU.mult))
            link(dve.tensor_scalar(turns[:], angle[:], float(1 / (2 * np.pi)), ROUND, ALU.mult, ALU.add))
            link(dve.tensor_scalar(turns[:], turns[:], ROUND, None, ALU.subtract))
            link(dve.tensor_scalar(high[:], turns[:], 1.0 / 256, ROUND, ALU.mult, ALU.add))
            link(dve.tensor_scalar(high[:], high[:], ROUND, 256.0, ALU.subtract, ALU.mult))
            link(dve.tensor_tensor(low[:], turns[:], high[:], ALU.subtract))
            for part in _parts_of_two_pi(5):
                for whole in (high, low):
                    link(dve.scalar_tensor_tensor(out=angle[:], in0=whole[:], scalar=-part, in1=angle[:],
                                                  op0=ALU.mult, op1=ALU.add))
            link(dve.tensor_scalar(m.cos[:], angle[:], float(np.pi / 2), None, ALU.add))
            link(dve.tensor_scalar(wrap[:], m.cos[:], float(np.pi), -float(2 * np.pi), ALU.is_gt, ALU.mult))
            link(dve.tensor_tensor(m.cos[:], m.cos[:], wrap[:], ALU.add))
            link(dve.tensor_scalar(m.cos[:], m.cos[:], BELOW_PI, -BELOW_PI, ALU.min, ALU.max))
            dve.tensor_scalar(m.sin[:], angle[:], BELOW_PI, -BELOW_PI, ALU.min, ALU.max).then_inc(angles_ready, 1)
            dve.wait_ge(exp_ready, 3)
            link(dve.tensor_scalar(s[:], y[:], 2.0, None, ALU.add))
            link(dve.reciprocal(s[:], s[:]))
            link(dve.tensor_tensor(s[:], s[:], y[:], ALU.mult))
            link(dve.tensor_tensor(s2[:], s[:], s[:], ALU.mult))
            link(dve.tensor_scalar(p[:], s2[:], 1.0 / 17, None, ALU.mult))
            for n in (15, 13, 11, 9, 7, 5, 3):
                link(dve.scalar_tensor_tensor(out=p[:], in0=p[:], scalar=1.0 / n, in1=s2[:], op0=ALU.add, op1=ALU.mult))
            link(dve.scalar_tensor_tensor(out=p[:], in0=p[:], scalar=1.0, in1=s[:], op0=ALU.add, op1=ALU.mult))
            link(dve.tensor_scalar(x[:], x[:], 0.0, None, ALU.max))
            link(dve.scalar_tensor_tensor(out=x[:], in0=p[:], scalar=2.0, in1=x[:], op0=ALU.mult, op1=ALU.add))
            link(dve.scalar_tensor_tensor(out=m.g[:], in0=x[:], scalar=-1.0, in1=bc(ea[:].unsqueeze(1), [P, NT, GH]),
                                          op0=ALU.mult, op1=ALU.mult))
            link(dve.tensor_scalar(eb[:], eb[:], 1.0, None, ALU.add))
            link(dve.reciprocal(m.beta[:], eb[:]))
            dve.wait_ge(sin_ready, 1)
            k1, k2 = m.k_rope[:, :, 0:HALF], m.k_rope[:, :, HALF:ROPE]
            dve.tensor_tensor(prod[0][:], k1, m.cos[:], ALU.mult)
            dve.tensor_tensor(prod[1][:], k2, m.sin[:], ALU.mult)
            dve.tensor_tensor(prod[2][:], k2, m.cos[:], ALU.mult)
            link(dve.tensor_tensor(prod[3][:], k1, m.sin[:], ALU.mult))
            dve.tensor_tensor(m.kh[:, :, NOPE:NOPE + HALF], prod[0][:], prod[1][:], ALU.subtract)
            link(dve.tensor_tensor(m.kh[:, :, NOPE + HALF:], prod[2][:], prod[3][:], ALU.add))

        @block.scalar
        def _(act):
            act.wait_ge(loaded, 48)
            act.activation(ea[:], a_log[:], ACT.Exp).then_inc(exp_ready, 1)
            act.activation(eb[:], m.ab[:, :, GH:], ACT.Exp, scale=-1.0).then_inc(exp_ready, 1)
            act.wait_ge(ax_ready, 1)
            act.activation(y[:], ax[:], ACT.Exp, scale=-1.0).then_inc(exp_ready, 1)
            act.wait_ge(angles_ready, 1)
            act.activation(m.cos[:], m.cos[:], ACT.Sin)
            act.activation(m.sin[:], m.sin[:], ACT.Sin).then_inc(sin_ready, 1)


LEVELS = range(1, 6)
_DELTA = (["rates", "scaled", "turn_k", "turn_q", "overlap", "x0"]
          + [f"{s}{n}" for n in LEVELS for s in ("y", "z")]
          + ["uw", "read0", "write0", "read1", "write1", "within", "gate"])
_ATTEND = ["up", "turn", "score0"]
for _j in range(1, NT + 1):
    if _j < NT:
        _ATTEND.append(f"score{_j}")
    _ATTEND += [f"spread{_j - 1}_{_g}" for _g in range((_j + 3) // 4)] + [f"value{_j - 1}"]
_ATTEND.append("heads_out")


def _merge(a, b):
    at = [((n + 0.5) / len(a), 0, x) for n, x in enumerate(a)] + [((n + 0.5) / len(b), 1, x) for n, x in enumerate(b)]
    return [x for _, _, x in sorted(at)]


ORDER = _merge(_DELTA, _ATTEND)


def mix(nc, A, m):
    with ExitStack() as own:
        def sb(name, shape, dt=F32):
            return own.enter_context(nc.sbuf_tensor(name, shape, dt))

        def sem(name):
            return own.enter_context(nc.semaphore(name))

        def heads(name):
            return sb(name, [P, GH, P])

        q_in, k_in, v_in, z_in = (heads(n) for n in ("q_in", "k_in", "v_in", "z_in"))
        g_cum, diff, decay = heads("g_cum"), heads("diff"), heads("decay")
        rate = sb("rate", [P, 4 * GH])
        rate_exp = sb("rate_exp", [P, 4 * GH])
        k_rate = sb("k_rate", [P, 2, GH])
        kb, kbe, qd, vb = (heads(n) for n in ("kb", "kbe", "qd", "vb"))
        kd = [heads(f"kd{j}") for j in range(2)]
        kT, kbT, qT, qdT = (heads(n) for n in ("kT", "kbT", "qT", "qdT"))
        AT, QKT, X, XT, Y = (heads(n) for n in ("AT", "QKT", "X", "XT", "Y"))
        LT = {n: heads(f"LT{n}") for n in LEVELS}
        first = heads("first_level")
        u, wT, v_new, S, S_decayed, o = (heads(n) for n in ("u", "wT", "v_new", "S", "S_decayed", "o"))
        o_norm, o_sq = heads("o_norm"), heads("o_sq")
        o_ms, o_rs, power = sb("o_ms", [P, GH]), sb("o_rs", [P, GH]), sb("o_power", [P, GH])
        w_uq = sb("w_uq_sb", [P, KQ, AH * QK])
        w_ukv = sb("w_ukv_sb", [P, KKV, AH * (NOPE + AV)])
        qh, kh, vh = sb("qh", [P, NT, QK]), m.kh, sb("vh", [P, NT, AV])
        prod = [sb(f"qprod{n}", [P, NT, HALF]) for n in range(4)]
        qhT, khT = sb("qhT", [QK, SEQ]), sb("khT", [QK, SEQ])
        probs = [sb(f"probs{b}", [P, SEQ]) for b in range(2)]
        probsT = [sb(f"probsT{b}", [P, NT, P]) for b in range(2)]
        neg_max, row_sum, row_inv = sb("neg_max", [P, NT]), sb("row_sum", [P, NT]), sb("row_inv", [P, NT])

        pS = own.enter_context(nc.psum_tensor("pS", [P, SEQ], F32))
        pT = [own.enter_context(nc.psum_tensor(f"bankT{b}", [P, 4, P], F32)) for b in range(2)]
        pO = own.enter_context(nc.psum_tensor("pO", [P, NT, AV], F32))
        gA, gB, gC = (own.enter_context(nc.psum_tensor(n, [P, GH, P], F32)) for n in ("gA", "gB", "gC"))
        pS4 = [pS[:, 512 * b:512 * b + 512].rearrange("p (t w) -> p t w", t=4) for b in range(2)]

        levels = [n for n in LEVELS]
        g_pe = Stages(sem("g_pe"), ["rates", "decay", "kT", "kbT", "qT", "qdT", "AT", "QKT", "X"]
                      + [f"{s}{n}" for n in levels[:-1] for s in ("Y", "Z", "ZT")] + ["Y5", "ZT5", "u", "wT"]
                      + [f"{s}{j}" for j in range(2) for s in ("wS", "qS", "dS")] + ["within"])
        g_dve = Stages(sem("g_dve"), ["g_cum", "rate_copy", "rate", "diff", "diff_masked", "decay", "kb", "k_rate",
                                      "kbe", "qd", "kbT", "qdT", "AT", "QKT", "first", "XT"]
                       + [f"{s}{n}" for n in levels[:-1] for s in ("X", "XT")] + ["XT5", "wT"]
                       + [f"{s}{j}" for j in range(2) for s in ("v_new", "S_decayed", "S")]
                       + ["o", "o_ms", "o_norm", "o_out"])
        g_act = Stages(sem("g_act"), ["rate_exp", "diff_exp", "kT", "qT", "X"] + [f"Y{n}" for n in levels]
                       + ["u", "o0", "o1", "o_sq"])
        g_pool = Stages(sem("g_pool"), ["vb", "kd0", "kd1"] + [f"LT{n}" for n in levels] + ["o_rs"])
        groups = {j: range((j + 4) // 4) for j in range(NT)}
        a_pe = Stages(sem("a_pe"), ["q0", "q1", "kv0", "kv1", "qT0", "qT1", "kT0", "kT1", "score0"]
                      + [x for j in range(NT) for x in
                         ([f"score{j + 1}"] if j + 1 < NT else []) + [f"spread{j}_{g}" for g in groups[j]] + [f"value{j}"]])
        on_dve = lambda j, g: (j + g) % 2 == 0
        a_dve = Stages(sem("a_dve"), ["k0", "v0", "products", "rope", "qT0", "qT1", "max0"]
                       + [x for j in range(NT) for x in
                          ([f"max{j + 1}"] if j + 1 < NT else []) + [f"spread{j}_{g}" for g in groups[j] if on_dve(j, g)]]
                       + ["row_inv", "out"])
        a_act = Stages(sem("a_act"), ["q0", "q1", "k1", "v1", "kT0", "kT1", "exp0"]
                       + [x for j in range(NT) for x in
                          ([f"exp{j + 1}"] if j + 1 < NT else []) + [f"spread{j}_{g}" for g in groups[j] if not on_dve(j, g)]])
        in_loaded = {n: sem(f"{n}_loaded") for n in ("q", "k", "v", "z")}
        weights_in, zeroed, pool_turn, gate = sem("weights_in"), sem("mix_zeroed"), sem("mix_pool_turn"), sem("gate")
        ident = m.c("ident")

        def width_of(j):
            return (j + 1) * P

        block = own.enter_context(nc.Block())

        @block.sync
        def _(sp):
            for k in range(KQ):
                sp.dma_start(w_uq[:, k, :], A["w_uq"][k * P:(k + 1) * P, :]).then_inc(weights_in, 16)
            for k in range(KKV):
                sp.dma_start(w_ukv[:, k, :], A["w_ukv"][k * P:(k + 1) * P, :]).then_inc(weights_in, 16)
            with sp.Fori(0, NT) as t:
                rows = m.gdn_in[ds(t * P, P), :]
                g_pe.wait(sp, "qdT", t, back=1)
                g_dve.wait(sp, "qd", t, back=1)
                g_pool.wait(sp, "kd1", t, back=1)
                sp.dma_start(k_in[:].rearrange("p h w -> p (h w)"), rows[:, GW:2 * GW]).then_inc(in_loaded["k"], 16)
                sp.dma_start(q_in[:].rearrange("p h w -> p (h w)"), rows[:, 0:GW]).then_inc(in_loaded["q"], 16)
                sp.dma_start(v_in[:].rearrange("p h w -> p (h w)"), rows[:, 2 * GW:3 * GW]).then_inc(in_loaded["v"], 16)
                g_dve.wait(sp, "o_out", t, back=1)
                sp.dma_start(z_in[:].rearrange("p h w -> p (h w)"), rows[:, 3 * GW:4 * GW]).then_inc(in_loaded["z"], 16)

        @block.gpsimd
        def _(pool):
            g_pool.start(pool)
            pool.memset(power[:], -0.5).then_inc(zeroed, 1)
            pool.memset(v_new[:], 0.0).then_inc(zeroed, 1)
            pool.memset(S[:], 0.0).then_inc(zeroed, 1)
            pool.wait_ge(zeroed, 3)
            with pool.Fori(0, NT) as t:
                pool.wait_ge(in_loaded["v"], 16 * t + 16)
                pool.wait_ge(in_loaded["k"], 16 * t + 16)
                g_pe.wait(pool, "u", t, back=1)
                pool.sem_inc(pool_turn, 1)
                g_pool.mark(pool.tensor_tensor(vb[:], v_in[:], over_width(m.beta[:, ds(t, 1), :].rearrange("p a h -> p (a h)"), P),
                                               ALU.mult), "vb")
                g_dve.wait(pool, "k_rate", t)
                g_pe.wait(pool, "dS1", t, back=1)
                pool.sem_inc(pool_turn, 1)
                for j in range(2):
                    g_pool.mark(pool.tensor_tensor(kd[j][:], k_in[:], over_width(k_rate[:, j, :], P), ALU.mult), f"kd{j}")
                g_dve.wait(pool, "AT", t)
                g_pe.wait(pool, "Y5", t, back=1)
                pool.sem_inc(pool_turn, 1)
                for n in LEVELS:
                    g_pool.mark(pool.tensor_tensor(LT[n][:], AT[:], over_heads(m.c(f"level{n}")), ALU.mult), f"LT{n}")
                g_dve.wait(pool, "o_ms", t)
                pool.sem_inc(pool_turn, 1)
                g_pool.mark(pool.tensor_tensor(o_rs[:], o_ms[:], power[:], ALU.pow), "o_rs")
            g_pool.end()

        @block.tensor
        def _(pe):
            g_pe.start(pe)
            a_pe.start(pe)
            pe.wait_ge(zeroed, 3)
            pe.wait_ge(weights_in, 16 * (KQ + KKV))

            def per_head(bank, lhsT, rhs, name):
                for h in range(GH):
                    last = pe.matmul(bank[:, h, :], lhsT[:, h, :], rhs[:, h, :], start=True, stop=True)
                g_pe.mark(last, name)

            def turn_heads(bank, src, name):
                for h in range(GH):
                    last = pe.transpose(bank[:, h, :], src[:, h, :], ident)
                g_pe.mark(last, name)

            def delta(step, t):
                if step == "rates":
                    g = m.g[:, ds(t, 1), :].rearrange("p a h -> p (a h)")
                    g_dve.wait(pe, "o", t, back=1)
                    g_act.wait(pe, "o1", t, back=1)
                    g_dve.wait(pe, "S1", t, back=1)
                    for n, which in enumerate(("cum", "same", "first", "second")):
                        last = pe.matmul(gA[:, 0, GH * n:GH * n + GH], m.c(which), g, start=True, stop=True)
                    g_pe.mark(last, "rates")
                    g_dve.wait(pe, "g_cum", t)
                    g_pe.mark(pe.matmul(gB[:], m.c("ones"), g_cum[:], start=True, stop=True), "decay")
                if step == "turn_k":
                    pe.wait_ge(in_loaded["k"], 16 * t + 16)
                    turn_heads(gC, k_in, "kT")
                    g_dve.wait(pe, "kb", t)
                    turn_heads(gA, kb, "kbT")
                if step == "turn_q":
                    pe.wait_ge(in_loaded["q"], 16 * t + 16)
                    g_dve.wait(pe, "qd", t)
                    turn_heads(gB, q_in, "qT")
                    g_act.wait(pe, "kT", t)
                    turn_heads(gC, qd, "qdT")
                if step == "overlap":
                    g_dve.wait(pe, "kbT", t)
                    per_head(gA, kT, kbT, "AT")
                    g_act.wait(pe, "qT", t)
                    per_head(gB, kT, qT, "QKT")
                if step == "x0":
                    g_dve.wait(pe, "XT", t)
                    turn_heads(gC, XT, "X")
                if step[0] == "y" and step[1:].isdigit():
                    n = int(step[1:])
                    g_pool.wait(pe, f"LT{n}", t)
                    g_act.wait(pe, "X", t) if n == 1 else g_dve.wait(pe, f"XT{n - 1}", t)
                    per_head(gA, LT[n], X, f"Y{n}")
                if step[0] == "z" and step[1:].isdigit():
                    n = int(step[1:])
                    g_act.wait(pe, f"Y{n}", t)
                    if n < 5:
                        per_head(gB, XT, Y, f"Z{n}")
                    per_head(gC, Y, XT, f"ZT{n}")
                if step == "uw":
                    g_dve.wait(pe, "XT5", t)
                    g_pool.wait(pe, "vb", t)
                    per_head(gA, XT, vb, "u")
                    per_head(gB, kbe, XT, "wT")
                if step[:-1] == "read":
                    j = int(step[-1])
                    if j == 0:
                        g_dve.wait(pe, "wT", t)
                        g_act.wait(pe, "u", t)
                    else:
                        g_dve.wait(pe, "S0", t)
                        g_act.wait(pe, "o0", t)
                    per_head(gC, wT, S, f"wS{j}")
                    per_head(gA, qdT, S, f"qS{j}")
                if step[:-1] == "write":
                    j = int(step[-1])
                    g_pool.wait(pe, f"kd{j}", t)
                    g_dve.wait(pe, f"v_new{j}", t)
                    per_head(gB, kd[j], v_new, f"dS{j}")
                if step == "within":
                    per_head(gC, QKT, v_new, "within")

            def attend(step, t):
                if step == "up":
                    a_act.wait(pe, "exp7", t, back=1)
                    for b in range(2):
                        for c in range(4):
                            for k in range(KQ):
                                last = pe.matmul(pS4[b][:, c, 0:QK], m.cqT[:, k, (4 * b + c) * P:(4 * b + c + 1) * P],
                                                 w_uq[:, k, ds(t * QK, QK)], start=k == 0, stop=k == KQ - 1)
                        a_pe.mark(last, f"q{b}")
                    a_dve.wait(pe, "out", t, back=1)
                    a_act.wait(pe, "spread7_0" if not on_dve(7, 0) else "spread7_1", t, back=1)
                    for b in range(2):
                        for c in range(4):
                            for k in range(KKV):
                                last = pe.matmul(pT[b][:, c, :], m.ckvT[:, k, (4 * b + c) * P:(4 * b + c + 1) * P],
                                                 w_ukv[:, k, ds(t * (NOPE + AV), NOPE + AV)], start=k == 0, stop=k == KKV - 1)
                        a_pe.mark(last, f"kv{b}")
                if step == "turn":
                    a_dve.wait(pe, "rope", t)
                    a_act.wait(pe, "v1", t)
                    for b in range(2):
                        for c in range(4):
                            last = pe.transpose(pS4[b][0:QK, c, :], qh[:, 4 * b + c, :], ident)
                        a_pe.mark(last, f"qT{b}")
                    for b in range(2):
                        for c in range(4):
                            last = pe.transpose(pT[b][0:QK, c, :], kh[:, 4 * b + c, :], ident)
                        a_pe.mark(last, f"kT{b}")
                if step[:5] == "score":
                    j = int(step[5:])
                    if j == 0:
                        a_dve.wait(pe, "qT1", t)
                        a_act.wait(pe, "kT1", t)
                    elif j < 4:
                        if j >= 2:
                            a_act.wait(pe, f"exp{j - 2}", t)
                    else:
                        a_act.wait(pe, f"exp{j - 1}", t)
                    base = 512 * (j % 2) if j < 4 else 0
                    for at in range(0, width_of(j), 512):
                        end = min(at + 512, width_of(j))
                        last_bank = end == width_of(j)
                        pe.matmul(pS[:, base + at:base + end], qhT[:, j * P:(j + 1) * P], khT[:, at:end],
                                  start=True, stop=not last_bank)
                    end = base + width_of(j)
                    a_pe.mark(pe.matmul(pS[:, end - CHUNK:end], m.c("seen_off", 1), m.c("hide", 1),
                                        start=False, stop=True), f"score{j}")
                if step[:6] == "spread":
                    j, g = int(step[6]), int(step[8])
                    a_act.wait(pe, f"exp{j}", t)
                    if (j, g) in last_use:
                        jj, gg = last_use[(j, g)]
                        (a_dve if on_dve(jj, gg) else a_act).wait(pe, f"spread{jj}_{gg}", t)
                    for c in range(4 * g, min(4 * g + 4, j + 1)):
                        last = pe.transpose(pT[bank_of[(j, g)]][:, c % 4, :], probs[j % 2][:, c * P:(c + 1) * P], ident)
                    a_pe.mark(last, step)
                if step[:5] == "value":
                    j = int(step[5:])
                    for g in groups[j]:
                        (a_dve if on_dve(j, g) else a_act).wait(pe, f"spread{j}_{g}", t)
                    for c in range(j + 1):
                        last = pe.matmul(pO[:, j, :], probsT[j % 2][:, c, :], vh[:, c, :], start=c == 0, stop=c == j)
                    a_pe.mark(last, step)

            order = [(j, g) for j in range(NT) for g in groups[j]]
            bank_of = {x: n % 2 for n, x in enumerate(order)}
            last_use = {order[n]: order[n - 2] for n in range(2, len(order))}
            with pe.Fori(0, NT) as t:
                for step in ORDER:
                    delta(step, t) if step in _DELTA else attend(step, t)
            g_pe.end()
            a_pe.end()

        @block.vector
        def _(dve):
            g_dve.start(dve)
            a_dve.start(dve)
            dve.wait_ge(zeroed, 3)

            def delta(step, t):
                if step == "rates":
                    g_pe.wait(dve, "decay", t, back=1)
                    g = m.g[:, ds(t, 1), :].rearrange("p a h -> p (a h)")
                    g_dve.mark(dve.tensor_tensor(g_cum[:], over_heads(m.c("cum")), over_width(g, P), ALU.mult), "g_cum")
                    g_pe.wait(dve, "rates", t)
                    g_pool.wait(dve, "kd1", t, back=1)
                    g_dve.mark(dve.tensor_copy(rate[:], gA[:, 0, 0:4 * GH]), "rate_copy")
                    g_dve.wait(dve, "rate_copy", t)
                    g_dve.mark(dve.tensor_tensor(rate[:, GH:2 * GH], rate[:, GH:2 * GH], rate[:, 0:GH], ALU.subtract), "rate")
                    g_pe.wait(dve, "decay", t)
                    g_dve.mark(dve.tensor_tensor(diff[:], gB[:], over_width(rate[:, 0:GH], P), ALU.subtract), "diff")
                    g_dve.wait(dve, "diff", t)
                    g_dve.mark(dve.tensor_tensor(diff[:], diff[:], over_heads(m.c("strict")), ALU.mult), "diff_masked")
                if step == "scaled":
                    g_act.wait(dve, "diff_exp", t)
                    g_dve.mark(dve.tensor_tensor(decay[:], diff[:], over_heads(m.c("causal")), ALU.mult), "decay")
                    dve.wait_ge(in_loaded["k"], 16 * t + 16)
                    beta = m.beta[:, ds(t, 1), :].rearrange("p a h -> p (a h)")
                    g_dve.mark(dve.tensor_tensor(kb[:], k_in[:], over_width(beta, P), ALU.mult), "kb")
                    for j in range(2):
                        last = dve.tensor_scalar(k_rate[:, j, :], rate_exp[:, GH:2 * GH],
                                                 m.c("chunk_cols")[:, j:j + 1], None, ALU.mult)
                    g_dve.mark(last, "k_rate")
                    g_dve.wait(dve, "kb", t)
                    g_dve.mark(dve.tensor_tensor(kbe[:], kb[:], over_width(rate_exp[:, 0:GH], P), ALU.mult), "kbe")
                    dve.wait_ge(in_loaded["q"], 16 * t + 16)
                    g_dve.mark(dve.tensor_tensor(qd[:], q_in[:], over_width(rate_exp[:, 0:GH], P), ALU.mult), "qd")
                if step == "turn_k":
                    g_pe.wait(dve, "kbT", t)
                    g_dve.mark(dve.tensor_copy(kbT[:], gA[:]), "kbT")
                if step == "turn_q":
                    g_pe.wait(dve, "qdT", t)
                    g_dve.mark(dve.tensor_copy(qdT[:], gC[:]), "qdT")
                if step == "overlap":
                    g_pe.wait(dve, "AT", t)
                    g_dve.mark(dve.tensor_tensor(AT[:], gA[:], decay[:], ALU.mult), "AT")
                    g_pe.wait(dve, "QKT", t)
                    g_dve.mark(dve.tensor_tensor(QKT[:], gB[:], decay[:], ALU.mult), "QKT")
                if step == "x0":
                    g_dve.wait(dve, "AT", t)
                    g_dve.mark(dve.tensor_tensor(first[:], AT[:], over_heads(m.c("level0")), ALU.mult), "first")
                    g_dve.wait(dve, "first", t)
                    g_dve.mark(dve.tensor_tensor(XT[:], over_heads(ident), first[:], ALU.subtract), "XT")
                if step[0] == "z" and step[1:].isdigit():
                    n = int(step[1:])
                    if n < 5:
                        g_pe.wait(dve, f"Z{n}", t)
                        g_dve.mark(dve.tensor_tensor(X[:], X[:], gB[:], ALU.subtract), f"X{n}")
                    g_pe.wait(dve, f"ZT{n}", t)
                    g_dve.mark(dve.tensor_tensor(XT[:], XT[:], gC[:], ALU.subtract), f"XT{n}")
                if step == "uw":
                    g_pe.wait(dve, "wT", t)
                    g_dve.mark(dve.tensor_copy(wT[:], gB[:]), "wT")
                if step[:-1] == "read":
                    j = int(step[-1])
                    rows = slice(CHUNK * j, CHUNK * (j + 1))
                    g_act.wait(dve, "u", t)
                    g_pe.wait(dve, f"wS{j}", t)
                    g_dve.mark(dve.tensor_tensor(v_new[rows], u[rows], gC[rows], ALU.subtract), f"v_new{j}")
                    g_dve.mark(dve.tensor_tensor(S_decayed[:], S[:], over_width(rate_exp[:, GH * (2 + j):GH * (3 + j)], P),
                                                 ALU.mult), f"S_decayed{j}")
                if step[:-1] == "write":
                    j = int(step[-1])
                    g_dve.wait(dve, f"S_decayed{j}", t)
                    g_pe.wait(dve, f"dS{j}", t)
                    g_dve.mark(dve.tensor_tensor(S[:], S_decayed[:], gB[:], ALU.add), f"S{j}")
                if step == "within":
                    g_act.wait(dve, "o1", t)
                    g_pe.wait(dve, "within", t)
                    g_dve.mark(dve.tensor_tensor(o[:], o[:], gC[:], ALU.add), "o")
                if step == "gate":
                    g_act.wait(dve, "o_sq", t)
                    g_dve.mark(dve.tensor_scalar(o_ms[:], o_ms[:], 1.0 / GDK, EPS, ALU.mult, ALU.add), "o_ms")
                    g_pool.wait(dve, "o_rs", t)
                    g_dve.mark(dve.tensor_tensor(o_norm[:], o[:], over_width(o_rs[:], P), ALU.mult), "o_norm")
                    dve.wait_ge(in_loaded["z"], 16 * t + 16)
                    g_dve.wait(dve, "o_norm", t)
                    g_dve.mark(dve.tensor_tensor(m.gdn_o[:, ds(t, 1), :].rearrange("p a (h w) -> p (a h) w", h=GH),
                                                 o_norm[:], z_in[:], ALU.mult), "o_out")

            def attend(step, t):
                if step == "up":
                    a_pe.wait(dve, "kv0", t)
                    a_dve.mark(dve.tensor_copy(kh[:, 0:4, 0:NOPE], pT[0][:, :, 0:NOPE]), "k0")
                    a_dve.mark(dve.tensor_copy(vh[:, 0:4, :], pT[0][:, :, NOPE:]), "v0")
                    a_act.wait(dve, "q1", t)
                    x1, x2 = qh[:, :, NOPE:NOPE + HALF], qh[:, :, NOPE + HALF:]
                    dve.tensor_tensor(prod[0][:], x1, m.cos[:], ALU.mult)
                    dve.tensor_tensor(prod[1][:], x2, m.sin[:], ALU.mult)
                    dve.tensor_tensor(prod[2][:], x2, m.cos[:], ALU.mult)
                    a_dve.mark(dve.tensor_tensor(prod[3][:], x1, m.sin[:], ALU.mult), "products")
                    a_dve.wait(dve, "products", t)
                    dve.tensor_tensor(x1, prod[0][:], prod[1][:], ALU.subtract)
                    a_dve.mark(dve.tensor_tensor(x2, prod[2][:], prod[3][:], ALU.add), "rope")
                if step == "turn":
                    for b in range(2):
                        a_pe.wait(dve, f"qT{b}", t)
                        a_dve.mark(dve.tensor_scalar(qhT[:, 512 * b:512 * b + 512], pS[0:QK, 512 * b:512 * b + 512],
                                                     QK ** -0.5, None, ALU.mult), f"qT{b}")
                if step[:5] == "score":
                    j = int(step[5:])
                    base = 512 * (j % 2) if j < 4 else 0
                    a_pe.wait(dve, step, t)
                    a_dve.mark(dve.tensor_reduce(neg_max[:, j:j + 1], pS[:, base:base + width_of(j)], AX_X, ALU.max,
                                                 negate=True), f"max{j}")
                if step[:6] == "spread":
                    j, g = int(step[6]), int(step[8])
                    if on_dve(j, g):
                        n = min(4, j + 1 - 4 * g)
                        a_pe.wait(dve, step, t)
                        a_dve.mark(dve.tensor_copy(probsT[j % 2][:, 4 * g:4 * g + n, :], pT[bank_of[(j, g)]][:, 0:n, :]), step)
                if step == "heads_out":
                    a_act.wait(dve, "exp7", t)
                    a_dve.mark(dve.reciprocal(row_inv[:], row_sum[:]), "row_inv")
                    a_dve.wait(dve, "row_inv", t)
                    a_pe.wait(dve, "value7", t)
                    a_dve.mark(dve.tensor_tensor(m.attn_o[:, :, ds(t * AV, AV)], pO[:], over_width(row_inv[:], AV), ALU.mult), "out")

            order = [(j, g) for j in range(NT) for g in groups[j]]
            bank_of = {x: n % 2 for n, x in enumerate(order)}
            with dve.Fori(0, NT) as t:
                for step in ORDER:
                    delta(step, t) if step in _DELTA else attend(step, t)
            g_dve.end()
            a_dve.end()

        @block.scalar
        def _(act):
            g_act.start(act)
            a_act.start(act)

            def delta(step, t):
                if step == "rates":
                    g_dve.wait(act, "rate", t)
                    g_act.mark(act.activation(rate_exp[:], rate[:], ACT.Exp), "rate_exp")
                    g_dve.wait(act, "diff_masked", t)
                    g_act.mark(act.activation(diff[:], diff[:], ACT.Exp), "diff_exp")
                if step == "turn_k":
                    g_pe.wait(act, "kT", t)
                    g_act.mark(act.copy(kT[:], gC[:]), "kT")
                if step == "turn_q":
                    g_pe.wait(act, "qT", t)
                    g_act.mark(act.copy(qT[:], gB[:]), "qT")
                if step == "x0":
                    g_pe.wait(act, "X", t)
                    g_act.mark(act.copy(X[:], gC[:]), "X")
                if step[0] == "y" and step[1:].isdigit():
                    n = int(step[1:])
                    g_pe.wait(act, f"Y{n}", t)
                    g_act.mark(act.copy(Y[:], gA[:]), f"Y{n}")
                if step == "uw":
                    g_pe.wait(act, "u", t)
                    g_act.mark(act.copy(u[:], gA[:]), "u")
                if step[:-1] == "read":
                    j = int(step[-1])
                    rows = slice(CHUNK * j, CHUNK * (j + 1))
                    g_pe.wait(act, f"qS{j}", t)
                    g_act.mark(act.copy(o[rows], gA[rows]), f"o{j}")
                if step == "within":
                    g_dve.wait(act, "o", t)
                    for h in range(GH):
                        last = act.activation(o_sq[:, h, :], o[:, h, :], ACT.Square, accum_out=o_ms[:, h:h + 1])
                    g_act.mark(last, "o_sq")

            def attend(step, t):
                if step == "up":
                    for b in range(2):
                        a_pe.wait(act, f"q{b}", t)
                        a_act.mark(act.copy(qh[:, 4 * b:4 * b + 4, :], pS4[b][:, :, 0:QK]), f"q{b}")
                    a_pe.wait(act, "kv1", t)
                    a_act.mark(act.copy(kh[:, 4:8, 0:NOPE], pT[1][:, :, 0:NOPE]), "k1")
                    a_act.mark(act.copy(vh[:, 4:8, :], pT[1][:, :, NOPE:]), "v1")
                if step == "turn":
                    for b in range(2):
                        a_pe.wait(act, f"kT{b}", t)
                        a_act.mark(act.copy(khT[:, 512 * b:512 * b + 512], pT[b][0:QK].rearrange("p t w -> p (t w)")), f"kT{b}")
                if step[:5] == "score":
                    j = int(step[5:])
                    base = 512 * (j % 2) if j < 4 else 0
                    a_dve.wait(act, f"max{j}", t)
                    a_act.mark(act.activation(probs[j % 2][:, 0:width_of(j)], pS[:, base:base + width_of(j)], ACT.Exp,
                                              bias=neg_max[:, j:j + 1], accum_out=row_sum[:, j:j + 1]), f"exp{j}")
                if step[:6] == "spread":
                    j, g = int(step[6]), int(step[8])
                    if not on_dve(j, g):
                        n = min(4, j + 1 - 4 * g)
                        a_pe.wait(act, step, t)
                        a_act.mark(act.copy(probsT[j % 2][:, 4 * g:4 * g + n, :], pT[bank_of[(j, g)]][:, 0:n, :]), step)

            order = [(j, g) for j in range(NT) for g in groups[j]]
            bank_of = {x: n % 2 for n, x in enumerate(order)}
            with act.Fori(0, NT) as t:
                for step in ORDER:
                    delta(step, t) if step in _DELTA else attend(step, t)
            g_act.end()
            a_act.end()


def route(nc, A, m):
    with ExitStack() as own:
        def sb(name, shape, dt=F32):
            return own.enter_context(nc.sbuf_tensor(name, shape, dt))

        def sem(name):
            return own.enter_context(nc.semaphore(name))

        def pair(name, shape, dt=F32):
            return [sb(f"{name}{u}", shape, dt) for u in range(2)]

        w_out = sb("w_out_sb", [P, KD, D_MODEL])
        router_w, router_b = sb("router_w_sb", [P, KD, NE]), sb("router_b_sb", [1, NE])
        gdn_w, mla_w, ffn_w = sb("gdn_w", [P, 1]), sb("mla_w", [P, 4]), sb("ffn_w", [P, KD])
        squares = pair("route_squares", [P, D_MODEL], mybir.dt.bfloat16)
        x, x2, h2 = pair("x", [P, D_MODEL]), pair("x2", [P, D_MODEL]), pair("h2", [P, D_MODEL])
        gdn_s, attn_n = pair("gdn_s", [P, GW]), pair("attn_n", [P, AH * AV])
        mixT, h2T = pair("mixT", [P, KD, P]), pair("h2T", [P, KD, P])
        ms_a, rs_a, ms_x, rs_x = (pair(n, [P, 1]) for n in ("ms_a", "rs_a", "ms_x", "rs_x"))
        power = sb("route_power", [P, 1])
        logits, top, index = pair("logits", [P, NE]), pair("top", [P, 8]), pair("index", [P, 8], U32)
        index_f, top_neg = pair("index_f", [P, TOPK]), pair("top_neg", [P, 1])
        chosen, placed = pair("chosen", [P, TOPK, NE]), pair("placed", [P, TOPK, NE])
        picked, seen, rows = pair("picked", [P, NE]), sb("seen", [P, NE]), pair("rows", [P, NE])
        dest_f, dest = pair("dest_f", [P, TOPK]), pair("dest", [P, TOPK], I32)
        gates, gate_sum, entry = pair("gates", [P, TOPK]), pair("gate_sum", [P, 1]), pair("entry", [P, TOPK, 2], I32)
        token = sb("token", [P, 1])
        pads = sb("pads", [P, NE * SEQ // P, 2], I32)
        count, items, ends, ended, base = (sb(n, [TABLE, NE]) for n in ("count", "items", "ends", "ended", "base"))
        over = sb("over", [TABLE, NE, ITEMS_OF_EXPERT])
        zeros = sb("zeros_e", [TABLE, NE])
        table_f = sb("table_f", [TABLE, 4])
        mine, tokens, wide = sb("mine", [TABLE, NE]), sb("tokens", [TABLE, 1]), sb("wide", [TABLE, WIDTHS])
        first_item = sb("first_item", [TABLE, 1])

        pT = [own.enter_context(nc.psum_tensor(f"rT{b}", [P, 4, P], F32)) for b in range(2)]
        pOut = [[own.enter_context(nc.psum_tensor(f"pOut{u}{b}", [P, 512], F32)) for b in range(2)] for u in range(2)]
        pL = own.enter_context(nc.psum_tensor("pL", [P, 512], F32))

        both = lambda names: [f"{n}{u}" for u in range(2) for n in names]
        r_pe = Stages(sem("r_pe"), both(["mixT", "out"]) + both(["h2T", "logits", "place"]))
        r_dve = Stages(sem("r_dve"), both(["ms_a", "attn_n", "mixT", "x2"])
                       + both(["ms_x", "h2", "h2T", "logits", "top", "index", "index_f", "chosen", "picked",
                               "top_neg", "rows", "seen", "placed", "dest_f", "dest", "gate_inv", "entry"]))
        r_act = Stages(sem("r_act"), both(["attn_sq", "gdn_s"]) + both(["x_sq", "gates"]))
        r_pool = Stages(sem("r_pool"), both(["rs_a"]) + both(["rs_x", "scattered"]))
        r_sp = Stages(sem("r_sp"), both(["stored"]))
        x_loaded = [sem(f"rx_loaded{u}") for u in range(2)]
        x2_stored, h2_stored = [sem(f"x2_stored{u}") for u in range(2)], [sem(f"h2_stored{u}") for u in range(2)]
        r_small, w_loaded, r_zeroed, pool_turn, dve_turn, pe_turn = (
            sem(n) for n in ("r_small", "w_out_loaded", "r_zeroed", "r_pool_turn", "r_dve_turn", "r_pe_turn"))
        filled, scattered, pads_made = sem("filled"), sem("scattered"), sem("pads_made")
        chain, counts_psum, table_psum = sem("r_chain"), sem("counts_psum"), sem("table_psum")
        ident = m.c("ident")
        block = own.enter_context(nc.Block())

        @block.sync
        def _(sp):
            r_sp.start(sp)
            sp.dma_start(gdn_w[:], A["gdn_norm"]).then_inc(r_small, 16)
            sp.dma_start(mla_w[:], A["mla_norm"]).then_inc(r_small, 16)
            sp.dma_start(ffn_w[:], A["norm_ffn"]).then_inc(r_small, 16)
            sp.dma_start(router_b[:], A["router_b"]).then_inc(r_small, 16)
            sp.dma_start(router_w[:], A["router_w"].rearrange("(k p) e -> p k e", p=P)).then_inc(r_small, 16)
            for k in range(KD):
                sp.dma_start(w_out[:, k, :], A["w_out"][k * P:(k + 1) * P, :]).then_inc(w_loaded, 16)
            sp.wait_ge(pads_made, 1)
            sp.dma_start(m.places.rearrange("(p n) c -> p n c", p=P), pads[:]).then_inc(filled, 16)
            with sp.Fori(0, NT // 2) as it:
                for u in range(2):
                    r_dve.wait(sp, f"x2{u}", it, back=1)
                    sp.dma_start(x[u][:], A["x"][ds((it * 2 + u) * P, P), :]).then_inc(x_loaded[u], 16)
                for u in range(2):
                    tile = ds((it * 2 + u) * P, P)
                    r_dve.wait(sp, f"x2{u}", it)
                    sp.dma_start(m.y[tile, :], x2[u][:]).then_inc(x2_stored[u], 16)
                    r_dve.wait(sp, f"h2{u}", it)
                    sp.dma_start(m.h2_rows[tile, :], h2[u][:]).then_inc(h2_stored[u], 16)
                    sp.wait_ge(x2_stored[u], 16 * it + 16)
                    sp.wait_ge(h2_stored[u], 16 * it + 16)
                    r_sp.mark_now(sp, f"stored{u}")
            r_sp.end()

        @block.gpsimd
        def _(pool):
            r_pool.start(pool)
            pool.memset(power[:], -0.5).then_inc(r_zeroed, 1)
            pool.memset(seen[:], 0.0).then_inc(r_zeroed, 1)
            pool.memset(zeros[:], 0.0).then_inc(r_zeroed, 1)
            pool.memset(pads[:, :, 1:2], 0)
            pool.memset(pads[:, :, 0:1], PAD).then_inc(pads_made, 1)
            pool.wait_ge(r_zeroed, 3)
            pool.wait_ge(filled, 16)
            with pool.Fori(0, NT // 2) as it:
                for u in range(2):
                    r_dve.wait(pool, f"ms_a{u}", it)
                    pool.sem_inc(pool_turn, 1)
                    r_pool.mark(pool.tensor_tensor(rs_a[u][:], ms_a[u][:], power[:], ALU.pow), f"rs_a{u}")
                for u in range(2):
                    r_dve.wait(pool, f"ms_x{u}", it)
                    pool.sem_inc(pool_turn, 1)
                    r_pool.mark(pool.tensor_tensor(rs_x[u][:], ms_x[u][:], power[:], ALU.pow), f"rs_x{u}")
                    r_dve.wait(pool, f"entry{u}", it)
                    pool.sem_inc(pool_turn, 1)
                    for k in range(TOPK):
                        pool.indirect_dma_start(m.places, bass.IndirectOffsetOnAxis(dest[u][:, k:k + 1].bitcast(U32), 0),
                                                entry[u][:, k, :], None).then_inc(scattered, 16)
                    pool.wait_ge(scattered, (it * 2 + u + 1) * 16 * TOPK)
                    r_pool.mark_now(pool, f"scattered{u}")
            r_pool.end()

        @block.tensor
        def _(pe):
            r_pe.start(pe)
            pe.wait_ge(w_loaded, 16 * KD)
            pe.wait_ge(r_small, 80)
            pe.wait_ge(r_zeroed, 3)
            with pe.Fori(0, NT // 2) as it:
                for u in range(2):
                    r_act.wait(pe, f"gdn_s{u}", it)
                    r_dve.wait(pe, f"attn_n{u}", it)
                    r_dve.wait(pe, "mixT0", it) if u else r_dve.wait(pe, "h2T1", it, back=1)
                    for k in range(4):
                        pe.transpose(pT[0][:, k, :], gdn_s[u][:, k * P:(k + 1) * P], ident)
                    for k in range(4):
                        last = pe.transpose(pT[1][:, k, :], attn_n[u][:, k * P:(k + 1) * P], ident)
                    r_pe.mark(last, f"mixT{u}")
                    r_dve.wait(pe, f"mixT{u}", it)
                    for b in range(2):
                        for k in range(KD):
                            last = pe.matmul(pOut[u][b][:], mixT[u][:, k, :], w_out[:, k, 512 * b:512 * b + 512],
                                             start=k == 0, stop=k == KD - 1)
                    r_pe.mark(last, f"out{u}")
                for u in range(2):
                    r_dve.wait(pe, f"h2{u}", it)
                    r_dve.wait(pe, "h2T0", it) if u else r_dve.wait(pe, "mixT1", it)
                    for k in range(KD):
                        last = pe.transpose(pT[k // 4][:, k % 4, :], h2[u][:, k * P:(k + 1) * P], ident)
                    r_pe.mark(last, f"h2T{u}")
                    r_dve.wait(pe, f"h2T{u}", it)
                    pe.matmul(pL[:, 0:NE], m.c("ones", 1), router_b[:], start=True, stop=False)
                    for k in range(KD):
                        last = pe.matmul(pL[:, 0:NE], h2T[u][:, k, :], router_w[:, k, :], start=False, stop=k == KD - 1)
                    r_pe.mark(last, f"logits{u}")
                    r_dve.wait(pe, f"picked{u}", it)
                    pe.matmul(pL[:, NE:2 * NE], m.c("before"), picked[u][:], start=True, stop=False)
                    r_pe.mark(pe.matmul(pL[:, NE:2 * NE], m.c("ones"), seen[:], start=False, stop=True), f"place{u}")
            r_pe.end()
            r_dve.wait(pe, "entry1", NT // 2 - 1)
            pe.matmul(pL[0:TABLE, 0:NE], m.c("ones")[:, 0:TABLE], seen[:], start=True, stop=True).then_inc(counts_psum, 1)
            pe.wait_ge(chain, 21)
            for c in range(4):
                last = pe.transpose(pL[0:1, TABLE * c:TABLE * (c + 1)], table_f[:, c:c + 1], ident[0:TABLE, 0:TABLE])
            last.then_inc(table_psum, 1)

        @block.scalar
        def _(act):
            r_act.start(act)
            with act.Fori(0, NT // 2) as it:
                for u in range(2):
                    i = ds(it * 2 + u, 1)
                    r_pool.wait(act, f"rs_a{u}", it, back=1)
                    act.sem_inc(dve_turn, 1)
                    r_act.mark(act.activation(squares[u][:, 0:AH * AV], m.attn_o[:, i, :].rearrange("p a w -> p (a w)"), ACT.Square,
                                              accum_out=ms_a[u][:]), f"attn_sq{u}")
                    r_pe.wait(act, f"mixT{u}", it, back=1)
                    act.sem_inc(dve_turn, 1)
                    r_act.mark(act.copy(gdn_s[u][:], m.gdn_o[:, i, :].rearrange("p a w -> p (a w)")), f"gdn_s{u}")
                for u in range(2):
                    r_dve.wait(act, f"x2{u}", it)
                    r_act.mark(act.activation(squares[u][:], x2[u][:], ACT.Square, accum_out=ms_x[u][:]), f"x_sq{u}")
                    r_dve.wait(act, f"top_neg{u}", it)
                    r_act.mark(act.activation(gates[u][:], top[u][:, 0:TOPK], ACT.Exp, bias=top_neg[u][:],
                                              accum_out=gate_sum[u][:]), f"gates{u}")
            r_act.end()

        @block.vector
        def _(dve):
            r_dve.start(dve)
            dve.wait_ge(r_small, 80)
            dve.wait_ge(r_zeroed, 3)
            dve.tensor_copy(token[:], m.c("row")).then_inc(r_zeroed, 1)
            dve.wait_ge(r_zeroed, 4)
            with dve.Fori(0, NT // 2) as it:
                for u in range(2):
                    r_act.wait(dve, f"attn_sq{u}", it)
                    r_dve.mark(dve.tensor_scalar(ms_a[u][:], ms_a[u][:], 1.0 / (AH * AV), EPS, ALU.mult, ALU.add), f"ms_a{u}")
                    r_pool.wait(dve, f"rs_a{u}", it)
                    r_dve.mark(dve.tensor_scalar(attn_n[u][:], m.attn_o[:, ds(it * 2 + u, 1), :].rearrange("p a w -> p (a w)"),
                                                 rs_a[u][:], None, ALU.mult), f"attn_n{u}")
                    r_pe.wait(dve, f"mixT{u}", it)
                    dve.tensor_scalar(mixT[u][:, 0:4, :], pT[0][:], gdn_w[:], None, ALU.mult)
                    r_dve.mark(dve.tensor_tensor(mixT[u][:, 4:8, :], pT[1][:], over_width(mla_w[:], P), ALU.mult), f"mixT{u}")
                    r_pe.wait(dve, f"out{u}", it)
                    dve.wait_ge(x_loaded[u], 16 * it + 16)
                    r_sp.wait(dve, f"stored{u}", it, back=1)
                    for b in range(2):
                        cols = slice(512 * b, 512 * b + 512)
                        last = dve.tensor_tensor(x2[u][:, cols], pOut[u][b][:], x[u][:, cols], ALU.add)
                    r_dve.mark(last, f"x2{u}")
                for u in range(2):
                    r_act.wait(dve, f"x_sq{u}", it)
                    r_dve.mark(dve.tensor_scalar(ms_x[u][:], ms_x[u][:], 1.0 / D_MODEL, EPS, ALU.mult, ALU.add), f"ms_x{u}")
                    r_pool.wait(dve, f"rs_x{u}", it)
                    r_dve.mark(dve.tensor_scalar(h2[u][:], x2[u][:], rs_x[u][:], None, ALU.mult), f"h2{u}")
                    r_pe.wait(dve, f"h2T{u}", it)
                    for b in range(2):
                        last = dve.tensor_tensor(h2T[u][:, 4 * b:4 * b + 4, :], pT[b][:], over_width(ffn_w[:, 4 * b:4 * b + 4], P), ALU.mult)
                    r_dve.mark(last, f"h2T{u}")
                    r_pe.wait(dve, f"logits{u}", it)
                    r_dve.mark(dve.tensor_copy(logits[u][:], pL[:, 0:NE]), f"logits{u}")
                    r_dve.wait(dve, f"logits{u}", it)
                    dve.sem_inc(dve_turn, 1)
                    r_dve.mark(dve.max(top[u][:], logits[u][:]), f"top{u}")
                    r_dve.wait(dve, f"top{u}", it)
                    dve.sem_inc(dve_turn, 1)
                    r_dve.mark(dve.max_index(index[u][:], top[u][:], logits[u][:]), f"index{u}")
                    r_dve.wait(dve, f"index{u}", it)
                    r_dve.mark(dve.tensor_copy(index_f[u][:], index[u][:, 0:TOPK]), f"index_f{u}")
                    r_dve.wait(dve, f"index_f{u}", it)
                    r_dve.mark(dve.tensor_tensor(chosen[u][:], over_heads(m.c("experts"), TOPK), over_width(index_f[u][:], NE),
                                                 ALU.is_equal), f"chosen{u}")
                    r_dve.wait(dve, f"chosen{u}", it)
                    r_dve.mark(dve.tensor_reduce(picked[u][:], chosen[u][:].rearrange("p k e -> p e k"), AX_X, ALU.add), f"picked{u}")
                    r_dve.mark(dve.tensor_scalar(top_neg[u][:], top[u][:, 0:1], -1.0, None, ALU.mult), f"top_neg{u}")
                    r_pe.wait(dve, f"place{u}", it)
                    r_dve.mark(dve.tensor_tensor(rows[u][:], pL[:, NE:2 * NE], m.c("expert_rows"), ALU.add), f"rows{u}")
                    r_dve.mark(dve.tensor_tensor(seen[:], seen[:], picked[u][:], ALU.add), f"seen{u}")
                    r_dve.wait(dve, f"rows{u}", it)
                    r_dve.mark(dve.tensor_tensor(placed[u][:], chosen[u][:], over_heads(rows[u][:], TOPK), ALU.mult), f"placed{u}")
                    r_dve.wait(dve, f"placed{u}", it)
                    r_dve.mark(dve.tensor_reduce(dest_f[u][:], placed[u][:], AX_X, ALU.add), f"dest_f{u}")
                    r_dve.wait(dve, f"dest_f{u}", it)
                    r_pool.wait(dve, f"scattered{u}", it, back=1)
                    r_dve.mark(dve.tensor_copy(dest[u][:], dest_f[u][:]), f"dest{u}")
                    r_act.wait(dve, f"gates{u}", it)
                    r_dve.mark(dve.reciprocal(gate_sum[u][:], gate_sum[u][:]), f"gate_inv{u}")
                    r_dve.wait(dve, f"gate_inv{u}", it)
                    dve.tensor_copy(entry[u][:, :, 0:1], bc(token[:].unsqueeze(2), [P, TOPK, 1]))
                    r_dve.mark(dve.tensor_scalar(entry[u][:, :, 1:2].bitcast(F32), gates[u][:].unsqueeze(2), gate_sum[u][:], None,
                                                 ALU.mult), f"entry{u}")
                    r_dve.wait(dve, f"entry{u}", it)
                    dve.tensor_scalar(token[:], token[:], float(P), None, ALU.add)
            r_dve.end()
            link = Chain(dve, chain).link
            dve.wait_ge(counts_psum, 1)
            link(dve.tensor_copy(count[:], pL[0:TABLE, 0:NE]))
            link(dve.tensor_tensor(over[:], over_width(count[:], ITEMS_OF_EXPERT), over_heads(m.c("bounds", TABLE), NE), ALU.is_gt))
            link(dve.tensor_reduce(items[:], over[:], AX_X, ALU.add))
            link(dve.tensor_tensor_scan(ends[:], items[:], zeros[:], 0.0, ALU.add, ALU.add))
            link(dve.tensor_scalar(ended[:], ends[:], m.c("row", TABLE), None, ALU.is_le))
            link(dve.tensor_tensor(base[:], ended[:], items[:], ALU.mult))
            link(dve.tensor_reduce(first_item[:], base[:], AX_X, ALU.add))
            link(dve.tensor_reduce(table_f[:, 0:1], ended[:], AX_X, ALU.add))
            link(dve.tensor_scalar(table_f[:, 0:1], table_f[:, 0:1], float(NE - 1), None, ALU.min))
            link(dve.tensor_tensor(first_item[:], m.c("row", TABLE), first_item[:], ALU.subtract))
            link(dve.tensor_scalar(table_f[:, 1:2], table_f[:, 0:1], float(SEQ), None, ALU.mult))
            link(dve.scalar_tensor_tensor(out=table_f[:, 1:2], in0=first_item[:], scalar=float(ITEM), in1=table_f[:, 1:2],
                                          op0=ALU.mult, op1=ALU.add))
            link(dve.tensor_scalar(table_f[:, 1:2], table_f[:, 1:2], float(PLACES - ITEM), None, ALU.min))
            link(dve.tensor_copy(table_f[:, 2:3], ends[:, NE - 1:NE]))
            link(dve.tensor_scalar(mine[:], m.c("experts", TABLE), table_f[:, 0:1], None, ALU.is_equal))
            link(dve.tensor_tensor(mine[:], mine[:], count[:], ALU.mult))
            link(dve.tensor_reduce(tokens[:], mine[:], AX_X, ALU.add))
            link(dve.scalar_tensor_tensor(out=tokens[:], in0=first_item[:], scalar=-float(ITEM), in1=tokens[:],
                                          op0=ALU.mult, op1=ALU.add))
            link(dve.tensor_scalar(wide[:], m.c("steps", TABLE), tokens[:], None, ALU.is_lt))
            link(dve.tensor_reduce(table_f[:, 3:4], wide[:], AX_X, ALU.add))
            link(dve.tensor_scalar(table_f[:, 3:4], table_f[:, 3:4], 1.0, None, ALU.max))
            dve.wait_ge(table_psum, 1)
            link(dve.tensor_copy(m.table[:], pL[0:1, 0:4 * TABLE]))


W1_CHUNKS, W2_CHUNKS = 4, 2


def experts(nc, A, m):
    with ExitStack() as own:
        def sb(name, shape, dt=F32):
            return own.enter_context(nc.sbuf_tensor(name, shape, dt))

        def sem(name):
            return own.enter_context(nc.semaphore(name))

        w1 = [sb(f"w1_{c}", [P, KD, 512]) for c in range(W1_CHUNKS)]
        w2 = [sb(f"w2_{c}", [P, KD, 512]) for c in range(W2_CHUNKS)]
        b1, b2, ffn_w = sb("b1_sb", [P, NE, KD, 2]), sb("b2_sb", [P, NE, KD]), sb("ffn_cols", [P, KD])
        b1_item, b2_item = sb("b1_item", [P, KD, 2]), sb("b2_item", [P, KD])
        next_places, places = sb("next_places", [P, BLOCKS, 2], I32), sb("item_places", [P, BLOCKS, 2], I32)
        rows = sb("item_rows", [P, BLOCKS, D_MODEL])
        xT, act_sb, yT = sb("xT", [P, KD, ITEM]), sb("act_sb", [P, KD, ITEM]), sb("yT", [P, KD, ITEM])
        glu, lin, sig = ([sb(f"{n}{u}", [P, ITEM]) for u in range(2)] for n in ("glu", "lin", "sig"))
        y_rows = sb("y_rows", [P, BLOCKS, D_MODEL])
        pH = [own.enter_context(nc.psum_tensor(f"pH{b}", [P, 2, ITEM], F32)) for b in range(4)]
        pY = [own.enter_context(nc.psum_tensor(f"pY{b}", [P, 2, ITEM], F32)) for b in range(2)]
        pT = [own.enter_context(nc.psum_tensor(f"yT{b}", [P, 2, 2, P], F32)) for b in range(2)]

        w1_in, w2_in = [sem(f"w1_in{c}") for c in range(W1_CHUNKS)], [sem(f"w2_in{c}") for c in range(W2_CHUNKS)]
        small, cleared, psum_cleared = sem("e_small"), sem("e_cleared"), sem("e_psum_cleared")
        pool_turn, dve_turn = sem("e_pool_turn"), sem("e_dve_turn")
        hidden = Stages(sem("hidden"), [str(j) for j in range(KD)])
        feature = Stages(sem("feature"), [str(k) for k in range(KD)])
        x_turned = Stages(sem("x_turned"), [str(f) for f in range(2 * BLOCKS)])
        y_turned = Stages(sem("y_turned"), [str(q) for q in range(KD // 2)])
        e_act = Stages(sem("e_act"), [f"sig{j}" for j in range(KD)] + [f"y{k}" for k in range(KD)])
        x_read = Stages(sem("x_read"), [str(f) for f in range(2 * BLOCKS)])
        e_dve = Stages(sem("e_dve"), ["bias"] + [x for j in range(KD + 1) for x in
                                                 ([f"glu{j}", f"lin{j}", f"one{j}", f"prod{j}"] if j < KD else [])
                                                 + ([f"act{j - 1}"] if j else [])]
                       + [f"y{q}" for q in range(KD // 2)])
        e_pool = Stages(sem("e_pool"), ["gathered_now", "current"])
        gathered, added, listed = sem("gathered"), sem("added"), sem("listed")
        ident = m.c("ident")

        def number_of_items(eng):
            return eng.value_load(m.table[0:1, 2 * TABLE:2 * TABLE + 1], min_val=1, max_val=MAX_ITEMS)

        def expert_of(eng, n):
            return eng.value_load(m.table[0:1, ds(n, 1)], min_val=0, max_val=NE - 1)

        def place_of(eng, n):
            return eng.value_load(m.table[0:1, ds(n + TABLE, 1)], min_val=0, max_val=PLACES - ITEM)

        def width_of(eng, n):
            return eng.value_load(m.table[0:1, ds(n + 3 * TABLE, 1)], min_val=1, max_val=WIDTHS)

        block = own.enter_context(nc.Block())

        @block.sync
        def _(sp):
            with sp.Fori(0, number_of_items(sp)) as n:
                e = expert_of(sp, n)
                w1_rows = A["w1"][ds(e, 1)].rearrange("a (k p) f -> p (a k) f", p=P)
                w2_rows = A["w2"][ds(e, 1)].rearrange("a (k p) f -> p (a k) f", p=P)
                for c in range(W1_CHUNKS):
                    hidden.wait(sp, str(2 * c + 1), n, back=1)
                    sp.dma_start(w1[c][:], w1_rows[:, :, 512 * c:512 * c + 512]).then_inc(w1_in[c], 16)
                for c in range(W2_CHUNKS):
                    feature.wait(sp, str(4 * c + 3), n, back=1)
                    sp.dma_start(w2[c][:], w2_rows[:, :, 512 * c:512 * c + 512]).then_inc(w2_in[c], 16)

        @block.gpsimd
        def _(pool):
            e_pool.start(pool)

            def list_places(n):
                pool.dma_start(next_places[:], m.places[ds(place_of(pool, n), ITEM), :].rearrange("(b p) c -> p b c", p=P))\
                    .then_inc(listed, 16)

            def gather():
                for b in range(BLOCKS):
                    pool.indirect_dma_start(rows[:, b, :], None, m.h2_rows,
                                            bass.IndirectOffsetOnAxis(next_places[:, b, 0:1].bitcast(U32), 0),
                                            bounds_check=SEQ - 1, oob_is_err=False).then_inc(gathered, 16)

            def take_places():
                pool.tensor_copy(places[:, :, 0:1], next_places[:, :, 0:1]).then_inc(pool_turn, 1)
                return pool.tensor_copy(places[:, :, 1:2].bitcast(F32), next_places[:, :, 1:2].bitcast(F32))

            pool.memset(rows[:], 0.0).then_inc(cleared, 1)
            pool.wait_ge(cleared, 1)
            items = number_of_items(pool)
            list_places(0)
            pool.wait_ge(listed, 16)
            gather()
            pool.wait_ge(gathered, 16 * BLOCKS)
            take_places().then_inc(cleared, 1)
            pool.wait_ge(cleared, 2)
            list_places(1)
            pool.wait_ge(listed, 32)
            with pool.Fori(0, items) as n:
                x_turned.wait(pool, "3", n, back=1)
                pool.sem_inc(pool_turn, 1)
                gather()
                pool.wait_ge(gathered, 16 * BLOCKS * n + 32 * BLOCKS)
                e_pool.mark_now(pool, "gathered_now")
                e_dve.wait(pool, "y3", n)
                pool.sem_inc(pool_turn, 1)
                for b in range(BLOCKS):
                    pool.indirect_dma_start(m.y, bass.IndirectOffsetOnAxis(places[:, b, 0:1].bitcast(U32), 0), y_rows[:, b, :],
                                            None, bounds_check=SEQ - 1, oob_is_err=False, compute_op=ALU.add).then_inc(added, 16)
                pool.wait_ge(added, 16 * BLOCKS * n + 16 * BLOCKS)
                pool.sem_inc(pool_turn, 1)
                e_pool.mark(take_places(), "current")
                e_pool.wait(pool, "current", n)
                pool.sem_inc(pool_turn, 1)
                list_places(n + 2)
                pool.wait_ge(listed, 16 * n + 48)
                pool.sem_inc(pool_turn, 1)
            e_pool.end()

        @block.tensor
        def _(pe):
            for stages in (hidden, feature, y_turned):
                stages.start(pe)
            items = number_of_items(pe)

            def turn_rows(n, first=False):
                for f in range(2 * BLOCKS):
                    if not first:
                        e_dve.wait(pe, f"prod{4 + f}", n)
                    for k in range(4):
                        at = (4 * (f % 2) + k) * P
                        last = pe.transpose(pH[f][:].rearrange("p a (b w) -> p (a b) w", w=P)[:, k, :],
                                            rows[:, f // 2, at:at + P], ident)
                    if first:
                        last.then_inc(x_turned.sem, 1)
                    else:
                        x_turned.mark(last, str(f))

            def hidden_products(n, width):
                hidden.made = []
                for j in range(KD):
                    if j % 2 == 0:
                        pe.wait_ge(w1_in[j // 2], 16 * n + 16)
                    if j < 4:
                        x_read.wait(pe, "3", n, back=1)
                    else:
                        e_dve.wait(pe, f"lin{j - 4}", n)
                    for part in range(2):
                        for k in range(KD):
                            at = 256 * (j % 2) + part
                            last = pe.matmul(pH[j % 4][:, part, 0:width], w1[j // 2][:, k, at:at + 255:2], xT[:, k, 0:width],
                                             start=k == 0, stop=k == KD - 1)
                    hidden.mark(last, str(j))

            def feature_products(n, q, width):
                for k in (2 * q, 2 * q + 1):
                    if k % 4 == 0:
                        pe.wait_ge(w2_in[k // 4], 16 * n + 16)
                    for j in range(KD):
                        last = pe.matmul(pY[q % 2][:, k % 2, 0:width], w2[k // 4][:, j, P * (k % 4):P * (k % 4) + P],
                                         act_sb[:, j, 0:width], start=j == 0, stop=j == KD - 1)
                    feature.mark(last, str(k))

            def turn_features(n, q):
                e_act.wait(pe, f"y{2 * q + 1}", n)
                if q >= 2:
                    e_dve.wait(pe, f"y{q - 2}", n)
                else:
                    e_dve.wait(pe, f"y{q + 2}", n, back=1)
                for b in range(BLOCKS):
                    for k in range(2):
                        last = pe.transpose(pT[q % 2][:, b, k, :], yT[:, 2 * q + k, b * P:(b + 1) * P], ident)
                return last

            pe.wait_ge(cleared, 2)
            pe.wait_ge(psum_cleared, 8)
            turn_rows(0, first=True)
            with pe.Fori(0, items) as n:
                width = width_of(pe, n)
                for steps in range(1, WIDTHS + 1):
                    with pe.If(width == steps):
                        hidden_products(n, steps * STEP)
                e_pool.wait(pe, "gathered_now", n)
                turn_rows(n)
                e_dve.wait(pe, f"act{KD - 1}", n)
                for steps in range(1, WIDTHS + 1):
                    with pe.If(width == steps):
                        feature.made, y_turned.made = [], []
                        for q in range(KD // 2 + 1):
                            if q < KD // 2:
                                if q >= 2:
                                    e_act.wait(pe, f"y{2 * q - 3}", n)
                                feature_products(n, q, steps * STEP)
                            if q:
                                y_turned.mark(turn_features(n, q - 1), str(q - 1))
            for stages in (hidden, feature, y_turned, x_turned):
                stages.end()

        @block.scalar
        def _(act):
            e_act.start(act)
            act.dma_start(b1[:], A["b1"]).then_inc(small, 16)
            act.dma_start(b2[:], A["b2"]).then_inc(small, 16)
            act.dma_start(ffn_w[:], A["norm_ffn"]).then_inc(small, 16)
            with act.Fori(0, number_of_items(act)) as n:
                for j in range(KD):
                    e_dve.wait(act, f"glu{j}", n)
                    e_act.mark(act.activation(sig[j % 2][:], glu[j % 2][:], ACT.Sigmoid, scale=ALPHA), f"sig{j}")
                for q in range(KD // 2):
                    for k in (2 * q, 2 * q + 1):
                        feature.wait(act, str(2 * q + 1), n)
                        e_act.mark(act.activation(yT[:, k, :], pY[q % 2][:, k % 2, :], ACT.Identity, bias=b2_item[:, k:k + 1]), f"y{k}")
            e_act.end()

        @block.vector
        def _(dve):
            e_dve.start(dve)
            for bank in pH + pY + pT:
                dve.memset(bank[:], 0.0).then_inc(psum_cleared, 1)
            dve.wait_ge(psum_cleared, 8)
            dve.wait_ge(small, 48)

            def take_rows(f):
                b, k = f // 2, 4 * (f % 2)
                return dve.tensor_tensor(xT[:, k:k + 4, b * P:(b + 1) * P], pH[f][:].rearrange("p a (b w) -> p (a b) w", w=P),
                                         over_width(ffn_w[:, k:k + 4], P), ALU.mult)

            for f in range(2 * BLOCKS):
                dve.wait_ge(x_turned.sem, f + 1)
                take_rows(f).then_inc(x_read.sem, 1)
            with dve.Fori(0, number_of_items(dve)) as n:
                e = expert_of(dve, n)
                e_act.wait(dve, f"y{KD - 1}", n, back=1)
                dve.sem_inc(dve_turn, 1)
                dve.tensor_copy(b1_item[:].unsqueeze(1), b1[:, ds(e, 1), :, :])
                e_dve.mark(dve.tensor_copy(b2_item[:].unsqueeze(1), b2[:, ds(e, 1), :]), "bias")
                e_dve.wait(dve, "bias", n)
                for j in range(KD + 1):
                    u = j % 2
                    if j < KD:
                        hidden.wait(dve, str(j), n)
                        if j >= 2:
                            e_dve.wait(dve, f"act{j - 2}", n)
                        e_dve.mark(dve.tensor_scalar(glu[u][:], pH[j % 4][:, 0, :], b1_item[:, j, 0:1], LIMIT, ALU.add, ALU.min), f"glu{j}")
                        e_dve.mark(dve.tensor_scalar(lin[u][:], pH[j % 4][:, 1, :], b1_item[:, j, 1:2], LIMIT, ALU.add, ALU.min), f"lin{j}")
                        e_dve.wait(dve, f"lin{j}", n)
                        e_dve.mark(dve.tensor_scalar(lin[u][:], lin[u][:], -LIMIT, 1.0, ALU.max, ALU.add), f"one{j}")
                        e_dve.wait(dve, f"one{j}", n)
                        e_dve.mark(dve.tensor_tensor(lin[u][:], lin[u][:], glu[u][:], ALU.mult), f"prod{j}")
                    if j:
                        e_act.wait(dve, f"sig{j - 1}", n)
                        e_dve.wait(dve, f"prod{j - 1}", n)
                        e_dve.mark(dve.tensor_tensor(act_sb[:, j - 1, :], lin[1 - u][:], sig[1 - u][:], ALU.mult), f"act{j - 1}")
                for f in range(2 * BLOCKS):
                    x_turned.wait(dve, str(f), n)
                    x_read.mark(take_rows(f), str(f))
                e_pool.wait(dve, "current", n, back=1)
                for q in range(KD // 2):
                    y_turned.wait(dve, str(q), n)
                    for b in range(BLOCKS):
                        last = dve.tensor_scalar(y_rows[:, b, 2 * q * P:(2 * q + 2) * P], pT[q % 2][:, b].rearrange("p k w -> p (k w)"),
                                                 places[:, b, 1:2].bitcast(F32), None, ALU.mult)
                    e_dve.mark(last, f"y{q}")
            e_dve.end()
            x_read.end()


def finish(nc, A, m, out):
    with ExitStack() as own:
        def sb(name, shape, dt=F32):
            return own.enter_context(nc.sbuf_tensor(name, shape, dt))

        def sem(name):
            return own.enter_context(nc.semaphore(name))

        y = [sb(f"y_in{i}", [P, D_MODEL]) for i in range(NT)]
        res = [sb(f"res{i}", [P, D_MODEL]) for i in range(NT)]
        sq = [sb(f"final_sq{i}", [P, D_MODEL], mybir.dt.bfloat16) for i in range(2)]
        ms, rs, power, w = sb("ms", [P, NT]), sb("rs_final", [P, NT]), sb("final_power", [P, NT]), sb("final_w", [P, D_MODEL])
        y_in, w_in = [sem(f"y_in_done{i}") for i in range(NT)], sem("final_w_in")
        squared, mean, root, ready, stored, f_zero = (sem(n) for n in ("squared", "mean", "root", "ready", "stored", "f_zero"))
        block = own.enter_context(nc.Block())

        @block.sync
        def _(sp):
            for i in range(NT):
                sp.dma_start(y[i][:], m.y[i * P:(i + 1) * P, :]).then_inc(y_in[i], 16)
            sp.dma_start(w[:], bc(A["norm_final"], [P, D_MODEL])).then_inc(w_in, 16)
            for i in range(NT):
                sp.wait_ge(ready, i + 1)
                sp.dma_start(out[i * P:(i + 1) * P, :], res[i][:]).then_inc(stored, 16)
            sp.wait_ge(stored, 16 * NT)

        @block.scalar
        def _(act):
            for i in range(NT):
                act.wait_ge(y_in[i], 16)
                if i >= 2:
                    act.wait_ge(squared, i - 1)
                act.activation(sq[i % 2][:], y[i][:], ACT.Square, accum_out=ms[:, i:i + 1]).then_inc(squared, 1)

        @block.gpsimd
        def _(pool):
            pool.memset(power[:], -0.5).then_inc(f_zero, 1)
            pool.wait_ge(f_zero, 1)
            for i in range(NT):
                pool.wait_ge(mean, i + 1)
                pool.tensor_tensor(rs[:, i:i + 1], ms[:, i:i + 1], power[:, 0:1], ALU.pow).then_inc(root, 1)

        @block.vector
        def _(dve):
            dve.wait_ge(w_in, 16)
            for i in range(NT):
                dve.wait_ge(squared, i + 1)
                dve.tensor_scalar(ms[:, i:i + 1], ms[:, i:i + 1], 1.0 / D_MODEL, EPS, ALU.mult, ALU.add).then_inc(mean, 1)
                dve.wait_ge(root, i + 1)
                dve.scalar_tensor_tensor(out=res[i][:], in0=y[i][:], scalar=rs[:, i:i + 1], in1=w[:],
                                         op0=ALU.mult, op1=ALU.mult).then_inc(ready, 1)


def build(nc, A, out):
    with ExitStack() as ctx:
        m = Memory()

        def sb_in(stack, name, shape, dt=F32):
            return stack.enter_context(nc.sbuf_tensor(name, shape, dt))

        m.const = sb_in(ctx, "const_sb", [P, CONSTS])
        m.gdn_in = nc.dram_tensor("gdn_in", [SEQ, 4 * GW], F32, kind="Internal").ap()
        m.y = nc.dram_tensor("y", [SEQ, D_MODEL], F32, kind="Internal").ap()
        m.h2_rows = nc.dram_tensor("h2_rows", [SEQ, D_MODEL], F32, kind="Internal").ap()
        m.places = nc.dram_tensor("places", [PLACES, 2], I32, kind="Internal").ap()
        m.table = sb_in(ctx, "table", [1, 4 * TABLE], I32)
        with ExitStack() as mixed:
            m.gdn_o = sb_in(mixed, "gdn_o", [P, NT, GW])
            m.attn_o = sb_in(mixed, "attn_o", [P, NT, AH * AV])
            with ExitStack() as front:
                m.cqT = sb_in(front, "cqT", [P, KQ, SEQ])
                m.ckvT = sb_in(front, "ckvT", [P, KKV, SEQ])
                m.ab = sb_in(front, "ab", [P, NT, 2 * GH])
                m.k_rope = sb_in(front, "k_rope", [P, NT, ROPE])
                m.g, m.beta = (sb_in(front, n, [P, NT, GH]) for n in ("g", "beta"))
                m.cos, m.sin = (sb_in(front, n, [P, NT, HALF]) for n in ("cos", "sin"))
                m.kh = sb_in(front, "kh", [P, NT, QK])
                project(nc, A, m)
                prepare(nc, A, m)
                mix(nc, A, m)
            route(nc, A, m)
        experts(nc, A, m)
        finish(nc, A, m, out)


def _cols(w, k):
    return np.ascontiguousarray(np.asarray(w).reshape(k, P).T)


def _layout(x, positions, norm_mix_w, w_in, conv_w, a_log, dt_bias, gdn_norm_w, q_norm_w, w_uq, kv_norm_w, w_ukv,
            mla_out_norm_w, w_out, norm_ffn_w, router_w, router_b, w1, b1, w2, b2, norm_final_w):
    return {
        "const": CONST,
        "x": np.asarray(x).reshape(SEQ, D_MODEL),
        "positions": np.ascontiguousarray(np.asarray(positions).reshape(NT, P).T),
        "norm_mix": _cols(norm_mix_w, KD),
        "w_in": np.asarray(w_in).reshape(D_MODEL, D_IN),
        "conv_w": np.ascontiguousarray(np.asarray(conv_w).reshape(CONV, 12, P).transpose(2, 1, 0)),
        "a_log": np.asarray(a_log).reshape(1, GH),
        "dt_bias": np.asarray(dt_bias).reshape(1, GH),
        "gdn_norm": _cols(gdn_norm_w, 1),
        "q_norm": _cols(q_norm_w, KQ),
        "w_uq": np.asarray(w_uq).reshape(Q_LORA, AH * QK),
        "kv_norm": _cols(kv_norm_w, KKV),
        "w_ukv": np.asarray(w_ukv).reshape(KV_LORA, AH * (NOPE + AV)),
        "mla_norm": _cols(mla_out_norm_w, AH * AV // P),
        "w_out": np.asarray(w_out).reshape(D_MODEL, D_MODEL),
        "norm_ffn": _cols(norm_ffn_w, KD),
        "router_w": np.asarray(router_w).reshape(D_MODEL, NE),
        "router_b": np.asarray(router_b).reshape(1, NE),
        "w1": np.asarray(w1).reshape(NE, D_MODEL, 2 * D_FF),
        "b1": np.ascontiguousarray(np.asarray(b1).reshape(NE, KD, P, 2).transpose(2, 0, 1, 3)),
        "w2": np.asarray(w2).reshape(NE, D_FF, D_MODEL),
        "b2": np.ascontiguousarray(np.asarray(b2).reshape(NE, KD, P).transpose(2, 0, 1)),
        "norm_final": np.asarray(norm_final_w).reshape(1, D_MODEL),
    }


def kernel(**inputs):
    import concourse.bacc as bacc
    from concourse.bass_utils import run_bass_kernel_spmd

    arrays = _layout(**inputs)
    nc = bacc.Bacc("TRN2", target_bir_lowering=False, num_devices=1)
    A = {name: nc.dram_tensor(f"in_{name}", list(a.shape), mybir.dt.from_np(a.dtype), kind="ExternalInput").ap()
         for name, a in arrays.items()}
    out = nc.dram_tensor("out", [SEQ, D_MODEL], F32, kind="ExternalOutput").ap()
    build(nc, A, out)
    r = run_bass_kernel_spmd(nc, [{f"in_{name}": a for name, a in arrays.items()}], core_ids=[0])
    return r.results[0]["out"].reshape(1, SEQ, D_MODEL)
```

```python
from contextlib import ExitStack

import concourse.bass as bass
import numpy as np
from concourse import mybir

F32 = mybir.dt.float32
F32R = mybir.dt.float32r
I32 = mybir.dt.int32
U32 = mybir.dt.uint32
ALU = mybir.AluOpType
ACT = mybir.ActivationFunctionType
AX_X = mybir.AxisListType.X
ds = bass.ds

P = 128
SEQ, D_MODEL = 1024, 1024
EPS = 1e-6
NT = SEQ // P
KD = D_MODEL // P
CHUNK = 64
GH, GDK, CONV = 4, 128, 4
GW = GH * GDK
AH, NOPE, ROPE, AV = 8, 64, 32, 64
QK = NOPE + ROPE
HALF = ROPE // 2
Q_LORA, KV_LORA = 384, 256
KQ, KKV = Q_LORA // P, KV_LORA // P
A0 = 4 * GW
CQ0 = A0 + 2 * GH
CKV0 = CQ0 + Q_LORA
KR0 = CKV0 + KV_LORA
D_IN = KR0 + ROPE
NE, TOPK, D_FF = 32, 4, 1024
LIMIT, ALPHA = 7.0, 1.702
ITEM = 256
BLOCKS = ITEM // P
WIDTHS = list(range(P, ITEM + 1, 16))
START = 2
MAX_ITEMS = SEQ * TOPK // ITEM + NE
TABLE = 64
ITEMS_OF_EXPERT = -(-SEQ // ITEM)
PLACES = NE * SEQ
PAD = SEQ
assert MAX_ITEMS + 3 <= TABLE

_COLS = {}


def _constants():
    parts, at = [], 0

    def put(name, a):
        nonlocal at
        a = np.broadcast_to(np.asarray(a, np.float32), (P, np.shape(a)[1]))
        _COLS[name] = (at, at + a.shape[1])
        at += a.shape[1]
        parts.append(a)

    r, c = np.arange(P)[:, None], np.arange(P)[None, :]
    same = r // CHUNK == c // CHUNK
    put("ident", r == c)
    put("ones", np.ones((P, P)))
    put("cum", (r <= c) & same)
    put("same", same)
    put("first", np.broadcast_to(r < CHUNK, (P, P)))
    put("second", np.broadcast_to(r >= CHUNK, (P, P)))
    put("causal", (c >= r) & same)
    put("strict", (c > r) & same)
    put("before", r < c)
    for n in range(6):
        b = 1 << n
        put(f"level{n}", (r // (2 * b) == c // (2 * b)) & (c // b > r // b))
    put("chunk_cols", np.concatenate([r < CHUNK, r >= CHUNK], 1))
    put("freq", np.float32(10000.0) ** (-np.arange(HALF, dtype=np.float32) / np.float32(HALF))[None])
    put("experts", np.arange(NE)[None])
    put("expert_rows", (np.arange(NE) * SEQ)[None])
    put("bounds", (np.arange(ITEMS_OF_EXPERT) * ITEM)[None])
    put("narrower", np.array([[0] + WIDTHS[:-1]]))
    put("row", np.arange(P)[:, None])
    put("seen_off", np.broadcast_to(np.where(np.arange(P) < CHUNK, 1.0, 0.0)[None], (P, P)))
    put("hide", np.full((1, CHUNK), -1e30))
    return np.concatenate(parts, 1)


CONST = _constants()
CONSTS = CONST.shape[1]


class Memory:

    def c(self, name, rows=P):
        return self.const[0:rows, _COLS[name][0]:_COLS[name][1]]


def bc(ap, shape):
    return ap.to_broadcast(list(shape))


def over_heads(ap, n=GH):
    return bc(ap.unsqueeze(1), [ap.shape[0], n, ap.shape[1]])


def over_width(ap, w):
    return bc(ap.unsqueeze(2), [ap.shape[0], ap.shape[1], w])


def starting(eng, *sems):
    for s in sems:
        eng.sem_inc(s, START)


class Chain:

    def __init__(self, eng, sem):
        self.eng, self.sem, self.n = eng, sem, 0

    def link(self, ins):
        self.n += 1
        ins.then_inc(self.sem, 1)
        self.eng.wait_ge(self.sem, self.n)


class Stages:

    def __init__(self, sem, names, lead=1):
        self.sem, self.names, self.per, self.lead, self.made = sem, names, len(names), lead, []

    def start(self, eng):
        eng.sem_inc(self.sem, self.lead * self.per)

    def mark(self, ins, name):
        expected = self.names[len(self.made) % self.per]
        assert expected == name, (name, expected)
        self.made.append(name)
        ins.then_inc(self.sem, 1)

    def mark_now(self, eng, name):
        expected = self.names[len(self.made) % self.per]
        assert expected == name, (name, expected)
        self.made.append(name)
        eng.sem_inc(self.sem, 1)

    def wait(self, eng, name, turn, back=0):
        assert back <= self.lead
        eng.wait_ge(self.sem, turn * self.per + (self.lead - back) * self.per + self.names.index(name) + 1)

    def end(self):
        assert self.made and len(self.made) % self.per == 0, (self.made, self.names)


def project(nc, A, m):
    with ExitStack() as own:
        def sb(name, shape, dt=F32):
            return own.enter_context(nc.sbuf_tensor(name, shape, dt))

        def sem(name):
            return own.enter_context(nc.semaphore(name))

        w_in = sb("w_in_sb", [P, KD, D_IN])
        norm_w = sb("norm_w", [P, KD])
        qn_w = sb("qn_w", [P, KQ])
        kvn_w = sb("kvn_w", [P, KKV])
        conv_w = sb("conv_w_sb", [P, 12, CONV])
        x_in = [sb(f"x_in{u}", [P, D_MODEL]) for u in range(2)]
        h = sb("h", [P, D_MODEL])
        hT = [sb(f"hT{u}", [P, KD, P]) for u in range(2)]
        taps = [sb(f"taps{u}", [P, 12, CONV - 1 + P]) for u in range(2)]
        conv = sb("conv", [P, 12, P])
        gout = sb("gout", [P, 4 * GW])
        cn = sb("cn", [P, Q_LORA + KV_LORA])
        ss = [sb(f"ss{u}", [P, 1]) for u in range(2)]
        rs = [sb(f"rs{u}", [P, 1]) for u in range(2)]
        ss10 = sb("ss10", [P, 10])
        rs10 = sb("rs10", [P, 10])
        power = sb("power", [P, 16])
        squares = sb("squares", [P, 2 * D_MODEL + Q_LORA + KV_LORA], mybir.dt.bfloat16)
        pT = [own.enter_context(nc.psum_tensor(f"pT{n}", [P, 4, P], F32)) for n in range(2)]
        pQKV = [own.enter_context(nc.psum_tensor(f"pQKV{n}", [P, 4, P], F32)) for n in range(3)]
        pZ = own.enter_context(nc.psum_tensor("pZ", [P, 512], F32))
        pC = own.enter_context(nc.psum_tensor("pC", [P, 512], F32))
        pK = own.enter_context(nc.psum_tensor("pK", [P, 512], F32))

        consts_in, small_in = sem("consts_in"), sem("small_in")
        w_columns = ((3 * GW, A0), (0, GW), (GW, 2 * GW), (2 * GW, 3 * GW), (A0, D_IN))
        w_loaded = [sem(f"w_loaded{c}") for c in range(len(w_columns))]
        x_loaded = [sem(f"x_loaded{u}") for u in range(2)]
        ss_ready, ms_ready, rs_ready = sem("ss_ready"), sem("ms_ready"), sem("rs_ready")
        h_ready, hT_psum, hT_ready = sem("h_ready"), sem("hT_psum"), sem("hT_ready")
        qkv_psum, zck_psum, taps_ready = sem("qkv_psum"), sem("zck_psum"), sem("taps_ready")
        head_ready, conv_step, z_ready = sem("head_ready"), sem("conv_step"), sem("z_ready")
        silu_ready, back_psum = sem("silu_ready"), sem("back_psum")
        ss10_ready, ms10_ready, rs10_ready, rsq_ready = (
            sem("ss10_ready"), sem("ms10_ready"), sem("rs10_ready"), sem("rsq_ready"))
        cn_ready, cT_psum, cT_done = sem("cn_ready"), sem("cT_psum"), sem("cT_done")
        gout_dve, gout_act, gout_stored, gout_free = sem("gout_dve"), sem("gout_act"), sem("gout_stored"), sem("gout_free")
        psum_read = sem("psum_read")
        pool_turn, zeroed, act_step = sem("pool_turn"), sem("zeroed"), sem("act_step")
        ident = m.c("ident")

        def tiles(eng, tile):
            tile(0, 0, first=True)
            with eng.Fori(0, (NT - 2) // 2) as it:
                tile(it * 2 + 1, 1)
                tile(it * 2 + 2, 0)
            tile(NT - 1, 1, last=True)

        block = own.enter_context(nc.Block())

        @block.sync
        def _(sp):
            sp.dma_start(x_in[0][:], A["x"][0:P, :]).then_inc(x_loaded[0], 16)
            sp.dma_start(m.const[:], A["const"]).then_inc(consts_in, 16)
            sp.dma_start(norm_w[:], A["norm_mix"]).then_inc(small_in, 16)
            sp.dma_start(qn_w[:], A["q_norm"]).then_inc(small_in, 16)
            sp.dma_start(kvn_w[:], A["kv_norm"]).then_inc(small_in, 16)
            sp.dma_start(conv_w[:], A["conv_w"]).then_inc(small_in, 16)
            sp.dma_start(x_in[1][:], A["x"][P:2 * P, :]).then_inc(x_loaded[1], 16)
            with sp.Fori(1, NT // 2) as it:
                for u in range(2):
                    i = it * 2 + u
                    sp.wait_ge(h_ready, START + i - 1)
                    sp.dma_start(x_in[u][:], A["x"][ds(i * P, P), :]).then_inc(x_loaded[u], 16)

        @block.gpsimd
        def _(pool):
            starting(pool, rs_ready, rs10_ready, gout_free)
            pool.memset(power[:], -0.5).then_inc(zeroed, 1)
            pool.memset(taps[0][:, :, 0:CONV - 1], 0.0).then_inc(zeroed, 1)
            pool.wait_ge(zeroed, 2)

            def root(i, u):
                pool.wait_ge(ms_ready, START + i + 1)
                pool.sem_inc(pool_turn, 1)
                pool.tensor_tensor(rs[u][:], ss[u][:], power[:, 0:1], ALU.pow).then_inc(rs_ready, 1)

            def tile(i, u, first=False, last=False):
                if not last:
                    root(i + 1, 1 - u)
                pool.wait_ge(ms10_ready, START + i + 1)
                pool.sem_inc(pool_turn, 1)
                pool.tensor_tensor(rs10[:], ss10[:], power[:, 0:10], ALU.pow).then_inc(rs10_ready, 1)
                pool.wait_ge(gout_dve, START + i + 1)
                pool.wait_ge(gout_act, START + i + 1)
                pool.sem_inc(pool_turn, 1)
                pool.dma_start(m.gdn_in[ds(i * P, P), :], gout[:]).then_inc(gout_stored, 16)
                pool.wait_ge(gout_stored, 16 * i + 16)
                pool.sem_inc(gout_free, 1)

            root(0, 0)
            tiles(pool, tile)

        @block.scalar
        def _(act):
            starting(act, ss_ready, taps_ready, head_ready, silu_ready, act_step, ss10_ready, gout_act, z_ready)
            act.wait_ge(x_loaded[0], 16)
            act.wait_ge(consts_in, 16)
            act.wait_ge(small_in, 64)
            for c, (at, end) in enumerate(w_columns):
                act.dma_start(w_in[:, :, at:end], A["w_in"].rearrange("(k p) f -> p k f", p=P)[:, :, at:end]).then_inc(w_loaded[c], 16)

            def square(i, u, loads):
                act.wait_ge(ss_ready, START + i)
                act.wait_ge(x_loaded[u], 16 * loads)
                act.activation(squares[:, 0:D_MODEL], x_in[u][:], ACT.Square, accum_out=ss[u][:]).then_inc(ss_ready, 1)

            def tile(i, u, loads=None):
                if loads is not None:
                    square(i + 1, 1 - u, loads)
                for g in range(3):
                    act.wait_ge(qkv_psum, START + 3 * i + g + 1)
                    act.copy(taps[u][:, 4 * g:4 * g + 4, CONV - 1:], pQKV[g][:]).then_inc(taps_ready, 1)
                act.wait_ge(taps_ready, START + 3 * i + 3)
                act.wait_ge(conv_step, START + 3 * CONV * i)
                act.copy(taps[1 - u][:, :, 0:CONV - 1], taps[u][:, :, P:]).then_inc(head_ready, 1)
                for g in range(3):
                    act.wait_ge(conv_step, START + 3 * CONV * i + CONV * (g + 1))
                    act.activation(conv[:, 4 * g:4 * g + 4, :], conv[:, 4 * g:4 * g + 4, :],
                                   ACT.Silu).then_inc(silu_ready, 1)
                act.wait_ge(gout_free, START + i)
                act.wait_ge(zck_psum, START + 3 * i + 1)
                act.activation(gout[:, 3 * GW:4 * GW], pZ[:], ACT.Silu).then_inc(z_ready, 1)
                act.wait_ge(zck_psum, START + 3 * i + 3)
                act.activation(squares[:, 2 * D_MODEL:2 * D_MODEL + Q_LORA], pC[:, CQ0 - A0:CKV0 - A0], ACT.Square,
                               accum_out=ss10[:, 8:9]).then_inc(act_step, 1)
                act.activation(squares[:, 2 * D_MODEL + Q_LORA:], pK[:, 0:KV_LORA], ACT.Square,
                               accum_out=ss10[:, 9:10]).then_inc(act_step, 1)
                act.wait_ge(back_psum, START + 3 * i + 3)
                act.copy(gout[:, 2 * GW:3 * GW].rearrange("p (h w) -> p h w", h=GH), pQKV[2][:]).then_inc(gout_act, 1)
                for g in range(2):
                    for a in range(GH):
                        done = act.activation(squares[:, D_MODEL + P * (4 * g + a):D_MODEL + P * (4 * g + a + 1)], pQKV[g][:, a, :], ACT.Square,
                                              accum_out=ss10[:, 4 * g + a:4 * g + a + 1])
                        if g == 0 or a < GH - 1:
                            done.then_inc(act_step, 1)
                done.then_inc(ss10_ready, 1)

            square(0, 0, 1)
            tile(0, 0, loads=1)
            with act.Fori(0, (NT - 2) // 2) as it:
                tile(it * 2 + 1, 1, loads=it + 2)
                tile(it * 2 + 2, 0, loads=it + 2)
            tile(NT - 1, 1)

        @block.vector
        def _(dve):
            starting(dve, ms_ready, h_ready, hT_ready, conv_step, ms10_ready, rsq_ready, cn_ready, gout_dve, psum_read, cT_done)
            dve.wait_ge(small_in, 64)
            dve.wait_ge(consts_in, 16)
            dve.wait_ge(zeroed, 2)

            def normalise(i, u):
                dve.wait_ge(ss_ready, START + i + 1)
                dve.tensor_scalar(ss[u][:], ss[u][:], 1.0 / D_MODEL, EPS, ALU.mult, ALU.add).then_inc(ms_ready, 1)
                dve.wait_ge(rs_ready, START + i + 1)
                dve.tensor_scalar(h[:], x_in[u][:], rs[u][:], None, ALU.mult).then_inc(h_ready, 1)

            def take_hT(i, u):
                for half in range(2):
                    at = 4 * half
                    dve.wait_ge(hT_psum, START + 2 * i + half + 1)
                    dve.tensor_tensor(hT[u][:, at:at + 4, :], pT[half][:], over_width(norm_w[:, at:at + 4], P), ALU.mult).then_inc(hT_ready, 1)

            def take_cT(i):
                dve.wait_ge(cT_psum, START + i + 1)
                dve.tensor_tensor(m.cqT[:, :, ds(i * P, P)], pT[0][:, 0:KQ, :], over_width(qn_w[:], P), ALU.mult)
                dve.tensor_tensor(m.ckvT[:, :, ds(i * P, P)], pT[1][:, 0:KKV, :], over_width(kvn_w[:], P), ALU.mult)\
                    .then_inc(cT_done, 1)

            def tile(i, u, first=False, last=False):
                if not last:
                    normalise(i + 1, 1 - u)
                if not first:
                    take_cT(i - 1)
                if not last:
                    take_hT(i + 1, 1 - u)
                dve.wait_ge(head_ready, START + i)
                for g in range(3):
                    dve.wait_ge(taps_ready, START + 3 * i + g + 1)
                    for tap in range(CONV - 1, -1, -1):
                        for ch in range(4 * g, 4 * g + 4):
                            src = taps[u][:, ch, tap:tap + P]
                            if tap == CONV - 1:
                                done = dve.tensor_scalar(conv[:, ch, :], src, conv_w[:, ch, tap:tap + 1], None, ALU.mult)
                            else:
                                done = dve.scalar_tensor_tensor(out=conv[:, ch, :], in0=src, scalar=conv_w[:, ch, tap:tap + 1],
                                                                in1=conv[:, ch, :], op0=ALU.mult, op1=ALU.add)
                        done.then_inc(conv_step, 1)
                        dve.wait_ge(conv_step, START + 3 * CONV * i + CONV * g + CONV - tap)
                dve.wait_ge(ss10_ready, START + i + 1)
                dve.tensor_scalar(ss10[:, 0:8], ss10[:, 0:8], EPS, None, ALU.add)
                dve.tensor_scalar(ss10[:, 8:9], ss10[:, 8:9], 1.0 / Q_LORA, EPS, ALU.mult, ALU.add)
                dve.tensor_scalar(ss10[:, 9:10], ss10[:, 9:10], 1.0 / KV_LORA, EPS, ALU.mult, ALU.add).then_inc(ms10_ready, 1)
                dve.wait_ge(rs10_ready, START + i + 1)
                dve.tensor_scalar(rs10[:, 0:GH], rs10[:, 0:GH], GDK ** -0.5, None, ALU.mult).then_inc(rsq_ready, 1)
                dve.tensor_scalar(cn[:, 0:Q_LORA], pC[:, CQ0 - A0:CKV0 - A0], rs10[:, 8:9], None, ALU.mult)
                dve.tensor_scalar(cn[:, Q_LORA:], pK[:, 0:KV_LORA], rs10[:, 9:10], None, ALU.mult).then_inc(cn_ready, 1)
                dve.wait_ge(rsq_ready, START + i + 1)
                dve.wait_ge(gout_free, START + i)
                for g in range(2):
                    done = dve.tensor_tensor(gout[:, g * GW:(g + 1) * GW].rearrange("p (h w) -> p h w", h=GH), pQKV[g][:],
                                             over_width(rs10[:, 4 * g:4 * g + 4], P), ALU.mult)
                done.then_inc(gout_dve, 1)
                dve.tensor_copy(m.ab[:, ds(i, 1), :], pC[:, 0:2 * GH].unsqueeze(1))
                dve.tensor_copy(m.k_rope[:, ds(i, 1), :], pK[:, KV_LORA:KV_LORA + ROPE].unsqueeze(1)).then_inc(psum_read, 1)

            normalise(0, 0)
            take_hT(0, 0)
            tiles(dve, tile)
            take_cT(NT - 1)

        @block.tensor
        def _(pe):
            starting(pe, hT_psum, qkv_psum, zck_psum, back_psum, cT_psum)
            pe.wait_ge(consts_in, 16)

            def turn_h(i):
                pe.wait_ge(h_ready, START + i + 1)
                for k in range(KD):
                    done = pe.transpose(pT[k // 4][:, k % 4, :], h[:, k * P:(k + 1) * P], ident)
                    if k % 4 == 3:
                        done.then_inc(hT_psum, 1)

            def turn_c(i):
                pe.wait_ge(cn_ready, START + i + 1)
                for k in range(KQ + KKV):
                    bank, at = (pT[0], k) if k < KQ else (pT[1], k - KQ)
                    done = pe.transpose(bank[:, at, :], cn[:, k * P:(k + 1) * P], ident)
                done.then_inc(cT_psum, 1)

            def rows_of(bank, u, at, end):
                for k in range(KD):
                    done = pe.matmul(bank[:, 0:end - at], hT[u][:, k, :], w_in[:, k, at:end], start=k == 0, stop=k == KD - 1)
                done.then_inc(zck_psum, 1)

            def tile(i, u, first=False, last=False):
                pe.wait_ge(hT_ready, START + 2 * i + 2)
                pe.wait_ge(z_ready, START + i)
                pe.wait_ge(w_loaded[0], 16)
                rows_of(pZ, u, 3 * GW, A0)
                if not first:
                    turn_c(i - 1)
                pe.wait_ge(ss10_ready, START + i)
                pe.wait_ge(gout_dve, START + i)
                pe.wait_ge(gout_act, START + i)
                for g in range(3):
                    pe.wait_ge(w_loaded[1 + g], 16)
                    for c in range(4):
                        for k in range(KD):
                            at = (4 * g + c) * P
                            done = pe.matmul(pQKV[g][:, c, :], w_in[:, k, at:at + P], hT[u][:, k, :],
                                             start=k == 0, stop=k == KD - 1)
                    done.then_inc(qkv_psum, 1)
                    if g == 0 and not last:
                        pe.wait_ge(cT_done, START + i)
                        turn_h(i + 1)
                pe.wait_ge(psum_read, START + i)
                pe.wait_ge(w_loaded[4], 16)
                rows_of(pC, u, A0, CKV0)
                rows_of(pK, u, CKV0, D_IN)
                for g in range(3):
                    pe.wait_ge(silu_ready, START + 3 * i + g + 1)
                    for c in range(4):
                        done = pe.transpose(pQKV[g][:, c, :], conv[:, 4 * g + c, :], ident)
                    done.then_inc(back_psum, 1)

            turn_h(0)
            tiles(pe, tile)
            pe.wait_ge(hT_ready, START + 2 * NT)
            turn_c(NT - 1)


def _parts_of_two_pi(n):
    rest, parts = 2 * np.pi, []
    for _ in range(n):
        step = 2.0 ** (np.floor(np.log2(rest)) - 7)
        parts.append(float(np.floor(rest / step) * step))
        rest -= parts[-1]
    return parts


ROUND = 1.5 * 2.0 ** 23
BELOW_PI = 3.1415925


def prepare(A, m, sb, sem):
    pos_i = sb("pos_i", [P, NT], I32)
    pos = sb("pos", [P, NT])
    angle, turns, high, low, wrap = (sb(n, [P, NT, HALF]) for n in ("angle", "turns", "high", "low", "wrap"))
    prod = [sb(f"kprod{n}", [P, NT, HALF]) for n in range(4)]
    a_log, dt_bias = sb("a_log_sb", [P, GH]), sb("dt_bias_sb", [P, GH])
    x, ax, y, s, s2, p = (sb(n, [P, NT, GH]) for n in ("sp_x", "sp_ax", "sp_y", "sp_s", "sp_s2", "sp_p"))
    eb = sb("eb", [P, NT, GH])
    ea = sb("ea", [P, GH])
    loaded, dve_chain = sem("prep_loaded"), sem("prep_dve")
    ax_ready, exp_ready = sem("ax_ready"), sem("exp_ready")
    angles_ready, sin_ready = sem("angles_ready"), sem("sin_ready")
    shape = [P, NT, HALF]

    def load(sp):
        sp.dma_start(pos_i[:], A["positions"]).then_inc(loaded, 16)
        sp.dma_start(a_log[:], bc(A["a_log"], [P, GH])).then_inc(loaded, 16)
        sp.dma_start(dt_bias[:], bc(A["dt_bias"], [P, GH])).then_inc(loaded, 16)

    def work_out(dve):
        link = Chain(dve, dve_chain).link
        dve.wait_ge(loaded, 48)
        link(dve.tensor_tensor(x[:], m.ab[:, :, 0:GH], bc(dt_bias[:].unsqueeze(1), [P, NT, GH]), ALU.add))
        dve.scalar_tensor_tensor(out=ax[:], in0=x[:], scalar=-1.0, in1=x[:], op0=ALU.mult, op1=ALU.max).then_inc(ax_ready, 1)
        link(dve.tensor_copy(pos[:], pos_i[:]))
        link(dve.tensor_tensor(angle[:], over_width(pos[:], HALF), over_heads(m.c("freq"), NT), ALU.mult))
        link(dve.tensor_scalar(turns[:], angle[:], float(1 / (2 * np.pi)), ROUND, ALU.mult, ALU.add))
        link(dve.tensor_scalar(turns[:], turns[:], ROUND, None, ALU.subtract))
        link(dve.tensor_scalar(high[:], turns[:], 1.0 / 256, ROUND, ALU.mult, ALU.add))
        link(dve.tensor_scalar(high[:], high[:], ROUND, 256.0, ALU.subtract, ALU.mult))
        link(dve.tensor_tensor(low[:], turns[:], high[:], ALU.subtract))
        for part in _parts_of_two_pi(5):
            for whole in (high, low):
                link(dve.scalar_tensor_tensor(out=angle[:], in0=whole[:], scalar=-part, in1=angle[:],
                                              op0=ALU.mult, op1=ALU.add))
        link(dve.tensor_scalar(m.cos[:], angle[:], float(np.pi / 2), None, ALU.add))
        link(dve.tensor_scalar(wrap[:], m.cos[:], float(np.pi), -float(2 * np.pi), ALU.is_gt, ALU.mult))
        link(dve.tensor_tensor(m.cos[:], m.cos[:], wrap[:], ALU.add))
        link(dve.tensor_scalar(m.cos[:], m.cos[:], BELOW_PI, -BELOW_PI, ALU.min, ALU.max))
        dve.tensor_scalar(m.sin[:], angle[:], BELOW_PI, -BELOW_PI, ALU.min, ALU.max).then_inc(angles_ready, 1)
        dve.wait_ge(exp_ready, 3)
        link(dve.tensor_scalar(s[:], y[:], 2.0, None, ALU.add))
        link(dve.reciprocal(s[:], s[:]))
        link(dve.tensor_tensor(s[:], s[:], y[:], ALU.mult))
        link(dve.tensor_tensor(s2[:], s[:], s[:], ALU.mult))
        link(dve.tensor_scalar(p[:], s2[:], 1.0 / 17, None, ALU.mult))
        for n in (15, 13, 11, 9, 7, 5, 3):
            link(dve.scalar_tensor_tensor(out=p[:], in0=p[:], scalar=1.0 / n, in1=s2[:], op0=ALU.add, op1=ALU.mult))
        link(dve.scalar_tensor_tensor(out=p[:], in0=p[:], scalar=1.0, in1=s[:], op0=ALU.add, op1=ALU.mult))
        link(dve.tensor_scalar(x[:], x[:], 0.0, None, ALU.max))
        link(dve.scalar_tensor_tensor(out=x[:], in0=p[:], scalar=2.0, in1=x[:], op0=ALU.mult, op1=ALU.add))
        link(dve.scalar_tensor_tensor(out=m.g[:], in0=x[:], scalar=-1.0, in1=bc(ea[:].unsqueeze(1), [P, NT, GH]),
                                      op0=ALU.mult, op1=ALU.mult))
        link(dve.tensor_scalar(eb[:], eb[:], 1.0, None, ALU.add))
        link(dve.reciprocal(m.beta[:], eb[:]))
        dve.wait_ge(sin_ready, 1)
        k1, k2 = m.k_rope[:, :, 0:HALF], m.k_rope[:, :, HALF:ROPE]
        dve.tensor_tensor(prod[0][:], k1, m.cos[:], ALU.mult)
        dve.tensor_tensor(prod[1][:], k2, m.sin[:], ALU.mult)
        dve.tensor_tensor(prod[2][:], k2, m.cos[:], ALU.mult)
        link(dve.tensor_tensor(prod[3][:], k1, m.sin[:], ALU.mult))
        dve.tensor_tensor(m.kh[:, :, NOPE:NOPE + HALF], prod[0][:], prod[1][:], ALU.subtract)
        link(dve.tensor_tensor(m.kh[:, :, NOPE + HALF:], prod[2][:], prod[3][:], ALU.add))

    def look_up(act):
        act.wait_ge(loaded, 48)
        act.activation(ea[:], a_log[:], ACT.Exp).then_inc(exp_ready, 1)
        act.activation(eb[:], m.ab[:, :, GH:], ACT.Exp, scale=-1.0).then_inc(exp_ready, 1)
        act.wait_ge(ax_ready, 1)
        act.activation(y[:], ax[:], ACT.Exp, scale=-1.0).then_inc(exp_ready, 1)
        act.wait_ge(angles_ready, 1)
        act.activation(m.cos[:], m.cos[:], ACT.Sin)
        act.activation(m.sin[:], m.sin[:], ACT.Sin).then_inc(sin_ready, 1)

    return load, work_out, look_up


LEVELS = range(1, 6)
_DELTA = (["rates", "scaled", "turn_k", "turn_q", "overlap", "x0"]
          + [f"{s}{n}" for n in LEVELS for s in ("y", "z")]
          + ["uw", "read0", "write0", "read1", "write1", "within", "gate"])
_ATTEND = ["up", "turn", "score0"]
for _j in range(1, NT + 1):
    if _j < NT:
        _ATTEND.append(f"score{_j}")
    _ATTEND += [f"spread{_j - 1}_{_g}" for _g in range((_j + 3) // 4)] + [f"value{_j - 1}"]
_ATTEND.append("heads_out")


_AHEAD = [1, 2, 3, 5, 7, 9, 11, 12, 12, 13, 14, 15, 17, 17, 19, 20, 22, 24, 25, 29, 31, 31, 31]


def _merge(chain, others, ahead):
    order = []
    for n, step in enumerate(chain):
        order += others[ahead[n - 1] if n else 0:ahead[n]] + [step]
    return order + others[ahead[-1]:]


ORDER = _merge(_DELTA, _ATTEND, _AHEAD)


def mix(nc, A, m):
    with ExitStack() as own:
        def sb(name, shape, dt=F32):
            return own.enter_context(nc.sbuf_tensor(name, shape, dt))

        def sem(name):
            return own.enter_context(nc.semaphore(name))

        def heads(name):
            return sb(name, [P, GH, P])

        q_in, k_in, v_in, z_in = (heads(n) for n in ("q_in", "k_in", "v_in", "z_in"))
        g_cum, diff, decay = heads("g_cum"), heads("diff"), heads("decay")
        rate = sb("rate", [P, 4 * GH])
        rate_exp = sb("rate_exp", [P, 4 * GH])
        k_rate = sb("k_rate", [P, 2, GH])
        kb, kbe, qd, vb = (heads(n) for n in ("kb", "kbe", "qd", "vb"))
        kd = [heads(f"kd{j}") for j in range(2)]
        kT, kbT, qT, qdT = (heads(n) for n in ("kT", "kbT", "qT", "qdT"))
        AT, QKT, X, XT, Y = (heads(n) for n in ("AT", "QKT", "X", "XT", "Y"))
        LT = {n: heads(f"LT{n}") for n in LEVELS}
        first = heads("first_level")
        u, wT, v_new, S, S_decayed, o = (heads(n) for n in ("u", "wT", "v_new", "S", "S_decayed", "o"))
        o_norm, o_sq = heads("o_norm"), heads("o_sq")
        o_ms, o_rs, power = sb("o_ms", [P, GH]), sb("o_rs", [P, GH]), sb("o_power", [P, GH])
        w_uq = sb("w_uq_sb", [P, KQ, AH * QK])
        w_ukv = sb("w_ukv_sb", [P, KKV, AH * (NOPE + AV)])
        qh, kh, vh = sb("qh", [P, NT, QK]), m.kh, sb("vh", [P, NT, AV])
        prod = [sb(f"qprod{n}", [P, NT, HALF]) for n in range(4)]
        qhT, khT = sb("qhT", [QK, SEQ]), sb("khT", [QK, SEQ])
        probs = [sb(f"probs{b}", [P, SEQ]) for b in range(2)]
        probsT = [sb(f"probsT{b}", [P, NT, P]) for b in range(2)]
        neg_max, row_sum, row_inv = sb("neg_max", [P, NT]), sb("row_sum", [P, NT]), sb("row_inv", [P, NT])

        pS = own.enter_context(nc.psum_tensor("pS", [P, SEQ], F32))
        pT = [own.enter_context(nc.psum_tensor(f"bankT{b}", [P, 4, P], F32)) for b in range(2)]
        pO = own.enter_context(nc.psum_tensor("pO", [P, NT, AV], F32))
        gA, gB, gC = (own.enter_context(nc.psum_tensor(n, [P, GH, P], F32)) for n in ("gA", "gB", "gC"))
        pS4 = [pS[:, 512 * b:512 * b + 512].rearrange("p (t w) -> p t w", t=4) for b in range(2)]

        levels = [n for n in LEVELS]
        g_pe = Stages(sem("g_pe"), ["rates", "decay", "kT", "kbT", "qT", "qdT", "AT", "QKT", "X"]
                      + [f"{s}{n}" for n in levels[:-1] for s in ("Y", "Z", "ZT")] + ["Y5", "ZT5", "u", "wT"]
                      + [f"{s}{j}" for j in range(2) for s in ("wS", "qS", "dS")] + ["within"])
        g_dve = Stages(sem("g_dve"), ["g_cum", "rate_copy", "rate", "diff", "diff_masked", "decay", "kb", "k_rate",
                                      "kbe", "qd", "kbT", "qdT", "AT", "QKT", "first", "XT"]
                       + [f"{s}{n}" for n in levels[:-1] for s in ("X", "XT")] + ["XT5", "wT"]
                       + [f"{s}{j}" for j in range(2) for s in ("v_new", "S_decayed", "S")]
                       + ["o", "o_ms", "o_norm", "o_out"])
        g_act = Stages(sem("g_act"), ["rate_exp", "diff_exp", "kT", "qT", "X"] + [f"Y{n}" for n in levels]
                       + ["u", "o0", "o1", "o_sq"])
        g_pool = Stages(sem("g_pool"), ["vb", "kd0", "kd1"] + [f"LT{n}" for n in levels] + ["o_rs"])
        groups = {j: range((j + 4) // 4) for j in range(NT)}
        a_pe = Stages(sem("a_pe"), ["q0", "q1", "kv0", "kv1", "qT0", "qT1", "kT0", "kT1", "score0"]
                      + [x for j in range(NT) for x in
                         ([f"score{j + 1}"] if j + 1 < NT else []) + [f"spread{j}_{g}" for g in groups[j]] + [f"value{j}"]])
        on_dve = lambda j, g: (j + g) % 2 == 0
        a_dve = Stages(sem("a_dve"), ["k0", "v0", "products", "rope", "qT0", "qT1", "max0"]
                       + [x for j in range(NT) for x in
                          ([f"max{j + 1}"] if j + 1 < NT else []) + [f"spread{j}_{g}" for g in groups[j] if on_dve(j, g)]]
                       + ["row_inv", "out"])
        a_act = Stages(sem("a_act"), ["q0", "q1", "k1", "v1", "kT0", "kT1", "exp0"]
                       + [x for j in range(NT) for x in
                          ([f"exp{j + 1}"] if j + 1 < NT else []) + [f"spread{j}_{g}" for g in groups[j] if not on_dve(j, g)]])
        in_loaded = {n: sem(f"{n}_loaded") for n in ("q", "k", "v", "z")}
        weights_in, zeroed, pool_turn, gate = sem("weights_in"), sem("mix_zeroed"), sem("mix_pool_turn"), sem("gate")
        ident = m.c("ident")

        def width_of(j):
            return (j + 1) * P

        load_small, work_out_rates, look_up = prepare(A, m, sb, sem)
        prepared = sem("prepared")
        block = own.enter_context(nc.Block())

        @block.sync
        def _(sp):
            load_small(sp)
            for k in range(KQ):
                sp.dma_start(w_uq[:, k, :], A["w_uq"][k * P:(k + 1) * P, :]).then_inc(weights_in, 16)
            for k in range(KKV):
                sp.dma_start(w_ukv[:, k, :], A["w_ukv"][k * P:(k + 1) * P, :]).then_inc(weights_in, 16)
            with sp.Fori(0, NT) as t:
                rows = m.gdn_in[ds(t * P, P), :]
                g_pe.wait(sp, "qdT", t, back=1)
                g_dve.wait(sp, "qd", t, back=1)
                g_pool.wait(sp, "kd1", t, back=1)
                sp.dma_start(k_in[:].rearrange("p h w -> p (h w)"), rows[:, GW:2 * GW]).then_inc(in_loaded["k"], 16)
                sp.dma_start(q_in[:].rearrange("p h w -> p (h w)"), rows[:, 0:GW]).then_inc(in_loaded["q"], 16)
                sp.dma_start(v_in[:].rearrange("p h w -> p (h w)"), rows[:, 2 * GW:3 * GW]).then_inc(in_loaded["v"], 16)
                g_dve.wait(sp, "o_out", t, back=1)
                sp.dma_start(z_in[:].rearrange("p h w -> p (h w)"), rows[:, 3 * GW:4 * GW]).then_inc(in_loaded["z"], 16)

        @block.gpsimd
        def _(pool):
            g_pool.start(pool)
            pool.memset(power[:], -0.5).then_inc(zeroed, 1)
            pool.memset(v_new[:], 0.0).then_inc(zeroed, 1)
            pool.memset(S[:], 0.0).then_inc(zeroed, 1)
            pool.wait_ge(zeroed, 3)
            pool.wait_ge(prepared, 1)
            with pool.Fori(0, NT) as t:
                pool.wait_ge(in_loaded["v"], 16 * t + 16)
                pool.wait_ge(in_loaded["k"], 16 * t + 16)
                g_pe.wait(pool, "u", t, back=1)
                pool.sem_inc(pool_turn, 1)
                g_pool.mark(pool.tensor_tensor(vb[:], v_in[:], over_width(m.beta[:, ds(t, 1), :].rearrange("p a h -> p (a h)"), P),
                                               ALU.mult), "vb")
                g_dve.wait(pool, "k_rate", t)
                g_pe.wait(pool, "dS1", t, back=1)
                pool.sem_inc(pool_turn, 1)
                for j in range(2):
                    g_pool.mark(pool.tensor_tensor(kd[j][:], k_in[:], over_width(k_rate[:, j, :], P), ALU.mult), f"kd{j}")
                g_dve.wait(pool, "AT", t)
                g_pe.wait(pool, "Y5", t, back=1)
                pool.sem_inc(pool_turn, 1)
                for n in LEVELS:
                    g_pool.mark(pool.tensor_tensor(LT[n][:], AT[:], over_heads(m.c(f"level{n}")), ALU.mult), f"LT{n}")
                g_dve.wait(pool, "o_ms", t)
                pool.sem_inc(pool_turn, 1)
                g_pool.mark(pool.tensor_tensor(o_rs[:], o_ms[:], power[:], ALU.pow), "o_rs")
            g_pool.end()

        @block.tensor
        def _(pe):
            g_pe.start(pe)
            a_pe.start(pe)
            pe.wait_ge(zeroed, 3)
            pe.wait_ge(weights_in, 16 * (KQ + KKV))

            def per_head(bank, lhsT, rhs, name):
                for h in range(GH):
                    last = pe.matmul(bank[:, h, :], lhsT[:, h, :], rhs[:, h, :], start=True, stop=True)
                g_pe.mark(last, name)

            def turn_heads(bank, src, name):
                for h in range(GH):
                    last = pe.transpose(bank[:, h, :], src[:, h, :], ident)
                g_pe.mark(last, name)

            def delta(step, t):
                if step == "rates":
                    g = m.g[:, ds(t, 1), :].rearrange("p a h -> p (a h)")
                    g_dve.wait(pe, "o", t, back=1)
                    g_act.wait(pe, "o1", t, back=1)
                    pe.wait_ge(prepared, 1)
                    g_dve.wait(pe, "S1", t, back=1)
                    for n, which in enumerate(("cum", "same", "first", "second")):
                        last = pe.matmul(gA[:, 0, GH * n:GH * n + GH], m.c(which), g, start=True, stop=True)
                    g_pe.mark(last, "rates")
                    g_dve.wait(pe, "g_cum", t)
                    g_pe.mark(pe.matmul(gB[:], m.c("ones"), g_cum[:], start=True, stop=True), "decay")
                if step == "turn_k":
                    pe.wait_ge(in_loaded["k"], 16 * t + 16)
                    turn_heads(gC, k_in, "kT")
                    g_dve.wait(pe, "kb", t)
                    turn_heads(gA, kb, "kbT")
                if step == "turn_q":
                    pe.wait_ge(in_loaded["q"], 16 * t + 16)
                    g_dve.wait(pe, "qd", t)
                    turn_heads(gB, q_in, "qT")
                    g_act.wait(pe, "kT", t)
                    turn_heads(gC, qd, "qdT")
                if step == "overlap":
                    g_dve.wait(pe, "kbT", t)
                    per_head(gA, kT, kbT, "AT")
                    g_act.wait(pe, "qT", t)
                    per_head(gB, kT, qT, "QKT")
                if step == "x0":
                    g_dve.wait(pe, "XT", t)
                    turn_heads(gC, XT, "X")
                if step[0] == "y" and step[1:].isdigit():
                    n = int(step[1:])
                    g_pool.wait(pe, f"LT{n}", t)
                    g_act.wait(pe, "X", t) if n == 1 else g_dve.wait(pe, f"XT{n - 1}", t)
                    per_head(gA, LT[n], X, f"Y{n}")
                if step[0] == "z" and step[1:].isdigit():
                    n = int(step[1:])
                    g_act.wait(pe, f"Y{n}", t)
                    if n < 5:
                        per_head(gB, XT, Y, f"Z{n}")
                    per_head(gC, Y, XT, f"ZT{n}")
                if step == "uw":
                    g_dve.wait(pe, "XT5", t)
                    g_pool.wait(pe, "vb", t)
                    per_head(gA, XT, vb, "u")
                    per_head(gB, kbe, XT, "wT")
                if step[:-1] == "read":
                    j = int(step[-1])
                    if j == 0:
                        g_dve.wait(pe, "wT", t)
                        g_act.wait(pe, "u", t)
                    else:
                        g_dve.wait(pe, "S0", t)
                        g_act.wait(pe, "o0", t)
                    per_head(gC, wT, S, f"wS{j}")
                    per_head(gA, qdT, S, f"qS{j}")
                if step[:-1] == "write":
                    j = int(step[-1])
                    g_pool.wait(pe, f"kd{j}", t)
                    g_dve.wait(pe, f"v_new{j}", t)
                    per_head(gB, kd[j], v_new, f"dS{j}")
                if step == "within":
                    per_head(gC, QKT, v_new, "within")

            def attend(step, t):
                if step == "up":
                    a_act.wait(pe, "exp7", t, back=1)
                    for b in range(2):
                        for c in range(4):
                            for k in range(KQ):
                                last = pe.matmul(pS4[b][:, c, 0:QK], m.cqT[:, k, (4 * b + c) * P:(4 * b + c + 1) * P],
                                                 w_uq[:, k, ds(t * QK, QK)], start=k == 0, stop=k == KQ - 1)
                        a_pe.mark(last, f"q{b}")
                    a_dve.wait(pe, "out", t, back=1)
                    a_act.wait(pe, "spread7_0" if not on_dve(7, 0) else "spread7_1", t, back=1)
                    for b in range(2):
                        for c in range(4):
                            for k in range(KKV):
                                last = pe.matmul(pT[b][:, c, :], m.ckvT[:, k, (4 * b + c) * P:(4 * b + c + 1) * P],
                                                 w_ukv[:, k, ds(t * (NOPE + AV), NOPE + AV)], start=k == 0, stop=k == KKV - 1)
                        a_pe.mark(last, f"kv{b}")
                if step == "turn":
                    a_dve.wait(pe, "rope", t)
                    a_act.wait(pe, "v1", t)
                    for b in range(2):
                        for c in range(4):
                            last = pe.transpose(pS4[b][0:QK, c, :], qh[:, 4 * b + c, :], ident)
                        a_pe.mark(last, f"qT{b}")
                    for b in range(2):
                        for c in range(4):
                            last = pe.transpose(pT[b][0:QK, c, :], kh[:, 4 * b + c, :], ident)
                        a_pe.mark(last, f"kT{b}")
                if step[:5] == "score":
                    j = int(step[5:])
                    if j == 0:
                        a_dve.wait(pe, "qT1", t)
                        a_act.wait(pe, "kT1", t)
                    elif j < 4:
                        if j >= 2:
                            a_act.wait(pe, f"exp{j - 2}", t)
                    else:
                        a_act.wait(pe, f"exp{j - 1}", t)
                    base = 512 * (j % 2) if j < 4 else 0
                    for at in range(0, width_of(j), 512):
                        end = min(at + 512, width_of(j))
                        last_bank = end == width_of(j)
                        pe.matmul(pS[:, base + at:base + end], qhT[:, j * P:(j + 1) * P], khT[:, at:end],
                                  start=True, stop=not last_bank)
                    end = base + width_of(j)
                    a_pe.mark(pe.matmul(pS[:, end - CHUNK:end], m.c("seen_off", 1), m.c("hide", 1),
                                        start=False, stop=True), f"score{j}")
                if step[:6] == "spread":
                    j, g = int(step[6]), int(step[8])
                    a_act.wait(pe, f"exp{j}", t)
                    if (j, g) in last_use:
                        jj, gg = last_use[(j, g)]
                        (a_dve if on_dve(jj, gg) else a_act).wait(pe, f"spread{jj}_{gg}", t)
                    for c in range(4 * g, min(4 * g + 4, j + 1)):
                        last = pe.transpose(pT[bank_of[(j, g)]][:, c % 4, :], probs[j % 2][:, c * P:(c + 1) * P], ident)
                    a_pe.mark(last, step)
                if step[:5] == "value":
                    j = int(step[5:])
                    for g in groups[j]:
                        (a_dve if on_dve(j, g) else a_act).wait(pe, f"spread{j}_{g}", t)
                    for c in range(j + 1):
                        last = pe.matmul(pO[:, j, :], probsT[j % 2][:, c, :], vh[:, c, :], start=c == 0, stop=c == j)
                    a_pe.mark(last, step)

            order = [(j, g) for j in range(NT) for g in groups[j]]
            bank_of = {x: n % 2 for n, x in enumerate(order)}
            last_use = {order[n]: order[n - 2] for n in range(2, len(order))}
            with pe.Fori(0, NT) as t:
                for step in ORDER:
                    delta(step, t) if step in _DELTA else attend(step, t)
            g_pe.end()
            a_pe.end()

        @block.vector
        def _(dve):
            g_dve.start(dve)
            a_dve.start(dve)
            work_out_rates(dve)
            dve.sem_inc(prepared, 1)
            dve.wait_ge(zeroed, 3)

            def delta(step, t):
                if step == "rates":
                    g_pe.wait(dve, "decay", t, back=1)
                    g = m.g[:, ds(t, 1), :].rearrange("p a h -> p (a h)")
                    g_dve.mark(dve.tensor_tensor(g_cum[:], over_heads(m.c("cum")), over_width(g, P), ALU.mult), "g_cum")
                    g_pe.wait(dve, "rates", t)
                    g_pool.wait(dve, "kd1", t, back=1)
                    g_dve.mark(dve.tensor_copy(rate[:], gA[:, 0, 0:4 * GH]), "rate_copy")
                    g_dve.wait(dve, "rate_copy", t)
                    g_dve.mark(dve.tensor_tensor(rate[:, GH:2 * GH], rate[:, GH:2 * GH], rate[:, 0:GH], ALU.subtract), "rate")
                    g_pe.wait(dve, "decay", t)
                    g_dve.mark(dve.tensor_tensor(diff[:], gB[:], over_width(rate[:, 0:GH], P), ALU.subtract), "diff")
                    g_dve.wait(dve, "diff", t)
                    g_dve.mark(dve.tensor_tensor(diff[:], diff[:], over_heads(m.c("strict")), ALU.mult), "diff_masked")
                if step == "scaled":
                    g_act.wait(dve, "diff_exp", t)
                    g_dve.mark(dve.tensor_tensor(decay[:], diff[:], over_heads(m.c("causal")), ALU.mult), "decay")
                    dve.wait_ge(in_loaded["k"], 16 * t + 16)
                    beta = m.beta[:, ds(t, 1), :].rearrange("p a h -> p (a h)")
                    g_dve.mark(dve.tensor_tensor(kb[:], k_in[:], over_width(beta, P), ALU.mult), "kb")
                    for j in range(2):
                        last = dve.tensor_scalar(k_rate[:, j, :], rate_exp[:, GH:2 * GH],
                                                 m.c("chunk_cols")[:, j:j + 1], None, ALU.mult)
                    g_dve.mark(last, "k_rate")
                    g_dve.wait(dve, "kb", t)
                    g_dve.mark(dve.tensor_tensor(kbe[:], kb[:], over_width(rate_exp[:, 0:GH], P), ALU.mult), "kbe")
                    dve.wait_ge(in_loaded["q"], 16 * t + 16)
                    g_dve.mark(dve.tensor_tensor(qd[:], q_in[:], over_width(rate_exp[:, 0:GH], P), ALU.mult), "qd")
                if step == "turn_k":
                    g_pe.wait(dve, "kbT", t)
                    g_dve.mark(dve.tensor_copy(kbT[:], gA[:]), "kbT")
                if step == "turn_q":
                    g_pe.wait(dve, "qdT", t)
                    g_dve.mark(dve.tensor_copy(qdT[:], gC[:]), "qdT")
                if step == "overlap":
                    g_pe.wait(dve, "AT", t)
                    g_dve.mark(dve.tensor_tensor(AT[:], gA[:], decay[:], ALU.mult), "AT")
                    g_pe.wait(dve, "QKT", t)
                    g_dve.mark(dve.tensor_tensor(QKT[:], gB[:], decay[:], ALU.mult), "QKT")
                if step == "x0":
                    g_dve.wait(dve, "AT", t)
                    g_dve.mark(dve.tensor_tensor(first[:], AT[:], over_heads(m.c("level0")), ALU.mult), "first")
                    g_dve.wait(dve, "first", t)
                    g_dve.mark(dve.tensor_tensor(XT[:], over_heads(ident), first[:], ALU.subtract), "XT")
                if step[0] == "z" and step[1:].isdigit():
                    n = int(step[1:])
                    if n < 5:
                        g_pe.wait(dve, f"Z{n}", t)
                        g_dve.mark(dve.tensor_tensor(X[:], X[:], gB[:], ALU.subtract), f"X{n}")
                    g_pe.wait(dve, f"ZT{n}", t)
                    g_dve.mark(dve.tensor_tensor(XT[:], XT[:], gC[:], ALU.subtract), f"XT{n}")
                if step == "uw":
                    g_pe.wait(dve, "wT", t)
                    g_dve.mark(dve.tensor_copy(wT[:], gB[:]), "wT")
                if step[:-1] == "read":
                    j = int(step[-1])
                    rows = slice(CHUNK * j, CHUNK * (j + 1))
                    g_act.wait(dve, "u", t)
                    g_pe.wait(dve, f"wS{j}", t)
                    g_dve.mark(dve.tensor_tensor(v_new[rows], u[rows], gC[rows], ALU.subtract), f"v_new{j}")
                    g_dve.mark(dve.tensor_tensor(S_decayed[:], S[:], over_width(rate_exp[:, GH * (2 + j):GH * (3 + j)], P),
                                                 ALU.mult), f"S_decayed{j}")
                if step[:-1] == "write":
                    j = int(step[-1])
                    g_dve.wait(dve, f"S_decayed{j}", t)
                    g_pe.wait(dve, f"dS{j}", t)
                    g_dve.mark(dve.tensor_tensor(S[:], S_decayed[:], gB[:], ALU.add), f"S{j}")
                if step == "within":
                    g_act.wait(dve, "o1", t)
                    g_pe.wait(dve, "within", t)
                    g_dve.mark(dve.tensor_tensor(o[:], o[:], gC[:], ALU.add), "o")
                if step == "gate":
                    g_act.wait(dve, "o_sq", t)
                    g_dve.mark(dve.tensor_scalar(o_ms[:], o_ms[:], 1.0 / GDK, EPS, ALU.mult, ALU.add), "o_ms")
                    g_pool.wait(dve, "o_rs", t)
                    g_dve.mark(dve.tensor_tensor(o_norm[:], o[:], over_width(o_rs[:], P), ALU.mult), "o_norm")
                    dve.wait_ge(in_loaded["z"], 16 * t + 16)
                    g_dve.wait(dve, "o_norm", t)
                    g_dve.mark(dve.tensor_tensor(m.gdn_o[:, ds(t, 1), :].rearrange("p a (h w) -> p (a h) w", h=GH),
                                                 o_norm[:], z_in[:], ALU.mult), "o_out")

            def attend(step, t):
                if step == "up":
                    a_pe.wait(dve, "kv0", t)
                    a_dve.mark(dve.tensor_copy(kh[:, 0:4, 0:NOPE], pT[0][:, :, 0:NOPE]), "k0")
                    a_dve.mark(dve.tensor_copy(vh[:, 0:4, :], pT[0][:, :, NOPE:]), "v0")
                    a_act.wait(dve, "q1", t)
                    x1, x2 = qh[:, :, NOPE:NOPE + HALF], qh[:, :, NOPE + HALF:]
                    dve.tensor_tensor(prod[0][:], x1, m.cos[:], ALU.mult)
                    dve.tensor_tensor(prod[1][:], x2, m.sin[:], ALU.mult)
                    dve.tensor_tensor(prod[2][:], x2, m.cos[:], ALU.mult)
                    a_dve.mark(dve.tensor_tensor(prod[3][:], x1, m.sin[:], ALU.mult), "products")
                    a_dve.wait(dve, "products", t)
                    dve.tensor_tensor(x1, prod[0][:], prod[1][:], ALU.subtract)
                    a_dve.mark(dve.tensor_tensor(x2, prod[2][:], prod[3][:], ALU.add), "rope")
                if step == "turn":
                    for b in range(2):
                        a_pe.wait(dve, f"qT{b}", t)
                        a_dve.mark(dve.tensor_scalar(qhT[:, 512 * b:512 * b + 512], pS[0:QK, 512 * b:512 * b + 512],
                                                     QK ** -0.5, None, ALU.mult), f"qT{b}")
                if step[:5] == "score":
                    j = int(step[5:])
                    base = 512 * (j % 2) if j < 4 else 0
                    a_pe.wait(dve, step, t)
                    a_dve.mark(dve.tensor_reduce(neg_max[:, j:j + 1], pS[:, base:base + width_of(j)], AX_X, ALU.max,
                                                 negate=True), f"max{j}")
                if step[:6] == "spread":
                    j, g = int(step[6]), int(step[8])
                    if on_dve(j, g):
                        n = min(4, j + 1 - 4 * g)
                        a_pe.wait(dve, step, t)
                        a_dve.mark(dve.tensor_copy(probsT[j % 2][:, 4 * g:4 * g + n, :], pT[bank_of[(j, g)]][:, 0:n, :]), step)
                if step == "heads_out":
                    a_act.wait(dve, "exp7", t)
                    a_dve.mark(dve.reciprocal(row_inv[:], row_sum[:]), "row_inv")
                    a_dve.wait(dve, "row_inv", t)
                    a_pe.wait(dve, "value7", t)
                    a_dve.mark(dve.tensor_tensor(m.attn_o[:, :, ds(t * AV, AV)], pO[:], over_width(row_inv[:], AV), ALU.mult), "out")

            order = [(j, g) for j in range(NT) for g in groups[j]]
            bank_of = {x: n % 2 for n, x in enumerate(order)}
            with dve.Fori(0, NT) as t:
                for step in ORDER:
                    delta(step, t) if step in _DELTA else attend(step, t)
            g_dve.end()
            a_dve.end()

        @block.scalar
        def _(act):
            g_act.start(act)
            a_act.start(act)
            look_up(act)

            def delta(step, t):
                if step == "rates":
                    g_dve.wait(act, "rate", t)
                    g_act.mark(act.activation(rate_exp[:], rate[:], ACT.Exp), "rate_exp")
                    g_dve.wait(act, "diff_masked", t)
                    g_act.mark(act.activation(diff[:], diff[:], ACT.Exp), "diff_exp")
                if step == "turn_k":
                    g_pe.wait(act, "kT", t)
                    g_act.mark(act.copy(kT[:], gC[:]), "kT")
                if step == "turn_q":
                    g_pe.wait(act, "qT", t)
                    g_act.mark(act.copy(qT[:], gB[:]), "qT")
                if step == "x0":
                    g_pe.wait(act, "X", t)
                    g_act.mark(act.copy(X[:], gC[:]), "X")
                if step[0] == "y" and step[1:].isdigit():
                    n = int(step[1:])
                    g_pe.wait(act, f"Y{n}", t)
                    g_act.mark(act.copy(Y[:], gA[:]), f"Y{n}")
                if step == "uw":
                    g_pe.wait(act, "u", t)
                    g_act.mark(act.copy(u[:], gA[:]), "u")
                if step[:-1] == "read":
                    j = int(step[-1])
                    rows = slice(CHUNK * j, CHUNK * (j + 1))
                    g_pe.wait(act, f"qS{j}", t)
                    g_act.mark(act.copy(o[rows], gA[rows]), f"o{j}")
                if step == "within":
                    g_dve.wait(act, "o", t)
                    for h in range(GH):
                        last = act.activation(o_sq[:, h, :], o[:, h, :], ACT.Square, accum_out=o_ms[:, h:h + 1])
                    g_act.mark(last, "o_sq")

            def attend(step, t):
                if step == "up":
                    for b in range(2):
                        a_pe.wait(act, f"q{b}", t)
                        a_act.mark(act.copy(qh[:, 4 * b:4 * b + 4, :], pS4[b][:, :, 0:QK]), f"q{b}")
                    a_pe.wait(act, "kv1", t)
                    a_act.mark(act.copy(kh[:, 4:8, 0:NOPE], pT[1][:, :, 0:NOPE]), "k1")
                    a_act.mark(act.copy(vh[:, 4:8, :], pT[1][:, :, NOPE:]), "v1")
                if step == "turn":
                    for b in range(2):
                        a_pe.wait(act, f"kT{b}", t)
                        a_act.mark(act.copy(khT[:, 512 * b:512 * b + 512], pT[b][0:QK].rearrange("p t w -> p (t w)")), f"kT{b}")
                if step[:5] == "score":
                    j = int(step[5:])
                    base = 512 * (j % 2) if j < 4 else 0
                    a_dve.wait(act, f"max{j}", t)
                    a_act.mark(act.activation(probs[j % 2][:, 0:width_of(j)], pS[:, base:base + width_of(j)], ACT.Exp,
                                              bias=neg_max[:, j:j + 1], accum_out=row_sum[:, j:j + 1]), f"exp{j}")
                if step[:6] == "spread":
                    j, g = int(step[6]), int(step[8])
                    if not on_dve(j, g):
                        n = min(4, j + 1 - 4 * g)
                        a_pe.wait(act, step, t)
                        a_act.mark(act.copy(probsT[j % 2][:, 4 * g:4 * g + n, :], pT[bank_of[(j, g)]][:, 0:n, :]), step)

            order = [(j, g) for j in range(NT) for g in groups[j]]
            bank_of = {x: n % 2 for n, x in enumerate(order)}
            with act.Fori(0, NT) as t:
                for step in ORDER:
                    delta(step, t) if step in _DELTA else attend(step, t)
            g_act.end()
            a_act.end()


def route(nc, A, m):
    with ExitStack() as own:
        def sb(name, shape, dt=F32):
            return own.enter_context(nc.sbuf_tensor(name, shape, dt))

        def sem(name):
            return own.enter_context(nc.semaphore(name))

        def pair(name, shape, dt=F32):
            return [sb(f"{name}{u}", shape, dt) for u in range(2)]

        w_out = sb("w_out_sb", [P, KD, D_MODEL])
        router_w, router_b = sb("router_w_sb", [P, KD, NE]), sb("router_b_sb", [1, NE])
        gdn_w, mla_w, ffn_w = sb("gdn_w", [P, 1]), sb("mla_w", [P, 4]), sb("ffn_w", [P, KD])
        squares = pair("route_squares", [P, D_MODEL], mybir.dt.bfloat16)
        x, x2, h2 = pair("x", [P, D_MODEL]), pair("x2", [P, D_MODEL]), pair("h2", [P, D_MODEL])
        gdn_s, attn_s = pair("gdn_s", [P, GW]), pair("attn_s", [P, AH * AV])
        mixT, h2T = pair("mixT", [P, KD, P]), pair("h2T", [P, KD, P])
        ms_a, rs_a = sb("ms_a", [P, NT]), sb("rs_a", [P, NT])
        ms_x, rs_x = pair("ms_x", [P, 1]), pair("rs_x", [P, 1])
        power = sb("route_power", [P, NT])
        logits, top, index = pair("logits", [P, NE]), pair("top", [P, 8]), pair("index", [P, 8], U32)
        index_f, top_neg = pair("index_f", [P, TOPK]), pair("top_neg", [P, 1])
        chosen, placed = pair("chosen", [P, TOPK, NE]), pair("placed", [P, TOPK, NE])
        picked, seen, rows = pair("picked", [P, NE]), sb("seen", [P, NE]), pair("rows", [P, NE])
        dest_f, dest = pair("dest_f", [P, TOPK]), pair("dest", [P, TOPK], I32)
        gates, gate_sum, entry = pair("gates", [P, TOPK]), pair("gate_sum", [P, 1]), pair("entry", [P, TOPK, 2], I32)
        token = sb("token", [P, 1])
        pads = sb("pads", [P, NE * SEQ // P, 2], I32)
        count, items, ends, ended, base = (sb(n, [TABLE, NE]) for n in ("count", "items", "ends", "ended", "base"))
        over = sb("over", [TABLE, NE, ITEMS_OF_EXPERT])
        zeros = sb("zeros_e", [TABLE, NE])
        table_f = sb("table_f", [TABLE, 4])
        mine, tokens, wide = sb("mine", [TABLE, NE]), sb("tokens", [TABLE, 1]), sb("wide", [TABLE, len(WIDTHS)])
        first_item = sb("first_item", [TABLE, 1])

        pT = [own.enter_context(nc.psum_tensor(f"rT{b}", [P, 4, P], F32)) for b in range(2)]
        pH = [own.enter_context(nc.psum_tensor(f"rH{b}", [P, 4, P], F32)) for b in range(2)]
        pOut = [own.enter_context(nc.psum_tensor(f"pOut{b}", [P, 512], F32)) for b in range(2)]
        pL = own.enter_context(nc.psum_tensor("pL", [P, 512], F32))

        mix_pe, out_pe = Stages(sem("mix_pe"), ["turned"]), Stages(sem("out_pe"), ["out"])
        route_pe = Stages(sem("route_pe"), ["h2T", "logits", "place"])
        copy_act, mix_act = Stages(sem("copy_act"), ["copied"]), Stages(sem("mix_act"), ["mixT"])
        x_act, gate_act = Stages(sem("x_act"), ["x_sq"]), Stages(sem("gate_act"), ["gates"])
        x_dve = Stages(sem("x_dve"), ["x2", "ms_x", "h2"])
        route_dve = Stages(sem("route_dve"), ["h2T", "logits", "top", "index", "index_f", "chosen", "picked", "top_neg",
                                              "rows", "seen", "placed", "dest_f", "dest", "gate_inv", "entry"])
        x_pool, list_pool = Stages(sem("x_pool"), ["rs_x"]), Stages(sem("list_pool"), ["scattered"], lead=2)
        store_sp = Stages(sem("store_sp"), ["stored"], lead=2)
        attn_sq, attn_ms, attn_rs, attn_n = (sem(n) for n in ("attn_sq", "attn_ms", "attn_rs", "attn_n"))
        x_loaded = [sem(f"rx_loaded{u}") for u in range(2)]
        x2_stored, h2_stored = [sem(f"x2_stored{u}") for u in range(2)], [sem(f"h2_stored{u}") for u in range(2)]
        w_loaded = [sem(f"w_out_loaded{b}") for b in range(2)]
        r_small, r_zeroed, pool_turn, dve_turn, act_turn = (
            sem(n) for n in ("r_small", "r_zeroed", "r_pool_turn", "r_dve_turn", "r_act_turn"))
        filled, scattered, pads_made = sem("filled"), sem("scattered"), sem("pads_made")
        chain, counts_psum, table_psum = sem("r_chain"), sem("counts_psum"), sem("table_psum")
        ident = m.c("ident")

        def slots(eng, slot):
            slot(0, 0, 0, first=True)
            with eng.Fori(0, (NT - 2) // 2) as it:
                slot(it * 2 + 1, 1, it)
                slot(it * 2 + 2, 0, it + 1)
            slot(NT - 1, 1, NT // 2 - 1, last=True)

        block = own.enter_context(nc.Block())

        @block.sync
        def _(sp):
            store_sp.start(sp)
            sp.dma_start(gdn_w[:], A["gdn_norm"]).then_inc(r_small, 16)
            sp.dma_start(mla_w[:], A["mla_norm"]).then_inc(r_small, 16)
            sp.dma_start(ffn_w[:], A["norm_ffn"]).then_inc(r_small, 16)
            sp.dma_start(router_b[:], A["router_b"]).then_inc(r_small, 16)
            sp.dma_start(router_w[:], A["router_w"].rearrange("(k p) e -> p k e", p=P)).then_inc(r_small, 16)
            for b in range(2):
                sp.dma_start(w_out[:, :, 512 * b:512 * b + 512],
                             A["w_out"].rearrange("(k p) f -> p k f", p=P)[:, :, 512 * b:512 * b + 512]).then_inc(w_loaded[b], 16)
            sp.wait_ge(pads_made, 1)
            sp.dma_start(m.places.rearrange("(p n) c -> p n c", p=P), pads[:]).then_inc(filled, 16)
            sp.dma_start(x[0][:], A["x"][0:P, :]).then_inc(x_loaded[0], 16)

            def slot(i, u, p, first=False, last=False):
                if not last:
                    x_dve.wait(sp, "x2", i, back=1)
                    sp.dma_start(x[1 - u][:], A["x"][ds((i + 1) * P, P), :]).then_inc(x_loaded[1 - u], 16)
                x_dve.wait(sp, "x2", i)
                sp.dma_start(m.y[ds(i * P, P), :], x2[u][:]).then_inc(x2_stored[u], 16)
                x_dve.wait(sp, "h2", i)
                sp.dma_start(m.h2_rows[ds(i * P, P), :], h2[u][:]).then_inc(h2_stored[u], 16)
                sp.wait_ge(x2_stored[u], 16 * p + 16)
                sp.wait_ge(h2_stored[u], 16 * p + 16)
                store_sp.mark_now(sp, "stored")

            slots(sp, slot)
            store_sp.end()

        @block.gpsimd
        def _(pool):
            for stages in (x_pool, list_pool):
                stages.start(pool)
            pool.memset(power[:], -0.5).then_inc(r_zeroed, 1)
            pool.memset(seen[:], 0.0).then_inc(r_zeroed, 1)
            pool.memset(zeros[:], 0.0).then_inc(r_zeroed, 1)
            pool.memset(pads[:, :, 1:2], 0)
            pool.memset(pads[:, :, 0:1], PAD).then_inc(pads_made, 1)
            pool.wait_ge(r_zeroed, 3)
            pool.wait_ge(attn_ms, 1)
            pool.tensor_tensor(rs_a[:], ms_a[:], power[:], ALU.pow).then_inc(attn_rs, 1)
            pool.wait_ge(filled, 16)

            def scatter(i, u):
                route_dve.wait(pool, "entry", i)
                pool.sem_inc(pool_turn, 1)
                for k in range(TOPK):
                    pool.indirect_dma_start(m.places, bass.IndirectOffsetOnAxis(dest[u][:, k:k + 1].bitcast(U32), 0),
                                            entry[u][:, k, :], None).then_inc(scattered, 16)
                pool.wait_ge(scattered, (i + 1) * 16 * TOPK)
                list_pool.mark_now(pool, "scattered")

            def slot(i, u, p, first=False, last=False):
                x_dve.wait(pool, "ms_x", i)
                pool.sem_inc(pool_turn, 1)
                x_pool.mark(pool.tensor_tensor(rs_x[u][:], ms_x[u][:], power[:, 0:1], ALU.pow), "rs_x")
                if not first:
                    scatter(i - 1, 1 - u)

            slots(pool, slot)
            scatter(NT - 1, 1)
            for stages in (x_pool, list_pool):
                stages.end()

        @block.tensor
        def _(pe):
            for stages in (mix_pe, out_pe, route_pe):
                stages.start(pe)
            pe.wait_ge(r_small, 80)
            pe.wait_ge(r_zeroed, 3)

            def turn_mixed(i, u):
                copy_act.wait(pe, "copied", i)
                mix_act.wait(pe, "mixT", i, back=1)
                for k in range(4):
                    pe.transpose(pT[0][:, k, :], gdn_s[u][:, k * P:(k + 1) * P], ident)
                for k in range(4):
                    done = pe.transpose(pT[1][:, k, :], attn_s[u][:, k * P:(k + 1) * P], ident)
                mix_pe.mark(done, "turned")

            def out_products(u, b, tiles):
                for k in tiles:
                    done = pe.matmul(pOut[b][:], mixT[u][:, k, :], w_out[:, k, 512 * b:512 * b + 512],
                                     start=k == 0, stop=k == KD - 1)
                return done

            def turn_h2(i, u):
                x_dve.wait(pe, "h2", i)
                route_dve.wait(pe, "h2T", i, back=1)
                for k in range(KD):
                    done = pe.transpose(pH[k // 4][:, k % 4, :], h2[u][:, k * P:(k + 1) * P], ident)
                route_pe.mark(done, "h2T")

            def router(i, u):
                route_dve.wait(pe, "h2T", i)
                pe.matmul(pL[:, 0:NE], m.c("ones", 1), router_b[:], start=True, stop=False)
                for k in range(KD):
                    done = pe.matmul(pL[:, 0:NE], h2T[u][:, k, :], router_w[:, k, :], start=False, stop=k == KD - 1)
                route_pe.mark(done, "logits")

            def count_earlier(i, u):
                route_dve.wait(pe, "picked", i)
                pe.matmul(pL[:, NE:2 * NE], m.c("before"), picked[u][:], start=True, stop=False)
                route_pe.mark(pe.matmul(pL[:, NE:2 * NE], m.c("ones"), seen[:], start=False, stop=True), "place")

            def slot(i, u, p, first=False, last=False):
                mix_act.wait(pe, "mixT", i)
                x_dve.wait(pe, "x2", i, back=1)
                pe.wait_ge(w_loaded[0], 16)
                out_products(u, 0, range(KD))
                if not first:
                    turn_h2(i - 1, 1 - u)
                pe.wait_ge(w_loaded[1], 16)
                out_products(u, 1, range(KD // 2))
                if not first:
                    router(i - 1, 1 - u)
                if not last:
                    turn_mixed(i + 1, 1 - u)
                out_pe.mark(out_products(u, 1, range(KD // 2, KD)), "out")
                if not first:
                    count_earlier(i - 1, 1 - u)

            turn_mixed(0, 0)
            slots(pe, slot)
            turn_h2(NT - 1, 1)
            router(NT - 1, 1)
            count_earlier(NT - 1, 1)
            for stages in (mix_pe, out_pe, route_pe):
                stages.end()
            route_dve.wait(pe, "entry", NT - 1)
            pe.matmul(pL[0:TABLE, 0:NE], m.c("ones")[:, 0:TABLE], seen[:], start=True, stop=True).then_inc(counts_psum, 1)
            pe.wait_ge(chain, 21)
            for c in range(4):
                last = pe.transpose(pL[0:1, TABLE * c:TABLE * (c + 1)], table_f[:, c:c + 1], ident[0:TABLE, 0:TABLE])
            last.then_inc(table_psum, 1)

        @block.scalar
        def _(act):
            for stages in (copy_act, mix_act, x_act, gate_act):
                stages.start(act)
            for i in range(NT):
                act.activation(squares[0][:, 0:AH * AV], m.attn_o[:, i, :], ACT.Square, accum_out=ms_a[:, i:i + 1]).then_inc(attn_sq, 1)
                act.wait_ge(attn_sq, i + 1)
            act.wait_ge(attn_n, NT)
            act.wait_ge(r_small, 80)

            def copy_mixed(i, u):
                mix_pe.wait(act, "turned", i, back=1)
                act.sem_inc(act_turn, 1)
                act.copy(gdn_s[u][:].unsqueeze(1), m.gdn_o[:, ds(i, 1), :])
                copy_act.mark(act.copy(attn_s[u][:].unsqueeze(1), m.attn_o[:, ds(i, 1), :]), "copied")

            def take_mixed(i, u):
                mix_pe.wait(act, "turned", i)
                out_pe.wait(act, "out", i, back=1)
                act.sem_inc(act_turn, 1)
                act.activation(mixT[u][:, 0:4, :], pT[0][:], ACT.Copy, scale=gdn_w[:])
                for k in range(4):
                    done = act.activation(mixT[u][:, 4 + k, :], pT[1][:, k, :], ACT.Copy, scale=mla_w[:, k:k + 1])
                mix_act.mark(done, "mixT")

            def take_gates(i, u):
                route_dve.wait(act, "top_neg", i)
                gate_act.mark(act.activation(gates[u][:], top[u][:, 0:TOPK], ACT.Exp, bias=top_neg[u][:],
                                             accum_out=gate_sum[u][:]), "gates")

            def slot(i, u, p, first=False, last=False):
                if not last:
                    copy_mixed(i + 1, 1 - u)
                    take_mixed(i + 1, 1 - u)
                if not first:
                    take_gates(i - 1, 1 - u)
                x_dve.wait(act, "x2", i)
                x_act.mark(act.activation(squares[u][:], x2[u][:], ACT.Square, accum_out=ms_x[u][:]), "x_sq")

            copy_mixed(0, 0)
            take_mixed(0, 0)
            slots(act, slot)
            take_gates(NT - 1, 1)
            for stages in (copy_act, mix_act, x_act, gate_act):
                stages.end()

        @block.vector
        def _(dve):
            for stages in (x_dve, route_dve):
                stages.start(dve)
            dve.wait_ge(r_small, 80)
            dve.wait_ge(r_zeroed, 3)
            dve.tensor_copy(token[:], m.c("row")).then_inc(r_zeroed, 1)
            dve.wait_ge(r_zeroed, 4)
            dve.wait_ge(attn_sq, NT)
            dve.tensor_scalar(ms_a[:], ms_a[:], 1.0 / (AH * AV), EPS, ALU.mult, ALU.add).then_inc(attn_ms, 1)
            dve.wait_ge(attn_rs, 1)
            for i in range(NT):
                dve.tensor_scalar(m.attn_o[:, i, :], m.attn_o[:, i, :], rs_a[:, i:i + 1], None, ALU.mult).then_inc(attn_n, 1)

            def choose(i, u):
                route_pe.wait(dve, "h2T", i)
                for b in range(2):
                    done = dve.tensor_tensor(h2T[u][:, 4 * b:4 * b + 4, :], pH[b][:], over_width(ffn_w[:, 4 * b:4 * b + 4], P), ALU.mult)
                route_dve.mark(done, "h2T")
                route_pe.wait(dve, "logits", i)
                route_dve.mark(dve.tensor_copy(logits[u][:], pL[:, 0:NE]), "logits")
                route_dve.wait(dve, "logits", i)
                dve.sem_inc(dve_turn, 1)
                route_dve.mark(dve.max(top[u][:], logits[u][:]), "top")
                route_dve.wait(dve, "top", i)
                dve.sem_inc(dve_turn, 1)
                route_dve.mark(dve.max_index(index[u][:], top[u][:], logits[u][:]), "index")
                route_dve.wait(dve, "index", i)
                route_dve.mark(dve.tensor_copy(index_f[u][:], index[u][:, 0:TOPK]), "index_f")
                route_dve.wait(dve, "index_f", i)
                route_dve.mark(dve.tensor_tensor(chosen[u][:], over_heads(m.c("experts"), TOPK), over_width(index_f[u][:], NE),
                                                 ALU.is_equal), "chosen")
                route_dve.wait(dve, "chosen", i)
                route_dve.mark(dve.tensor_reduce(picked[u][:], chosen[u][:].rearrange("p k e -> p e k"), AX_X, ALU.add), "picked")
                route_dve.mark(dve.tensor_scalar(top_neg[u][:], top[u][:, 0:1], -1.0, None, ALU.mult), "top_neg")

            def list_tile(i, u):
                route_pe.wait(dve, "place", i)
                route_dve.mark(dve.tensor_tensor(rows[u][:], pL[:, NE:2 * NE], m.c("expert_rows"), ALU.add), "rows")
                route_dve.mark(dve.tensor_tensor(seen[:], seen[:], picked[u][:], ALU.add), "seen")
                route_dve.wait(dve, "rows", i)
                route_dve.mark(dve.tensor_tensor(placed[u][:], chosen[u][:], over_heads(rows[u][:], TOPK), ALU.mult), "placed")
                route_dve.wait(dve, "placed", i)
                route_dve.mark(dve.tensor_reduce(dest_f[u][:], placed[u][:], AX_X, ALU.add), "dest_f")
                route_dve.wait(dve, "dest_f", i)
                list_pool.wait(dve, "scattered", i, back=2)
                route_dve.mark(dve.tensor_copy(dest[u][:], dest_f[u][:]), "dest")
                gate_act.wait(dve, "gates", i)
                route_dve.mark(dve.reciprocal(gate_sum[u][:], gate_sum[u][:]), "gate_inv")
                route_dve.wait(dve, "gate_inv", i)
                dve.tensor_copy(entry[u][:, :, 0:1], bc(token[:].unsqueeze(2), [P, TOPK, 1]))
                route_dve.mark(dve.tensor_scalar(entry[u][:, :, 1:2].bitcast(F32), gates[u][:].unsqueeze(2), gate_sum[u][:], None,
                                                 ALU.mult), "entry")
                route_dve.wait(dve, "entry", i)
                dve.tensor_scalar(token[:], token[:], float(P), None, ALU.add)

            def slot(i, u, p, first=False, last=False):
                if not first:
                    choose(i - 1, 1 - u)
                out_pe.wait(dve, "out", i)
                dve.wait_ge(x_loaded[u], 16 * p + 16)
                store_sp.wait(dve, "stored", i, back=2)
                for b in range(2):
                    cols = slice(512 * b, 512 * b + 512)
                    done = dve.tensor_tensor(x2[u][:, cols], pOut[b][:], x[u][:, cols], ALU.add)
                x_dve.mark(done, "x2")
                if not first:
                    list_tile(i - 1, 1 - u)
                x_act.wait(dve, "x_sq", i)
                x_dve.mark(dve.tensor_scalar(ms_x[u][:], ms_x[u][:], 1.0 / D_MODEL, EPS, ALU.mult, ALU.add), "ms_x")
                x_pool.wait(dve, "rs_x", i)
                x_dve.mark(dve.tensor_scalar(h2[u][:], x2[u][:], rs_x[u][:], None, ALU.mult), "h2")

            slots(dve, slot)
            choose(NT - 1, 1)
            list_tile(NT - 1, 1)
            for stages in (x_dve, route_dve):
                stages.end()
            link = Chain(dve, chain).link
            dve.wait_ge(counts_psum, 1)
            link(dve.tensor_copy(count[:], pL[0:TABLE, 0:NE]))
            link(dve.tensor_tensor(over[:], over_width(count[:], ITEMS_OF_EXPERT), over_heads(m.c("bounds", TABLE), NE), ALU.is_gt))
            link(dve.tensor_reduce(items[:], over[:], AX_X, ALU.add))
            link(dve.tensor_tensor_scan(ends[:], items[:], zeros[:], 0.0, ALU.add, ALU.add))
            link(dve.tensor_scalar(ended[:], ends[:], m.c("row", TABLE), None, ALU.is_le))
            link(dve.tensor_tensor(base[:], ended[:], items[:], ALU.mult))
            link(dve.tensor_reduce(first_item[:], base[:], AX_X, ALU.add))
            link(dve.tensor_reduce(table_f[:, 0:1], ended[:], AX_X, ALU.add))
            link(dve.tensor_scalar(table_f[:, 0:1], table_f[:, 0:1], float(NE - 1), None, ALU.min))
            link(dve.tensor_tensor(first_item[:], m.c("row", TABLE), first_item[:], ALU.subtract))
            link(dve.tensor_scalar(table_f[:, 1:2], table_f[:, 0:1], float(SEQ), None, ALU.mult))
            link(dve.scalar_tensor_tensor(out=table_f[:, 1:2], in0=first_item[:], scalar=float(ITEM), in1=table_f[:, 1:2],
                                          op0=ALU.mult, op1=ALU.add))
            link(dve.tensor_scalar(table_f[:, 1:2], table_f[:, 1:2], float(PLACES - ITEM), None, ALU.min))
            link(dve.tensor_copy(table_f[:, 2:3], ends[:, NE - 1:NE]))
            link(dve.tensor_scalar(mine[:], m.c("experts", TABLE), table_f[:, 0:1], None, ALU.is_equal))
            link(dve.tensor_tensor(mine[:], mine[:], count[:], ALU.mult))
            link(dve.tensor_reduce(tokens[:], mine[:], AX_X, ALU.add))
            link(dve.scalar_tensor_tensor(out=tokens[:], in0=first_item[:], scalar=-float(ITEM), in1=tokens[:],
                                          op0=ALU.mult, op1=ALU.add))
            link(dve.tensor_scalar(wide[:], m.c("narrower", TABLE), tokens[:], None, ALU.is_lt))
            link(dve.tensor_reduce(table_f[:, 3:4], wide[:], AX_X, ALU.add))
            link(dve.tensor_scalar(table_f[:, 3:4], table_f[:, 3:4], 1.0, None, ALU.max))
            dve.wait_ge(table_psum, 1)
            link(dve.tensor_copy(m.table[:], pL[0:1, 0:4 * TABLE]))


W1_CHUNKS, W2_CHUNKS = 4, 2


def experts(nc, A, m):
    with ExitStack() as own:
        def sb(name, shape, dt=F32):
            return own.enter_context(nc.sbuf_tensor(name, shape, dt))

        def sem(name):
            return own.enter_context(nc.semaphore(name))

        w1 = [sb(f"w1_{c}", [P, KD, 512]) for c in range(W1_CHUNKS)]
        w2 = [sb(f"w2_in_sb{h}", [P, KD // 2, 512]) for h in range(2)]
        w2_hi = [sb(f"w2_hi{c}", [P, KD, 512], F32R) for c in range(W2_CHUNKS)]
        w2_lo = [sb(f"w2_lo{c}", [P, KD, 512], F32R) for c in range(W2_CHUNKS)]
        b1, ffn_w = sb("b1_sb", [P, NE, KD, 2]), sb("ffn_cols", [P, KD])
        b1_item, b2_item = sb("b1_item", [P, KD, 2]), sb("b2_item", [P, D_MODEL])
        later_places, next_places, places = (sb(n, [P, BLOCKS, 2], I32) for n in ("later_places", "next_places", "item_places"))
        rows = sb("item_rows", [P, BLOCKS, D_MODEL])
        xT, act_hi, act_lo = sb("xT", [P, KD, ITEM]), sb("act_hi", [P, KD, ITEM], F32R), sb("act_lo", [P, KD, ITEM], F32R)
        glu, lin, sig, act_sb = ([sb(f"{n}{u}", [P, ITEM]) for u in range(2)] for n in ("glu", "lin", "sig", "act_sb"))
        y_rows = sb("y_rows", [P, BLOCKS, D_MODEL])
        pH = [own.enter_context(nc.psum_tensor(f"pH{b}", [P, 2, ITEM], F32)) for b in range(4)]
        pY = [[own.enter_context(nc.psum_tensor(f"pY{b}{c}", [P, 512], F32)) for c in range(W2_CHUNKS)] for b in range(BLOCKS)]

        w1_in, w2_in = [sem(f"w1_in{c}") for c in range(W1_CHUNKS)], [sem(f"w2_in{h}") for h in range(2)]
        small, cleared, psum_cleared = sem("e_small"), sem("e_cleared"), sem("e_psum_cleared")
        pool_turn, dve_turn, sp_turn = sem("e_pool_turn"), sem("e_dve_turn"), sem("e_sp_turn")
        hidden = Stages(sem("hidden"), [str(j) for j in range(KD)])
        block_pe = [Stages(sem(f"block_pe{b}"), [str(c) for c in range(W2_CHUNKS)]) for b in range(BLOCKS)]
        x_turned = Stages(sem("x_turned"), [str(f) for f in range(2 * BLOCKS)])
        eighth_at = {0: 0, 1: 1, 2: 2, 3: 3, 5: 4, 6: 5}
        later = [j for j in range(KD) if j not in eighth_at.values()]
        e_act = Stages(sem("e_act"), [x for j in range(KD) for x in
                                      [f"sig{j}"] + ([f"w2_hi{eighth_at[j]}"] if j in eighth_at else []) + [f"act_hi{j}"]]
                       + [f"w2_hi{j}" for j in later])
        x_read = Stages(sem("x_read"), [str(f) for f in range(2 * BLOCKS)])
        e_dve = Stages(sem("e_dve"), ["bias"] + [x for j in range(KD) for x in
                                                 [f"glu{j}", f"lin{j}", f"prod{j}", f"act{j}"]
                                                 + ([f"w2_lo{eighth_at[j]}"] if j in eighth_at else []) + [f"act_lo{j}"]]
                       + [f"w2_lo{j}" for j in later]
                       + [f"{x}{c}{b}" for c in range(W2_CHUNKS) for b in range(BLOCKS) for x in ("sum", "y")])
        e_pool = Stages(sem("e_pool"), ["current", "gathered", "next"])
        b2_in = sem("b2_in")
        gathered, added, listed = sem("gathered"), sem("added"), sem("listed")
        ident = m.c("ident")

        def number_of_items(eng):
            return eng.value_load(m.table[0:1, 2 * TABLE:2 * TABLE + 1], min_val=1, max_val=MAX_ITEMS)

        def expert_of(eng, n):
            return eng.value_load(m.table[0:1, ds(n, 1)], min_val=0, max_val=NE - 1)

        def place_of(eng, n):
            return eng.value_load(m.table[0:1, ds(n + TABLE, 1)], min_val=0, max_val=PLACES - ITEM)

        def read_width(eng, register, n):
            eng.reg_load(register, m.table[0:1, ds(n + 3 * TABLE, 1)])

        block = own.enter_context(nc.Block())

        @block.sync
        def _(sp):
            items = number_of_items(sp)

            def load_w1(e, c):
                rows = A["w1"][ds(e, 1)].rearrange("a (k p) f -> p (a k) f", p=P)
                sp.dma_start(w1[c][:], rows[:, :, 512 * c:512 * c + 512]).then_inc(w1_in[c], 16)

            def load_w2(e, c, h):
                rows = A["w2"][ds(e, 1)].rearrange("a (k p) f -> p (a k) f", p=P)
                sp.dma_start(w2[h][:], rows[:, 4 * h:4 * h + 4, 512 * c:512 * c + 512]).then_inc(w2_in[h], 16)

            e = expert_of(sp, 0)
            load_w1(e, 0)
            sp.wait_ge(gathered, 16 * BLOCKS)
            load_w1(e, 1)
            with sp.Fori(0, items) as n:
                e, next_e = expert_of(sp, n), expert_of(sp, n + 1)
                for c in (2, 3):
                    hidden.wait(sp, str(2 * c + 1), n, back=1)
                    load_w1(e, c)
                for h in range(2):
                    e_dve.wait(sp, f"w2_lo{5 + 2 * h}", n, back=1)
                    load_w2(e, 0, h)
                e_dve.wait(sp, "y11", n, back=1)
                sp.dma_start(b2_item[:], bc(A["b2"][ds(e, 1), :], [P, D_MODEL])).then_inc(b2_in, 16)
                e_dve.wait(sp, "w2_lo1", n)
                load_w2(e, 1, 0)
                hidden.wait(sp, "1", n)
                load_w1(next_e, 0)
                e_dve.wait(sp, "w2_lo3", n)
                load_w2(e, 1, 1)
                hidden.wait(sp, "3", n)
                load_w1(next_e, 1)
            for c in (0, 1):
                sp.wait_ge(w1_in[c], 16 * items + 16)
                sp.sem_inc(sp_turn, 1)

        @block.gpsimd
        def _(pool):
            e_pool.start(pool)

            def list_places(n):
                pool.dma_start(later_places[:], m.places[ds(place_of(pool, n), ITEM), :].rearrange("(b p) c -> p b c", p=P))\
                    .then_inc(listed, 16)

            def gather():
                for b in range(BLOCKS):
                    pool.indirect_dma_start(rows[:, b, :], None, m.h2_rows,
                                            bass.IndirectOffsetOnAxis(later_places[:, b, 0:1].bitcast(U32), 0),
                                            bounds_check=SEQ - 1, oob_is_err=False).then_inc(gathered, 16)

            def copy_places(to, of):
                pool.tensor_copy(to[:, :, 0:1], of[:, :, 0:1]).then_inc(pool_turn, 1)
                return pool.tensor_copy(to[:, :, 1:2].bitcast(F32), of[:, :, 1:2].bitcast(F32))

            pool.memset(rows[:], 0.0).then_inc(cleared, 1)
            pool.wait_ge(cleared, 1)
            items = number_of_items(pool)
            list_places(0)
            pool.wait_ge(listed, 16)
            gather()
            pool.wait_ge(gathered, 16 * BLOCKS)
            copy_places(places, later_places).then_inc(cleared, 1)
            pool.wait_ge(cleared, 2)
            list_places(1)
            pool.wait_ge(listed, 32)
            pool.wait_ge(x_turned.sem, 2 * BLOCKS)
            gather()
            pool.wait_ge(gathered, 32 * BLOCKS)
            copy_places(next_places, later_places).then_inc(cleared, 1)
            pool.wait_ge(cleared, 3)
            list_places(2)
            with pool.Fori(0, items) as n:
                pool.wait_ge(listed, 16 * n + 48)
                x_turned.wait(pool, "3", n)
                pool.sem_inc(pool_turn, 1)
                gather()
                e_dve.wait(pool, "y11", n)
                pool.sem_inc(pool_turn, 1)
                for b in range(BLOCKS):
                    pool.indirect_dma_start(m.y, bass.IndirectOffsetOnAxis(places[:, b, 0:1].bitcast(U32), 0), y_rows[:, b, :],
                                            None, bounds_check=SEQ - 1, oob_is_err=False, compute_op=ALU.add).then_inc(added, 16)
                pool.wait_ge(added, 16 * BLOCKS * n + 16 * BLOCKS)
                pool.sem_inc(pool_turn, 1)
                e_pool.mark(copy_places(places, next_places), "current")
                e_pool.wait(pool, "current", n)
                pool.wait_ge(gathered, 16 * BLOCKS * n + 48 * BLOCKS)
                e_pool.mark_now(pool, "gathered")
                e_pool.mark(copy_places(next_places, later_places), "next")
                e_pool.wait(pool, "next", n)
                pool.sem_inc(pool_turn, 1)
                list_places(n + 3)
            pool.wait_ge(listed, 16 * items + 48)
            pool.sem_inc(pool_turn, 1)
            e_pool.end()

        @block.tensor
        def _(pe):
            for stages in (hidden, *block_pe):
                stages.start(pe)
            items = number_of_items(pe)

            def turn_rows(n, fills, first=False):
                for f in fills:
                    if not first:
                        e_dve.wait(pe, f"prod{4 + f}", n)
                    for k in range(4):
                        at = (4 * (f % 2) + k) * P
                        last = pe.transpose(pH[f][:].rearrange("p a (b w) -> p (a b) w", w=P)[:, k, :],
                                            rows[:, f // 2, at:at + P], ident)
                    if first:
                        last.then_inc(x_turned.sem, 1)
                    else:
                        x_turned.mark(last, str(f))

            def hidden_products(n, width):
                hidden.made = []
                for j in range(KD):
                    if j % 2 == 0:
                        pe.wait_ge(w1_in[j // 2], 16 * n + 16)
                    if j < 4:
                        x_read.wait(pe, "3", n, back=1)
                    else:
                        e_dve.wait(pe, f"lin{j - 4}", n)
                    for part in range(2):
                        for k in range(KD):
                            at = 256 * (j % 2) + part
                            last = pe.matmul(pH[j % 4][:, part, 0:width], w1[j // 2][:, k, at:at + 255:2], xT[:, k, 0:width],
                                             start=k == 0, stop=k == KD - 1)
                    hidden.mark(last, str(j))

            def token_products(n, b, c):
                e_dve.wait(pe, f"w2_lo{4 * c + 3}", n)
                e_dve.wait(pe, f"y{c}{b}", n, back=1)
                for j in range(KD):
                    if (b, c) == (0, 0) and j >= KD - 3:
                        e_dve.wait(pe, f"act_lo{j}", n)
                    hi, lo = act_hi[:, j, b * P:(b + 1) * P], act_lo[:, j, b * P:(b + 1) * P]
                    pe.matmul(pY[b][c][:], hi, w2_hi[c][:, j, :], start=j == 0, stop=False)
                    pe.matmul(pY[b][c][:], hi, w2_lo[c][:, j, :], start=False, stop=False)
                    last = pe.matmul(pY[b][c][:], lo, w2_hi[c][:, j, :], start=False, stop=j == KD - 1)
                block_pe[b].mark(last, str(c))

            def for_width(width, products):
                half = P * 5 // 4
                low = [r for r, columns in enumerate(WIDTHS, 1) if columns <= half]
                for upper, ranks in ((False, low), (True, range(len(low) + 1, len(WIDTHS) + 1))):
                    with pe.If(width > len(low) if upper else width <= len(low)):
                        for rank in ranks:
                            with pe.If(width == rank):
                                products(WIDTHS[rank - 1])

            pe.wait_ge(cleared, 2)
            pe.wait_ge(psum_cleared, 8)
            turn_rows(0, range(2 * BLOCKS), first=True)
            next_width = pe.alloc_register("next_width")
            read_width(pe, next_width, 0)
            with pe.Fori(0, items) as n:
                width = pe.snap(next_width, min_val=1, max_val=len(WIDTHS))
                for_width(width, lambda columns: hidden_products(n, columns))
                e_pool.wait(pe, "gathered", n, back=1)
                pe.wait_ge(cleared, 3)
                turn_rows(n, range(2 * BLOCKS - 1))
                read_width(pe, next_width, n + 1)
                e_dve.wait(pe, f"act_lo{KD - 4}", n)
                for c in range(W2_CHUNKS):
                    token_products(n, 0, c)
                    if c == 0:
                        turn_rows(n, [2 * BLOCKS - 1])
                    with pe.If(width > 1):
                        token_products(n, 1, c)
                    with pe.If(width == 1):
                        pe.sem_inc(block_pe[1].sem, 1)
            for stages in (hidden, x_turned, *block_pe):
                stages.end()

        @block.scalar
        def _(act):
            e_act.start(act)
            act.dma_start(b1[:], A["b1"]).then_inc(small, 16)
            act.dma_start(ffn_w[:], A["norm_ffn"]).then_inc(small, 16)
            with act.Fori(0, number_of_items(act)) as n:
                def high_part(j):
                    c, k = j // 4, 2 * (j % 4)
                    act.wait_ge(w2_in[k // 4], 16 * W2_CHUNKS * n + 16 * c + 16)
                    if k == 0:
                        for b in range(BLOCKS):
                            block_pe[b].wait(act, str(c), n, back=1)
                    e_act.mark(act.copy(w2_hi[c][:, k:k + 2, :], w2[k // 4][:, k % 4:k % 4 + 2, :]), f"w2_hi{j}")

                for j in range(KD):
                    e_dve.wait(act, f"glu{j}", n)
                    e_act.mark(act.activation(sig[j % 2][:], glu[j % 2][:], ACT.Sigmoid, scale=ALPHA), f"sig{j}")
                    if j in eighth_at:
                        high_part(eighth_at[j])
                    e_dve.wait(act, f"act{j}", n)
                    e_act.mark(act.copy(act_hi[:, j, :], act_sb[j % 2][:]), f"act_hi{j}")
                for j in later:
                    high_part(j)
            e_act.end()

        @block.vector
        def _(dve):
            e_dve.start(dve)
            for bank in pH + pY[0] + pY[1]:
                dve.memset(bank[:], 0.0).then_inc(psum_cleared, 1)
            dve.wait_ge(psum_cleared, 8)
            dve.wait_ge(small, 32)
            dve.tensor_scalar(b1[:, :, :, 1:2], b1[:, :, :, 1:2], 1.0, None, ALU.add).then_inc(psum_cleared, 1)
            dve.wait_ge(psum_cleared, 9)

            def take_rows(f):
                b, k = f // 2, 4 * (f % 2)
                return dve.tensor_tensor(xT[:, k:k + 4, b * P:(b + 1) * P], pH[f][:].rearrange("p a (b w) -> p (a b) w", w=P),
                                         over_width(ffn_w[:, k:k + 4], P), ALU.mult)

            for f in range(2 * BLOCKS):
                dve.wait_ge(x_turned.sem, f + 1)
                take_rows(f).then_inc(x_read.sem, 1)
            with dve.Fori(0, number_of_items(dve)) as n:
                e = expert_of(dve, n)
                e_dve.wait(dve, "y11", n, back=1)
                dve.sem_inc(dve_turn, 1)
                e_dve.mark(dve.tensor_copy(b1_item[:].unsqueeze(1), b1[:, ds(e, 1), :, :]), "bias")
                e_dve.wait(dve, "bias", n)

                def low_part(j):
                    c, k = j // 4, 2 * (j % 4)
                    e_act.wait(dve, f"w2_hi{j}", n)
                    e_dve.mark(dve.tensor_tensor(w2_lo[c][:, k:k + 2, :], w2[k // 4][:, k % 4:k % 4 + 2, :], w2_hi[c][:, k:k + 2, :].bitcast(F32),
                                                 ALU.subtract), f"w2_lo{j}")

                for j in range(KD):
                    u = j % 2
                    hidden.wait(dve, str(j), n)
                    if j >= 2:
                        e_dve.wait(dve, f"act_lo{j - 2}", n)
                    e_dve.mark(dve.tensor_scalar(glu[u][:], pH[j % 4][:, 0, :], b1_item[:, j, 0:1], LIMIT, ALU.add, ALU.min), f"glu{j}")
                    e_dve.mark(dve.tensor_scalar(lin[u][:], pH[j % 4][:, 1, :], b1_item[:, j, 1:2], LIMIT + 1, ALU.add, ALU.min), f"lin{j}")
                    e_dve.wait(dve, f"lin{j}", n)
                    e_dve.mark(dve.scalar_tensor_tensor(out=lin[u][:], in0=lin[u][:], scalar=1 - LIMIT, in1=glu[u][:],
                                                        op0=ALU.max, op1=ALU.mult), f"prod{j}")
                    e_act.wait(dve, f"sig{j}", n)
                    e_dve.wait(dve, f"prod{j}", n)
                    e_dve.mark(dve.tensor_tensor(act_sb[u][:], lin[u][:], sig[u][:], ALU.mult), f"act{j}")
                    if j in eighth_at:
                        low_part(eighth_at[j])
                    e_act.wait(dve, f"act_hi{j}", n)
                    e_dve.wait(dve, f"act{j}", n)
                    e_dve.mark(dve.tensor_tensor(act_lo[:, j, :], act_sb[u][:], act_hi[:, j, :].bitcast(F32), ALU.subtract), f"act_lo{j}")
                for j in later:
                    low_part(j)

                def next_rows(f):
                    x_turned.wait(dve, str(f), n)
                    x_read.mark(take_rows(f), str(f))

                for f in range(2 * BLOCKS - 1):
                    next_rows(f)
                e_pool.wait(dve, "current", n, back=1)
                dve.wait_ge(b2_in, 16 * n + 16)
                for c in range(W2_CHUNKS):
                    for b in range(BLOCKS):
                        y = y_rows[:, b, 512 * c:512 * c + 512]
                        block_pe[b].wait(dve, str(c), n)
                        e_dve.mark(dve.tensor_tensor(y, pY[b][c][:], b2_item[:, 512 * c:512 * c + 512], ALU.add), f"sum{c}{b}")
                        e_dve.wait(dve, f"sum{c}{b}", n)
                        e_dve.mark(dve.tensor_scalar(y, y, places[:, b, 1:2].bitcast(F32), None, ALU.mult), f"y{c}{b}")
                        if (b, c) == (0, 0):
                            next_rows(2 * BLOCKS - 1)
            e_dve.end()
            x_read.end()


def finish(nc, A, m, out):
    with ExitStack() as own:
        def sb(name, shape, dt=F32):
            return own.enter_context(nc.sbuf_tensor(name, shape, dt))

        def sem(name):
            return own.enter_context(nc.semaphore(name))

        y = [sb(f"y_in{i}", [P, D_MODEL]) for i in range(NT)]
        res = [sb(f"res{i}", [P, D_MODEL]) for i in range(NT)]
        sq = [sb(f"final_sq{i}", [P, D_MODEL], mybir.dt.bfloat16) for i in range(2)]
        ms, rs, power, w = sb("ms", [P, NT]), sb("rs_final", [P, NT]), sb("final_power", [P, NT]), sb("final_w", [P, D_MODEL])
        y_in, w_in = [sem(f"y_in_done{i}") for i in range(NT)], sem("final_w_in")
        squared, mean, root, ready, stored, f_zero = (sem(n) for n in ("squared", "mean", "root", "ready", "stored", "f_zero"))
        block = own.enter_context(nc.Block())

        @block.sync
        def _(sp):
            for i in range(NT):
                sp.dma_start(y[i][:], m.y[i * P:(i + 1) * P, :]).then_inc(y_in[i], 16)
            sp.dma_start(w[:], bc(A["norm_final"], [P, D_MODEL])).then_inc(w_in, 16)
            for i in range(NT):
                sp.wait_ge(ready, i + 1)
                sp.dma_start(out[i * P:(i + 1) * P, :], res[i][:]).then_inc(stored, 16)
            sp.wait_ge(stored, 16 * NT)

        @block.scalar
        def _(act):
            for i in range(NT):
                act.wait_ge(y_in[i], 16)
                if i >= 2:
                    act.wait_ge(squared, i - 1)
                act.activation(sq[i % 2][:], y[i][:], ACT.Square, accum_out=ms[:, i:i + 1]).then_inc(squared, 1)

        @block.gpsimd
        def _(pool):
            pool.memset(power[:], -0.5).then_inc(f_zero, 1)
            pool.wait_ge(f_zero, 1)
            for i in range(NT):
                pool.wait_ge(mean, i + 1)
                pool.tensor_tensor(rs[:, i:i + 1], ms[:, i:i + 1], power[:, 0:1], ALU.pow).then_inc(root, 1)

        @block.vector
        def _(dve):
            dve.wait_ge(w_in, 16)
            for i in range(NT):
                dve.wait_ge(squared, i + 1)
                dve.tensor_scalar(ms[:, i:i + 1], ms[:, i:i + 1], 1.0 / D_MODEL, EPS, ALU.mult, ALU.add).then_inc(mean, 1)
                dve.wait_ge(root, i + 1)
                dve.scalar_tensor_tensor(out=res[i][:], in0=y[i][:], scalar=rs[:, i:i + 1], in1=w[:],
                                         op0=ALU.mult, op1=ALU.mult).then_inc(ready, 1)


def build(nc, A, out):
    with ExitStack() as ctx:
        m = Memory()

        def sb_in(stack, name, shape, dt=F32):
            return stack.enter_context(nc.sbuf_tensor(name, shape, dt))

        m.const = sb_in(ctx, "const_sb", [P, CONSTS])
        m.gdn_in = nc.dram_tensor("gdn_in", [SEQ, 4 * GW], F32, kind="Internal").ap()
        m.y = nc.dram_tensor("y", [SEQ, D_MODEL], F32, kind="Internal").ap()
        m.h2_rows = nc.dram_tensor("h2_rows", [SEQ, D_MODEL], F32, kind="Internal").ap()
        m.places = nc.dram_tensor("places", [PLACES, 2], I32, kind="Internal").ap()
        m.table = sb_in(ctx, "table", [1, 4 * TABLE], I32)
        with ExitStack() as mixed:
            m.gdn_o = sb_in(mixed, "gdn_o", [P, NT, GW])
            m.attn_o = sb_in(mixed, "attn_o", [P, NT, AH * AV])
            with ExitStack() as front:
                m.cqT = sb_in(front, "cqT", [P, KQ, SEQ])
                m.ckvT = sb_in(front, "ckvT", [P, KKV, SEQ])
                m.ab = sb_in(front, "ab", [P, NT, 2 * GH])
                m.k_rope = sb_in(front, "k_rope", [P, NT, ROPE])
                m.g, m.beta = (sb_in(front, n, [P, NT, GH]) for n in ("g", "beta"))
                m.cos, m.sin = (sb_in(front, n, [P, NT, HALF]) for n in ("cos", "sin"))
                m.kh = sb_in(front, "kh", [P, NT, QK])
                project(nc, A, m)
                mix(nc, A, m)
            route(nc, A, m)
        experts(nc, A, m)
        finish(nc, A, m, out)


def _cols(w, k):
    return np.ascontiguousarray(np.asarray(w).reshape(k, P).T)


def _layout(x, positions, norm_mix_w, w_in, conv_w, a_log, dt_bias, gdn_norm_w, q_norm_w, w_uq, kv_norm_w, w_ukv,
            mla_out_norm_w, w_out, norm_ffn_w, router_w, router_b, w1, b1, w2, b2, norm_final_w):
    return {
        "const": CONST,
        "x": np.asarray(x).reshape(SEQ, D_MODEL),
        "positions": np.ascontiguousarray(np.asarray(positions).reshape(NT, P).T),
        "norm_mix": _cols(norm_mix_w, KD),
        "w_in": np.asarray(w_in).reshape(D_MODEL, D_IN),
        "conv_w": np.ascontiguousarray(np.asarray(conv_w).reshape(CONV, 12, P).transpose(2, 1, 0)),
        "a_log": np.asarray(a_log).reshape(1, GH),
        "dt_bias": np.asarray(dt_bias).reshape(1, GH),
        "gdn_norm": _cols(gdn_norm_w, 1),
        "q_norm": _cols(q_norm_w, KQ),
        "w_uq": np.asarray(w_uq).reshape(Q_LORA, AH * QK),
        "kv_norm": _cols(kv_norm_w, KKV),
        "w_ukv": np.asarray(w_ukv).reshape(KV_LORA, AH * (NOPE + AV)),
        "mla_norm": _cols(mla_out_norm_w, AH * AV // P),
        "w_out": np.asarray(w_out).reshape(D_MODEL, D_MODEL),
        "norm_ffn": _cols(norm_ffn_w, KD),
        "router_w": np.asarray(router_w).reshape(D_MODEL, NE),
        "router_b": np.asarray(router_b).reshape(1, NE),
        "w1": np.asarray(w1).reshape(NE, D_MODEL, 2 * D_FF),
        "b1": np.ascontiguousarray(np.asarray(b1).reshape(NE, KD, P, 2).transpose(2, 0, 1, 3)),
        "w2": np.asarray(w2).reshape(NE, D_FF, D_MODEL),
        "b2": np.asarray(b2).reshape(NE, D_MODEL),
        "norm_final": np.asarray(norm_final_w).reshape(1, D_MODEL),
    }


def kernel(**inputs):
    import concourse.bacc as bacc
    from concourse.bass_utils import run_bass_kernel_spmd

    arrays = _layout(**inputs)
    nc = bacc.Bacc("TRN2", target_bir_lowering=False, num_devices=1)
    A = {name: nc.dram_tensor(f"in_{name}", list(a.shape), mybir.dt.from_np(a.dtype), kind="ExternalInput").ap()
         for name, a in arrays.items()}
    out = nc.dram_tensor("out", [SEQ, D_MODEL], F32, kind="ExternalOutput").ap()
    build(nc, A, out)
    r = run_bass_kernel_spmd(nc, [{f"in_{name}": a for name, a in arrays.items()}], core_ids=[0])
    return r.results[0]["out"].reshape(1, SEQ, D_MODEL)
```
